# Optimizing a Trainium2 kernel written in Bass

```python
import math
import jax, jax.numpy as jnp
from jax import lax
import numpy as np

D_MODEL = 1024
BATCH = 1
SEQ = 256
DEPTH = 1

CHUNK = 64
D_MIX = D_MODEL
GM_GROUPS = 8
GM_GROUP_DIM = 64
GM_WIDTH = GM_GROUPS * GM_GROUP_DIM
GM_BLOCK = 128
DN_HEADS = 4
DN_HEAD_DIM = 128
DN_WIDTH = DN_HEADS * DN_HEAD_DIM
DN_CONV = 4
D_IN = 2 * GM_WIDTH + 4 * DN_WIDTH + 2 * DN_HEADS
D_FF = 2816
EPS = 1e-6


def rmsnorm(x, g):
    xf = x.astype(jnp.float32)
    y = xf * lax.rsqrt(jnp.mean(xf * xf, axis=-1, keepdims=True) + EPS)
    return (y * g.astype(jnp.float32)).astype(x.dtype)

def layernorm(x, g, b):
    xf = x.astype(jnp.float32)
    mu = jnp.mean(xf, axis=-1, keepdims=True)
    var = jnp.mean(jnp.square(xf - mu), axis=-1, keepdims=True)
    y = (xf - mu) * lax.rsqrt(var + EPS)
    return (y * g.astype(jnp.float32) + b.astype(jnp.float32)).astype(x.dtype)

def l2norm(x):
    return x * lax.rsqrt(jnp.sum(x * x, axis=-1, keepdims=True) + EPS)

def swiglu(x, w_gate, w_up, w_down):
    return (jax.nn.silu(x @ w_gate) * (x @ w_up)) @ w_down

def chunk_causal_mask(n):
    c = jnp.arange(n) // CHUNK
    return c[None, :] <= c[:, None]

def spatial_gating(u, v, w_s, b_s, ln_g, ln_b):
    B, T, _ = v.shape
    v = layernorm(v, ln_g, ln_b)
    nb = T // GM_BLOCK
    vb = v.reshape(B, nb, GM_BLOCK, GM_GROUPS, GM_GROUP_DIM)
    w = jnp.where(chunk_causal_mask(GM_BLOCK)[None], w_s, 0.0).astype(v.dtype)
    mixed = jnp.einsum('gij,bnjgc->bnigc', w, vb) + b_s.T[:, :, None].astype(v.dtype)
    return u * mixed.reshape(B, T, GM_WIDTH)

def causal_dwconv(x, w):
    K, C = w.shape
    return lax.conv_general_dilated(
        x, w[:, None, :].astype(x.dtype), window_strides=(1,), padding=[(K - 1, 0)],
        dimension_numbers=('NWC', 'WIO', 'NWC'), feature_group_count=C)

def gated_delta_rule(q, k, v, beta, g):
    B, T, H, Dk = q.shape
    Dv = v.shape[-1]
    C = CHUNK
    N = T // C
    scale = Dk ** -0.5

    def to_chunks(t):
        return t.reshape(B, N, C, H, *t.shape[3:]).swapaxes(2, 3)

    q, k, v = to_chunks(q * scale), to_chunks(k), to_chunks(v)
    beta, g = to_chunks(beta), to_chunks(g)
    g = jnp.cumsum(g, axis=-1)
    tri = jnp.tril(jnp.ones((C, C), bool))
    strict = jnp.tril(jnp.ones((C, C), bool), -1)
    decay = jnp.exp(jnp.where(tri, g[..., :, None] - g[..., None, :], -jnp.inf))
    k_beta = k * beta[..., None]
    v_beta = v * beta[..., None]
    L = jnp.where(strict, jnp.einsum('bnhid,bnhjd->bnhij', k_beta, k) * decay, 0.0)
    eye = jnp.eye(C, dtype=L.dtype)
    rhs = jnp.concatenate([v_beta, k_beta * jnp.exp(g)[..., None]], axis=-1)
    sol = lax.linalg.triangular_solve(L + eye, rhs, left_side=True, lower=True,
                                      unit_diagonal=True)
    u_c, w_c = sol[..., :Dv], sol[..., Dv:]
    attn = jnp.where(tri, jnp.einsum('bnhid,bnhjd->bnhij', q, k) * decay, 0.0)
    g_last = g[..., -1]
    k_dec = k * jnp.exp(g_last[..., None] - g)[..., None]
    q_dec = q * jnp.exp(g)[..., None]
    xs = tuple(jnp.moveaxis(t, 1, 0) for t in (q_dec, k_dec, u_c, w_c, attn, g_last))

    def step(S, inp):
        qd, kd, uc, wc, a, gl = inp
        v_new = uc - jnp.einsum('bhcd,bhde->bhce', wc, S)
        o = jnp.einsum('bhcd,bhde->bhce', qd, S) + jnp.einsum('bhij,bhje->bhie', a, v_new)
        S = S * jnp.exp(gl)[..., None, None] + jnp.einsum('bhcd,bhce->bhde', kd, v_new)
        return S, o

    S0 = jnp.zeros((B, H, Dk, Dv), q.dtype)
    _, o = lax.scan(step, S0, xs)
    return jnp.moveaxis(o, 0, 1).swapaxes(2, 3).reshape(B, T, H, Dv)

def first_inputs(seed: int = 0) -> dict:
    key = jax.random.key(seed)
    ks = jax.random.split(key, 24)
    f32 = jnp.float32
    L = DEPTH

    def nrm(k, shape, scale):
        return jax.random.normal(k, shape, f32) * scale

    def gain(k, shape):
        return 1.0 + 0.05 * jax.random.normal(k, shape, f32)

    dt = jnp.exp(jax.random.uniform(ks[13], (L, DN_HEADS), f32, math.log(1e-3), math.log(1e-1)))
    return {
        "x": jax.random.normal(ks[0], (BATCH, SEQ, D_MODEL), f32),
        "ffn1_norm": gain(ks[1], (L, D_MODEL)),
        "ffn1_w_gate": nrm(ks[2], (L, D_MODEL, D_FF), D_MODEL ** -0.5),
        "ffn1_w_up": nrm(ks[3], (L, D_MODEL, D_FF), D_MODEL ** -0.5),
        "ffn1_w_down": nrm(ks[4], (L, D_FF, D_MODEL), D_FF ** -0.5),
        "mix_norm": gain(ks[5], (L, D_MODEL)),
        "w_in": nrm(ks[6], (L, D_MODEL, D_IN), D_MODEL ** -0.5),
        "gm_ln_g": gain(ks[7], (L, GM_WIDTH)),
        "gm_ln_b": nrm(ks[8], (L, GM_WIDTH), 0.02),
        "gm_w_s": nrm(ks[9], (L, GM_GROUPS, GM_BLOCK, GM_BLOCK), GM_BLOCK ** -0.5),
        "gm_b_s": 1.0 + nrm(ks[10], (L, GM_GROUPS, GM_BLOCK), 0.1),
        "dn_conv_w": nrm(ks[11], (L, DN_CONV, 3 * DN_WIDTH), DN_CONV ** -0.5),
        "dn_a_log": jnp.log(jax.random.uniform(ks[12], (L, DN_HEADS), f32, 1.0, 16.0)),
        "dn_dt_bias": dt + jnp.log(-jnp.expm1(-dt)),
        "dn_norm": gain(ks[14], (L, DN_HEAD_DIM)),
        "w_out": nrm(ks[15], (L, D_MIX, D_MODEL), D_MIX ** -0.5),
        "ffn2_norm": gain(ks[16], (L, D_MODEL)),
        "ffn2_w_gate": nrm(ks[17], (L, D_MODEL, D_FF), D_MODEL ** -0.5),
        "ffn2_w_up": nrm(ks[18], (L, D_MODEL, D_FF), D_MODEL ** -0.5),
        "ffn2_w_down": nrm(ks[19], (L, D_FF, D_MODEL), D_FF ** -0.5),
        "final_norm": gain(ks[20], (D_MODEL,)),
    }

def first_block(x, ffn1_norm, ffn1_w_gate, ffn1_w_up, ffn1_w_down, mix_norm, w_in,
              gm_ln_g, gm_ln_b, gm_w_s, gm_b_s, dn_conv_w, dn_a_log, dn_dt_bias, dn_norm,
              w_out, ffn2_norm, ffn2_w_gate, ffn2_w_up, ffn2_w_down, final_norm):
    B, T, _ = x.shape
    split_at = [GM_WIDTH, 2 * GM_WIDTH, 2 * GM_WIDTH + 3 * DN_WIDTH,
                2 * GM_WIDTH + 4 * DN_WIDTH, 2 * GM_WIDTH + 4 * DN_WIDTH + DN_HEADS]
    for l in range(DEPTH):
        x = x + 0.5 * swiglu(rmsnorm(x, ffn1_norm[l]), ffn1_w_gate[l], ffn1_w_up[l], ffn1_w_down[l])

        h = rmsnorm(x, mix_norm[l])
        p = h @ w_in[l]
        u_a, v_a, qkv, z, b_raw, a_raw = jnp.split(p, split_at, axis=-1)

        y_a = spatial_gating(jax.nn.gelu(u_a), jax.nn.gelu(v_a), gm_w_s[l], gm_b_s[l],
                             gm_ln_g[l], gm_ln_b[l])

        qkv = jax.nn.silu(causal_dwconv(qkv, dn_conv_w[l])).astype(jnp.float32)
        q, k, v = jnp.split(qkv, 3, axis=-1)
        q = l2norm(q.reshape(B, T, DN_HEADS, DN_HEAD_DIM))
        k = l2norm(k.reshape(B, T, DN_HEADS, DN_HEAD_DIM))
        v = v.reshape(B, T, DN_HEADS, DN_HEAD_DIM)
        beta = jax.nn.sigmoid(b_raw.astype(jnp.float32))
        g = -jnp.exp(dn_a_log[l].astype(jnp.float32)) * jax.nn.softplus(
            a_raw.astype(jnp.float32) + dn_dt_bias[l].astype(jnp.float32))
        o = gated_delta_rule(q, k, v, beta, g)
        zg = jax.nn.silu(z.astype(jnp.float32)).reshape(B, T, DN_HEADS, DN_HEAD_DIM)
        y_b = (rmsnorm(o, dn_norm[l]) * zg).reshape(B, T, DN_WIDTH).astype(x.dtype)

        x = x + jnp.concatenate([y_a, y_b], axis=-1) @ w_out[l]

        x = x + 0.5 * swiglu(rmsnorm(x, ffn2_norm[l]), ffn2_w_gate[l], ffn2_w_up[l], ffn2_w_down[l])
    return rmsnorm(x, final_norm)


DEPTH_2 = 2

HEAD_DIM = 64
FOX_HEADS = 8
FOX_WIDTH = FOX_HEADS * HEAD_DIM
POOL_GROUPS = 4
POOL_WINDOWS = (2, 4, 8, 16)
POOL_WIDTH = D_MODEL - FOX_WIDTH
POOL_GROUP_DIM = POOL_WIDTH // POOL_GROUPS
Q_BLOCK = 128
IN_COLS = 4 * FOX_WIDTH + FOX_HEADS + POOL_WIDTH
SPLITS = (FOX_WIDTH, 2 * FOX_WIDTH, 3 * FOX_WIDTH, 4 * FOX_WIDTH, 4 * FOX_WIDTH + FOX_HEADS)
RWKV_HEADS = D_MODEL // HEAD_DIM
DECAY_LORA = 64
AAA_LORA = 64
MV_LORA = 32
GATE_LORA = 160
D_FF_2 = -(-(8 * D_MODEL) // (3 * 256)) * 256
RMS_EPS = 1e-6
GN_EPS = 64e-5
N_EVEN = (DEPTH_2 + 1) // 2
N_ODD = DEPTH_2 // 2


def _rmsnorm(x, gain):
    xf = x.astype(jnp.float32)
    y = xf * lax.rsqrt(jnp.mean(xf * xf, axis=-1, keepdims=True) + RMS_EPS)
    return (y * gain.astype(jnp.float32)).astype(x.dtype)

def _swiglu(h, w_gate, w_up, w_down):
    return (jax.nn.silu(h @ w_gate) * (h @ w_up)) @ w_down

def _token_shift(x):
    return jnp.pad(x, ((0, 0), (1, 0), (0, 0)))[:, :-1]

def _forgetting_attention(q, k, v, cum):
    b, h, s, dh = q.shape
    nb = s // Q_BLOCK
    scale = dh ** -0.5
    qb = q.reshape(b, h, nb, Q_BLOCK, dh).transpose(2, 0, 1, 3, 4)
    cb = cum.reshape(b, h, nb, Q_BLOCK).transpose(2, 0, 1, 3)
    key_pos = jnp.arange(s)

    def one_block(args):
        i, q_i, c_i = args
        q_pos = i * Q_BLOCK + jnp.arange(Q_BLOCK)
        logits = (jnp.einsum('bhqd,bhkd->bhqk', q_i, k).astype(jnp.float32) * scale
                  + c_i[..., :, None] - cum[..., None, :])
        causal = key_pos[None, :] <= q_pos[:, None]
        p = jax.nn.softmax(jnp.where(causal, logits, -1e30), axis=-1)
        return jnp.einsum('bhqk,bhkd->bhqd', p.astype(v.dtype), v)

    out = lax.map(one_block, (jnp.arange(nb), qb, cb))
    return out.transpose(1, 2, 0, 3, 4).reshape(b, h, s, dh)

def _multiscale_causal_pool(u, pool_w, pool_scale):
    b, s, _ = u.shape
    uf = u.astype(jnp.float32).reshape(b, s, POOL_GROUPS, POOL_GROUP_DIM)
    csum = jnp.cumsum(uf, axis=1)
    pos = jnp.arange(s)
    groups = []
    for g, w in enumerate(POOL_WINDOWS):
        cg = csum[:, :, g]
        prev = jnp.pad(cg, ((0, 0), (w, 0), (0, 0)))[:, :s]
        count = jnp.minimum(pos + 1, w).astype(jnp.float32)[None, :, None]
        groups.append((cg - prev) / count - uf[:, :, g])
    pooled = jnp.stack(groups, axis=2).astype(u.dtype)
    mixed = jnp.einsum('bsgc,gcd->bsgd', pooled, pool_w)
    return mixed.reshape(b, s, POOL_WIDTH) * pool_scale

def _fox_pool_mixer(h, w_in, f_bias, q_gain, k_gain, pool_w, pool_scale, w_out):
    b, s, _ = h.shape
    proj = h @ w_in
    q, k, v, og, f_logit, u = jnp.split(proj, SPLITS, axis=-1)

    def heads(t):
        return t.reshape(b, s, FOX_HEADS, HEAD_DIM)

    q = _rmsnorm(heads(q), q_gain).transpose(0, 2, 1, 3)
    k = _rmsnorm(heads(k), k_gain).transpose(0, 2, 1, 3)
    v = heads(v).transpose(0, 2, 1, 3)
    log_f = jax.nn.log_sigmoid(f_logit.astype(jnp.float32) + f_bias.astype(jnp.float32))
    cum = jnp.cumsum(log_f, axis=1).transpose(0, 2, 1)
    attn = _forgetting_attention(q, k, v, cum).transpose(0, 2, 1, 3).reshape(b, s, FOX_WIDTH)
    attn = attn * jax.nn.sigmoid(og)
    pool = _multiscale_causal_pool(u, pool_w, pool_scale)
    return jnp.concatenate([attn, pool], axis=-1) @ w_out

def _rwkv7_step(state, inp):
    r_t, w_t, k_t, v_t, a_t, b_t = inp
    sa = jnp.einsum('bhvk,bhk->bhv', state, a_t)
    state = (state * w_t[:, :, None, :] + sa[..., None] * b_t[:, :, None, :]
             + v_t[..., None] * k_t[:, :, None, :])
    return state, jnp.einsum('bhvk,bhk->bhv', state, r_t)

def _rwkv7_time_mix(h, mu, w_r, w_k, w_v, w0, w1, w2, a0, a1, a2, g1, g2,
                    k_k, k_a, r_k, ln_w, ln_b, w_o, v_first, v_mix):
    b, s, d = h.shape
    f32 = jnp.float32
    xx = _token_shift(h) - h
    xr, xw, xk, xv, xa, xg = [h + xx * mu[i] for i in range(6)]
    r = (xr @ w_r).astype(f32)
    k = (xk @ w_k).astype(f32)
    v = (xv @ w_v).astype(f32)
    w = -jax.nn.softplus(-(w0 + jnp.tanh(xw @ w1) @ w2).astype(f32)) - 0.5
    a = jax.nn.sigmoid((a0 + (xa @ a1) @ a2).astype(f32))
    g = jax.nn.sigmoid(xg @ g1) @ g2
    if v_mix is None:
        v_first = v
    else:
        v0, v1, v2 = v_mix
        v = v + (v_first - v) * jax.nn.sigmoid((v0 + (xv @ v1) @ v2).astype(f32))

    def heads(t):
        return t.reshape(b, s, RWKV_HEADS, HEAD_DIM)

    kk = heads(k * k_k.astype(f32))
    kk = kk / jnp.maximum(jnp.sqrt(jnp.sum(kk * kk, axis=-1, keepdims=True)), 1e-12)
    k = k * (1.0 + (a - 1.0) * k_a.astype(f32))
    decay = jnp.exp(-jnp.exp(w))
    rh, kh, vh, ah = heads(r), heads(k), heads(v), heads(a)
    seq_first = lambda t: t.transpose(1, 0, 2, 3)
    xs = (seq_first(rh), seq_first(heads(decay)), seq_first(kh), seq_first(vh),
          seq_first(-kk), seq_first(kk * ah))
    state0 = jnp.zeros((b, RWKV_HEADS, HEAD_DIM, HEAD_DIM), f32)
    _, ys = lax.scan(_rwkv7_step, state0, xs)
    y = ys.transpose(1, 0, 2, 3)
    mean = jnp.mean(y, axis=-1, keepdims=True)
    var = jnp.mean(jnp.square(y - mean), axis=-1, keepdims=True)
    y = ((y - mean) * lax.rsqrt(var + GN_EPS)).reshape(b, s, d) * ln_w.astype(f32) + ln_b.astype(f32)
    bonus = jnp.sum(rh * kh * r_k.astype(f32), axis=-1, keepdims=True) * vh
    y = (y + bonus.reshape(b, s, d)).astype(h.dtype)
    return (y * g) @ w_o, v_first

def second_inputs(seed: int = 0) -> dict:
    key = jax.random.key(seed)
    keys = jax.random.split(key, 40)
    counter = [0]
    f32 = jnp.float32

    def nk():
        counter[0] += 1
        return keys[counter[0] - 1]

    def nrm(shape, scale):
        return jax.random.normal(nk(), shape, f32) * scale

    def gain(shape):
        return 1.0 + 0.1 * jax.random.normal(nk(), shape, f32)

    D, F, ne, no = D_MODEL, D_FF_2, N_EVEN, N_ODD
    return {
        'x': nrm((BATCH, SEQ, D), 1.0),
        'mix_norm': gain((DEPTH_2, D)),
        'ffn_norm': gain((DEPTH_2, D)),
        'ffn_w_gate': nrm((DEPTH_2, D, F), D ** -0.5),
        'ffn_w_up': nrm((DEPTH_2, D, F), D ** -0.5),
        'ffn_w_down': nrm((DEPTH_2, F, D), F ** -0.5),
        'hy_w_in': nrm((ne, D, IN_COLS), D ** -0.5),
        'hy_f_bias': 2.0 + 0.5 * jax.random.normal(nk(), (ne, FOX_HEADS), f32),
        'hy_q_gain': gain((ne, HEAD_DIM)),
        'hy_k_gain': gain((ne, HEAD_DIM)),
        'hy_pool_w': nrm((ne, POOL_GROUPS, POOL_GROUP_DIM, POOL_GROUP_DIM), POOL_GROUP_DIM ** -0.5),
        'hy_pool_scale': gain((ne, POOL_WIDTH)),
        'hy_w_out': nrm((ne, D, D), D ** -0.5),
        'rw_mu': jax.random.uniform(nk(), (no, 6, D), f32),
        'rw_w_r': nrm((no, D, D), D ** -0.5),
        'rw_w_k': nrm((no, D, D), D ** -0.5),
        'rw_w_v': nrm((no, D, D), D ** -0.5),
        'rw_w0': nrm((no, D), 0.5),
        'rw_w1': nrm((no, D, DECAY_LORA), D ** -0.5),
        'rw_w2': nrm((no, DECAY_LORA, D), 0.5 * DECAY_LORA ** -0.5),
        'rw_a0': nrm((no, D), 0.5),
        'rw_a1': nrm((no, D, AAA_LORA), D ** -0.5),
        'rw_a2': nrm((no, AAA_LORA, D), 0.5 * AAA_LORA ** -0.5),
        'rw_g1': nrm((no, D, GATE_LORA), D ** -0.5),
        'rw_g2': nrm((no, GATE_LORA, D), GATE_LORA ** -0.5),
        'rw_k_k': gain((no, D)),
        'rw_k_a': gain((no, D)),
        'rw_r_k': nrm((no, RWKV_HEADS, HEAD_DIM), 0.1),
        'rw_ln_w': gain((no, D)),
        'rw_ln_b': nrm((no, D), 0.02),
        'rw_w_o': nrm((no, D, D), D ** -0.5),
        'rw_v0': nrm((max(no - 1, 0), D), 0.5),
        'rw_v1': nrm((max(no - 1, 0), D, MV_LORA), D ** -0.5),
        'rw_v2': nrm((max(no - 1, 0), MV_LORA, D), 0.5 * MV_LORA ** -0.5),
    }

def second_block(x, mix_norm, ffn_norm, ffn_w_gate, ffn_w_up, ffn_w_down,
              hy_w_in, hy_f_bias, hy_q_gain, hy_k_gain, hy_pool_w, hy_pool_scale, hy_w_out,
              rw_mu, rw_w_r, rw_w_k, rw_w_v, rw_w0, rw_w1, rw_w2, rw_a0, rw_a1, rw_a2,
              rw_g1, rw_g2, rw_k_k, rw_k_a, rw_r_k, rw_ln_w, rw_ln_b, rw_w_o,
              rw_v0, rw_v1, rw_v2):
    v_first = None
    for layer in range(DEPTH_2):
        h = _rmsnorm(x, mix_norm[layer])
        if layer % 2 == 0:
            e = layer // 2
            y = _fox_pool_mixer(h, hy_w_in[e], hy_f_bias[e], hy_q_gain[e], hy_k_gain[e],
                                hy_pool_w[e], hy_pool_scale[e], hy_w_out[e])
        else:
            o = layer // 2
            v_mix = None if o == 0 else (rw_v0[o - 1], rw_v1[o - 1], rw_v2[o - 1])
            y, v_first = _rwkv7_time_mix(h, rw_mu[o], rw_w_r[o], rw_w_k[o], rw_w_v[o],
                                         rw_w0[o], rw_w1[o], rw_w2[o], rw_a0[o], rw_a1[o], rw_a2[o],
                                         rw_g1[o], rw_g2[o], rw_k_k[o], rw_k_a[o], rw_r_k[o],
                                         rw_ln_w[o], rw_ln_b[o], rw_w_o[o], v_first, v_mix)
        x = x + y
        x = x + _swiglu(_rmsnorm(x, ffn_norm[layer]), ffn_w_gate[layer], ffn_w_up[layer], ffn_w_down[layer])
    return x


def setup_inputs(seed=0):
    out = dict(first_inputs(seed))
    for name, value in second_inputs(seed + 1).items():
        if name != "x":
            out[name + "_2"] = value
    return out


def reference(
    x, ffn1_norm, ffn1_w_gate, ffn1_w_up, ffn1_w_down, mix_norm, w_in, gm_ln_g, gm_ln_b, gm_w_s,
    gm_b_s, dn_conv_w, dn_a_log, dn_dt_bias, dn_norm, w_out, ffn2_norm, ffn2_w_gate, ffn2_w_up,
    ffn2_w_down, final_norm, mix_norm_2, ffn_norm_2, ffn_w_gate_2, ffn_w_up_2, ffn_w_down_2,
    hy_w_in_2, hy_f_bias_2, hy_q_gain_2, hy_k_gain_2, hy_pool_w_2, hy_pool_scale_2, hy_w_out_2,
    rw_mu_2, rw_w_r_2, rw_w_k_2, rw_w_v_2, rw_w0_2, rw_w1_2, rw_w2_2, rw_a0_2, rw_a1_2, rw_a2_2,
    rw_g1_2, rw_g2_2, rw_k_k_2, rw_k_a_2, rw_r_k_2, rw_ln_w_2, rw_ln_b_2, rw_w_o_2, rw_v0_2,
    rw_v1_2, rw_v2_2,
):
    x = first_block(
        x, ffn1_norm, ffn1_w_gate, ffn1_w_up, ffn1_w_down, mix_norm, w_in, gm_ln_g, gm_ln_b,
        gm_w_s, gm_b_s, dn_conv_w, dn_a_log, dn_dt_bias, dn_norm, w_out, ffn2_norm, ffn2_w_gate,
        ffn2_w_up, ffn2_w_down, final_norm,
    )
    return second_block(
        x, mix_norm_2, ffn_norm_2, ffn_w_gate_2, ffn_w_up_2, ffn_w_down_2, hy_w_in_2,
        hy_f_bias_2, hy_q_gain_2, hy_k_gain_2, hy_pool_w_2, hy_pool_scale_2, hy_w_out_2,
        rw_mu_2, rw_w_r_2, rw_w_k_2, rw_w_v_2, rw_w0_2, rw_w1_2, rw_w2_2, rw_a0_2, rw_a1_2,
        rw_a2_2, rw_g1_2, rw_g2_2, rw_k_k_2, rw_k_a_2, rw_r_k_2, rw_ln_w_2, rw_ln_b_2, rw_w_o_2,
        rw_v0_2, rw_v1_2, rw_v2_2,
    )


_drawn_inputs = setup_inputs


def setup_inputs(seed=0):
    import zlib

    import numpy as np

    out = dict(_drawn_inputs(seed))
    spreads = {}
    factors = {'gm_ln_b': 6.432,
     'hy_q_gain_2': 4.054,
     'hy_k_gain_2': 4.273,
     'rw_k_k_2': 6.054,
     'rw_ln_b_2': 6.831}
    for name, (base, spread) in spreads.items():
        noise = np.random.default_rng([zlib.crc32(name.encode()), seed]).standard_normal(out[name].shape)
        drawn = base * np.exp(spread * noise) if base else spread * noise
        out[name] = __import__('jax').numpy.asarray(drawn.astype(out[name].dtype))
    for name, factor in factors.items():
        out[name] = (out[name] * factor).astype(out[name].dtype)
    return out
```

```python
from contextlib import ExitStack

import numpy as np

import concourse.bass as bass
from concourse import mybir

P = 128
TOK = 256
TT = TOK // P
D = 1024
KT = D // P
FF = 2816
GROUPS = FF // 256
CHUNK_COLS = 2048
RAW = 3
SPLIT = 3
EPS = 1e-6

F32 = mybir.dt.float32
F32R = mybir.dt.float32r
ALU = mybir.AluOpType
ACT = mybir.ActivationFunctionType
AX_X = mybir.AxisListType.X


def ffn_chunks(f):
    names = [("gate", f, 0), ("up", f, 0)]
    for g in range(1, GROUPS):
        names += [("gate", f, g), ("up", f, g), ("down", f, g - 1)]
    return names + [("down", f, GROUPS - 1)]


def stream_plan(stages):
    names = []
    for s in stages:
        if s[0] == "ffn":
            names += ffn_chunks(s[1])
        if s[0] == "mix1":
            names += [("w_in", 0, j) for j in MIX1_ORDER] + [("w_out", 0, j) for j in range(4)]
        if s[0] == "fox":
            names += [("hy_w_in", 0, j) for j in FOX_ORDER] + [("hy_w_out", 0, j) for j in range(4)]
        if s[0] == "rwkv":
            names += RWKV_ORDER
    return names


MIX1_ORDER = [12, 6, 7, 4, 5, 8, 9, 10, 11, 2, 3, 0, 1]
FOX_ORDER = [8, 0, 1, 2, 3, 4, 5, 9, 10, 6, 7]
RWKV_ORDER = [("lora", 0, 0), ("lora", 0, 1)] + [("rw", 0, j) for j in range(12)] + [("lora", 0, 2)] + \
    [("rw_o", 0, j) for j in range(4)]
STAGES = [("ffn", 0), ("mix1", 0), ("ffn", 1), ("rms", 0), ("fox", 0), ("ffn", 2), ("rwkv", 0), ("ffn", 3)]


def col_chunk(w, c0, n=256):
    part = w[:, c0:c0 + n]
    if part.shape[1] < 256:
        part = np.concatenate([part, np.zeros((w.shape[0], 256 - part.shape[1]), w.dtype)], 1)
    return part.reshape(KT, P, 256).transpose(1, 0, 2).reshape(P, CHUNK_COLS)


def row_chunk(w, g):
    return w[g * 256:(g + 1) * 256].reshape(2, P, D).transpose(1, 0, 2).reshape(P, CHUNK_COLS)


def lay_out_chunk(name, a):
    kind, f, j = name
    ffn = {0: ("ffn1_w_gate", "ffn1_w_up", "ffn1_w_down", 0), 1: ("ffn2_w_gate", "ffn2_w_up", "ffn2_w_down", 0),
           2: ("ffn_w_gate_2", "ffn_w_up_2", "ffn_w_down_2", 0), 3: ("ffn_w_gate_2", "ffn_w_up_2", "ffn_w_down_2", 1)}
    if kind in ("gate", "up", "down"):
        w = a[ffn[f][("gate", "up", "down").index(kind)]][ffn[f][3]]
        return row_chunk(w, j) if kind == "down" else col_chunk(w, j * 256)
    if kind == "rw":
        return col_chunk(a[("rw_w_r_2", "rw_w_k_2", "rw_w_v_2")[j // 4]][0], (j % 4) * 256)
    if kind == "rw_o":
        return col_chunk(a["rw_w_o_2"][0], j * 256)
    if kind == "lora":
        g1, g2 = a["rw_g1_2"][0], a["rw_g2_2"][0]
        if j == 0:
            return col_chunk(np.concatenate([a["rw_w1_2"][0], a["rw_a1_2"][0], g1[:, :P]], 1), 0)
        if j == 1:
            tail = g1[:, P:].reshape(KT, P, 32).transpose(1, 0, 2).reshape(P, 256)
            top = np.concatenate([a["rw_w2_2"][0], a["rw_a2_2"][0]], 0)
            return np.concatenate([top, tail, np.zeros((P, 768), g1.dtype)], 1)
        return np.concatenate([g2[:P], np.concatenate([g2[P:], np.zeros((96, D), g2.dtype)], 0)], 1)
    if kind == "hy_w_in":
        return col_chunk(a["hy_w_in_2"][0], *{8: (2048, 8), 9: (2056,), 10: (2312,)}.get(j, (j * 256,)))
    return col_chunk(a[{"w_in": "w_in", "w_out": "w_out", "hy_w_in": "hy_w_in_2", "hy_w_out": "hy_w_out_2"}[kind]][0], j * 256)


def shape_constants():
    i = np.arange(P)[None, :]
    j = np.arange(P)[:, None]
    same = (i // 64) == (j // 64)
    parts = {
        "ident": i == j,
        "before": (j < i) & same,
        "upto": (j <= i) & same,
        "neg_upto": -1.0 * ((j <= i) & same),
        "after": (j > i) & same,
        "chunk0": (j < 64) & (i >= 0),
        "chunk1": (j >= 64) & (i >= 0),
        "upto_all": j <= i,
        "ones": (i >= 0) & (j >= 0),
        "same64": same,
        "gm_mask": ~((j >= 64) & (i < 64)),
    }
    for s in (1, 2, 4, 8, 16, 32):
        parts[f"level{s}"] = (i // (2 * s) == j // (2 * s)) & ((i // s) % 2 == 1) & ((j // s) % 2 == 0)
    cols, at = [], {}
    n = 0
    for name, m in parts.items():
        at[name] = n
        cols.append(np.asarray(m).astype(np.float32))
        n += P
    at["zero_causal"] = n
    n += P
    at["causal"] = n
    cols.append(np.zeros((P, P), np.float32))
    cols.append(np.where(i > j, np.float32(-1e30), np.float32(0)).astype(np.float32))
    n += P
    at["pool"] = n
    t = np.arange(16)
    pool = np.concatenate([1.0 / np.minimum(t + 1, w) for w in (2, 4, 8, 16)]).astype(np.float32)
    cols.append(np.broadcast_to(pool, (P, 64)))
    n += 64
    at["restart"] = n
    cols.append(np.broadcast_to((np.arange(TOK) % 64 != 0).astype(np.float32), (P, TOK)))
    n += TOK
    return np.ascontiguousarray(np.concatenate(cols, 1)), at


CONSTS, CONST_AT = shape_constants()

VEC = [("ffn1_norm", 8), ("mix_norm", 8), ("ffn2_norm", 8), ("mix_norm_2a", 8), ("ffn_norm_2a", 8),
       ("mix_norm_2b", 8), ("ffn_norm_2b", 8), ("conv", 48), ("pool_scale", 4), ("q_gain", 1), ("k_gain", 1),
       ("mu", 48), ("w0", 8), ("a0", 8), ("k_k", 8), ("k_a", 8), ("r_k", 8), ("ln_w", 8), ("ln_b", 8)]
VEC_AT = {}
_n = 0
for _name, _w in VEC:
    VEC_AT[_name] = _n
    _n += _w
VEC_COLS = _n


def lay_out_vectors(a):
    cm = lambda v: v.reshape(-1, P).T
    twice = lambda v: np.concatenate([v, v]).reshape(1, P).T
    parts = [cm(a["ffn1_norm"][0]), cm(a["mix_norm"][0]), cm(a["ffn2_norm"][0]), cm(a["mix_norm_2"][0]),
             cm(a["ffn_norm_2"][0]), cm(a["mix_norm_2"][1]), cm(a["ffn_norm_2"][1]),
             np.concatenate([cm(a["dn_conv_w"][0, k]) for k in range(4)], 1),
             cm(a["hy_pool_scale_2"][0]), twice(a["hy_q_gain_2"][0]), twice(a["hy_k_gain_2"][0]),
             np.concatenate([cm(a["rw_mu_2"][0, k]) for k in range(6)], 1),
             cm(a["rw_w0_2"][0]), cm(a["rw_a0_2"][0]), cm(a["rw_k_k_2"][0]), cm(a["rw_k_a_2"][0]),
             cm(a["rw_r_k_2"][0]), cm(a["rw_ln_w_2"][0]), cm(a["rw_ln_b_2"][0])]
    return np.ascontiguousarray(np.concatenate(parts, 1))


def build(nc, stream, consts, vectors, x_in, rows, kept_x, out):
    names = stream_plan(STAGES)
    CH = {name: c for c, name in enumerate(names)}
    NCH = len(names)
    ctx = ExitStack()
    with ctx:
        def sb(name, shape, dt=F32):
            return ctx.enter_context(nc.sbuf_tensor(name, shape, dt))

        def sem(name):
            return ctx.enter_context(nc.semaphore(name))

        raw = sb("raw", [P, RAW, CHUNK_COLS])
        whi = sb("whi", [P, SPLIT, CHUNK_COLS], F32R)
        wlo = sb("wlo", [P, SPLIT, CHUNK_COLS], F32R)
        hhi = sb("hhi", [P, KT, TOK], F32R)
        hlo = sb("hlo", [P, KT, TOK], F32R)
        ahi = sb("ahi", [P, 2, 2, TOK], F32R)
        alo = sb("alo", [P, 2, 2, TOK], F32R)
        x = sb("x", [P, TT, D])
        con = sb("con", [P, CONSTS.shape[1]])
        vec = sb("vec", [P, VEC_COLS])
        stat = sb("stat", [P, 64])
        ARENA = 23360
        arena = sb("arena", [P, ARENA])
        psum = ctx.enter_context(nc.psum_tensor("psum", [P, 8, 512], F32))

        def const(name, n=P):
            return con[:, CONST_AT[name]:CONST_AT[name] + n]

        def area(at, *shape):
            n = int(np.prod(shape))
            assert at + n <= ARENA, (at, shape)
            v = arena[:, at:at + n]
            if len(shape) == 2:
                v = v.rearrange("p (a b) -> p a b", a=shape[0])
            if len(shape) == 3:
                v = v.rearrange("p (a b c) -> p a b c", a=shape[0], b=shape[1])
            return v

        xn = area(0, TT, D)
        junk = area(2048, TT, D)
        sg = area(4096, 2, 512)
        act = area(5120, 2, 512)

        S = {}

        def s(name):
            if name not in S:
                S[name] = sem(name)
            return S[name]

        raw_loaded = [sem(f"raw_loaded{i}") for i in range(RAW)]
        for n in ("high_made", "low_made", "chunk_used", "const_loaded", "x_loaded", "stored",
                  "x_ready", "rms_squares", "rms_root", "rms_scale", "rows_scaled", "turned", "h_high", "h_low",
                  "act_step", "dve_step", "eps_ready"):
            s(n)
        x_ready = S["x_ready"]
        high_made, low_made, chunk_used = S["high_made"], S["low_made"], S["chunk_used"]

        STEPS_DONE = {}

        class Steps:

            def __init__(self, eng, name):
                self.eng, self.sem, self.n = eng, s(name), STEPS_DONE.get(name, 0)
                self.name = name

            def __call__(self, ins):
                ins.then_inc(self.sem, 1)
                self.n += 1
                STEPS_DONE[self.name] = self.n
                self.eng.wait_ge(self.sem, self.n)

        def high(eng, c, i=None):
            loaded, used, slot = 16 * (c // RAW + 1), c - SPLIT + 1, c % SPLIT
            eng.wait_ge(raw_loaded[c % RAW], loaded if i is None else loaded + 32 * i)
            if used > 0:
                eng.wait_ge(chunk_used, used if i is None else used + 6 * i)
            nc.scalar.activation(whi[:, slot, :], raw[:, c % RAW, :], ACT.Copy).then_inc(high_made, 1)

        x_base, bank_reads_before = {}, {}
        for k_, st_ in enumerate(STAGES):
            kind_ = {"mix1": "w_out", "fox": "hy_w_out", "rwkv": "rw_o"}.get(st_[0])
            if kind_:
                x_base[kind_] = 4 * k_

        norm_of, last_use, n = {}, {}, 0
        for st in STAGES:
            if st[0] != "rms":
                norm_of[st] = n
                n += 1
        firsts = [CH.get(("gate", st[1], 0)) for st in STAGES]

        class Highs:

            def __init__(self, eng):
                self.eng, self.next = eng, 0

            def upto(self, c):
                while self.next <= min(c, NCH - 1):
                    high(self.eng, self.next)
                    self.next += 1

        def three_passes(out, w_hi, w_lo, h_hi, h_lo, weights_stand, start, stop):
            if weights_stand:
                nc.tensor.matmul(out, w_hi, h_hi, start=start, stop=False)
                nc.tensor.matmul(out, w_hi, h_lo, start=False, stop=False)
                return nc.tensor.matmul(out, w_lo, h_hi, start=False, stop=stop)
            nc.tensor.matmul(out, h_hi, w_hi, start=start, stop=False)
            nc.tensor.matmul(out, h_hi, w_lo, start=False, stop=False)
            return nc.tensor.matmul(out, h_lo, w_hi, start=False, stop=stop)

        def columns_out(slot, bank, hi=hhi, lo=hlo):
            for j in range(2):
                for k in range(KT):
                    w = (slice(None), slot, slice(k * 256 + j * P, k * 256 + j * P + P))
                    mm = three_passes(psum[:, bank, j * 256:(j + 1) * 256], whi[w], wlo[w], hi[:, k, :], lo[:, k, :],
                                      True, k == 0, k == KT - 1)
            return mm

        def tokens_out(slot, bank, hi=hhi, lo=hlo, n=256):
            for m in range(TT):
                for k in range(KT):
                    w = (slice(None), slot, slice(k * 256, k * 256 + n))
                    t = (slice(None), k, slice(m * P, m * P + P))
                    mm = three_passes(psum[:, bank, m * 256:m * 256 + n], whi[w], wlo[w], hi[t], lo[t],
                                      False, k == 0, k == KT - 1)
            return mm

        NORMS = ["ffn1_norm", "mix_norm", "ffn2_norm", "mix_norm_2a", "ffn_norm_2a", "mix_norm_2b", "ffn_norm_2b"]

        def norm_scalar(eng, n, last_use, stage):
            if n == 0:
                eng.wait_ge(S["x_loaded"], 16)
            else:
                eng.wait_ge(x_ready, 4 * stage)
                eng.wait_ge(S["rms_scale"], 2 * n)
            for m in range(TT):
                nc.scalar.activation(junk[:, m, :], x[:, m, :], ACT.Square, scale=1.0 / 32, accum_out=stat[:, m:m + 1])\
                    .then_inc(S["rms_squares"], 1)
            eng.wait_ge(S["rms_squares"], 2 * (n + 1))
            nc.scalar.activation(stat[:, 2:4], stat[:, 0:2], ACT.Sqrt, bias=stat[:, 63:64]).then_inc(S["rms_root"], 1)
            if last_use is not None:
                eng.wait_ge(chunk_used, last_use + 1)
            gain = VEC_AT[NORMS[n]]
            for b in range(4):
                eng.wait_ge(S["turned"], 4 * n + b + 1)
                for k in (2 * b, 2 * b + 1):
                    nc.scalar.activation(hhi[:, k, :], psum[:, b, (k % 2) * 256:(k % 2) * 256 + 256], ACT.Copy,
                                         scale=vec[:, gain + k:gain + k + 1]).then_inc(S["h_high"], 1)

        def norm_vector(eng, n):
            eng.wait_ge(S["rms_root"], n + 1)
            nc.vector.reciprocal(stat[:, 4:6], stat[:, 2:4]).then_inc(S["rms_scale"], 1)
            eng.wait_ge(S["rms_scale"], 2 * n + 1)
            for m in range(TT):
                nc.vector.tensor_scalar(xn[:, m, :], x[:, m, :], stat[:, 4 + m:5 + m], None, ALU.mult)\
                    .then_inc(S["rows_scaled"], 1)
            gain = VEC_AT[NORMS[n]]
            for b in range(4):
                for k in (2 * b, 2 * b + 1):
                    eng.wait_ge(S["h_high"], 8 * n + 2 * b + 2)
                    ins = nc.vector.scalar_tensor_tensor(
                        out=hlo[:, k, :], in0=psum[:, b, (k % 2) * 256:(k % 2) * 256 + 256],
                        scalar=vec[:, gain + k:gain + k + 1], in1=hhi[:, k, :].bitcast(F32),
                        op0=ALU.mult, op1=ALU.subtract)
                    ins.then_inc(S["h_low"], 1)
            eng.wait_ge(S["h_low"], 8 * n + 8)
            nc.vector.tensor_copy(stat[:, 6:7], stat[:, 5:6]).then_inc(S["rms_scale"], 1)

        def norm_tensor(eng, n):
            for b in range(4):
                if n:
                    eng.wait_ge(S["h_low"], 8 * n)
                for k in (2 * b, 2 * b + 1):
                    for m in range(TT):
                        eng.wait_ge(S["rows_scaled"], 2 * n + m + 1)
                        at = (k % 2) * 256 + m * P
                        mm = nc.tensor.transpose(psum[:, b, at:at + P], xn[:, m, k * P:(k + 1) * P], const("ident"))
                mm.then_inc(S["turned"], 1)

        def ffn_tensor(eng, f, n):
            product, act_low = s("ffn_product"), s("ffn_act_low")
            c0 = CH[("gate", f, 0)]

            def step(kind, c, g, start=False, stop=False, i=None):
                b, slot, more = g % 2, c % SPLIT, lambda v, k: v if i is None else v + k * i
                eng.wait_ge(low_made, more(c + 1, 6))
                if kind == "gate":
                    if g >= 2:
                        eng.wait_ge(product, GROUPS * f + more(g - 1, 2))
                    columns_out(slot, b).then_inc(chunk_used, 1)
                if kind == "up":
                    columns_out(slot, 2 + b).then_inc(chunk_used, 1)
                if kind == "down":
                    eng.wait_ge(act_low, GROUPS * f + more(g + 1, 2))
                    for m in range(TT):
                        for half in range(2):
                            for j in range(2):
                                t = (slice(None), b, j, slice(m * P, m * P + P))
                                w = (slice(None), slot, slice(j * D + half * 512, j * D + half * 512 + 512))
                                mm = three_passes(psum[:, 4 + 2 * m + half, :], whi[w], wlo[w], ahi[t], alo[t],
                                                  False, start and j == 0, stop and j == 1)
                    mm.then_inc(chunk_used, 1)

            def group(c, g, start=False, i=None):
                step("gate", c, g, i=i)
                step("up", c + 1, g, i=i)
                step("down", c + 2, g - 1, start=start, i=i)

            eng.wait_ge(S["h_low"], 8 * n + 8)
            step("gate", c0, 0)
            step("up", c0 + 1, 0)
            group(c0 + 2, 1, start=True)
            group(c0 + 5, 2)
            with eng.Fori(0, (GROUPS - 3) // 2) as i:
                group(c0 + 8, 3, i=i)
                group(c0 + 11, 4, i=i)
            step("down", c0 + 32, GROUPS - 1, stop=True)

        def ffn_scalar(eng, f, highs):
            silu_done, act_high, product = s("ffn_silu_done"), s("ffn_act_high"), s("ffn_product")
            c0 = CH[("gate", f, 0)]

            def silu(c, g, i=None):
                more = lambda v, k: v if i is None else v + k * i
                eng.wait_ge(chunk_used, more(c + 1, 6))
                if g >= 2:
                    eng.wait_ge(product, GROUPS * f + more(g - 1, 2))
                nc.scalar.activation(sg[:, g % 2, :], psum[:, g % 2, :], ACT.Silu).then_inc(silu_done, 1)

            def act_highs(c, g, i=None):
                more = lambda v, k: v if i is None else v + k * i
                eng.wait_ge(product, GROUPS * f + more(g + 1, 2))
                if g >= 2:
                    eng.wait_ge(chunk_used, more(c, 6))
                b = g % 2
                nc.scalar.activation(ahi[:, b, :, :], act[:, b, :].rearrange("p (a b) -> p a b", a=2), ACT.Copy)\
                    .then_inc(act_high, 1)

            def group(c, g, i=None):
                if i is None:
                    highs.upto(c + 3)
                else:
                    high(eng, c + 3, i)
                silu(c, g, i)
                if i is None:
                    highs.upto(c + 4)
                else:
                    high(eng, c + 4, i)
                act_highs(c, g, i)
                if i is None:
                    highs.upto(c + 5)
                else:
                    high(eng, c + 5, i)

            highs.upto(c0 + 2)
            silu(c0, 0)
            highs.upto(c0 + 3)
            act_highs(c0, 0)
            highs.upto(c0 + 4)
            group(c0 + 2, 1)
            group(c0 + 5, 2)
            with eng.Fori(0, (GROUPS - 5) // 2) as i:
                group(c0 + 8, 3, i)
                group(c0 + 11, 4, i)
            highs.next = c0 + 8 + 3 * (GROUPS - 5) + 3
            group(c0 + 26, 9)
            group(c0 + 29, 10)

        def ffn_vector(eng, f, factor):
            silu_done, act_high, act_low = s("ffn_silu_done"), s("ffn_act_high"), s("ffn_act_low")
            product = s("ffn_product")
            c0 = CH[("gate", f, 0)]

            def group(c, g, i=None):
                more = lambda v, k: v if i is None else v + k * i
                b = g % 2
                eng.wait_ge(silu_done, GROUPS * f + more(g + 1, 2))
                eng.wait_ge(chunk_used, more(c + 2, 6))
                if g >= 2:
                    eng.wait_ge(act_low, GROUPS * f + more(g - 1, 2))
                nc.vector.tensor_tensor(act[:, b, :], sg[:, b, :], psum[:, 2 + b, :], ALU.mult).then_inc(product, 1)
                eng.wait_ge(act_high, GROUPS * f + more(g + 1, 2))
                flat = lambda t: t[:, b, :, :].rearrange("p a b -> p (a b)")
                nc.vector.tensor_tensor(flat(alo), act[:, b, :], flat(ahi).bitcast(F32), ALU.subtract)\
                    .then_inc(act_low, 1)

            group(c0, 0)
            group(c0 + 2, 1)
            group(c0 + 5, 2)
            with eng.Fori(0, (GROUPS - 3) // 2) as i:
                group(c0 + 8, 3, i)
                group(c0 + 11, 4, i)
            eng.wait_ge(chunk_used, c0 + 33)
            for m in range(TT):
                for half in range(2):
                    xs = x[:, m, half * 512:half * 512 + 512]
                    nc.vector.scalar_tensor_tensor(out=xs, in0=psum[:, 4 + 2 * m + half, :], scalar=factor, in1=xs,
                                                   op0=ALU.mult, op1=ALU.add).then_inc(x_ready, 1)

        LEVELS = (2, 4, 8, 16, 32)
        for n_ in ("inv_start", "inv_turned", "inv_copied", "inv_masked", "inv_x", "inv_x_copied", "inv_summed",
                   "inv_updated"):
            s(n_)
        INV = {k: S[k] for k in S if k.startswith("inv_")}

        def inverse_vector(eng, u, steps, LT, T, TTr, NT, ident4, op=ALU.subtract, x_shares=False):
            for g in range(2):
                steps(nc.vector.tensor_tensor(NT[g], LT[g], four(const("level1")), ALU.mult))
                nc.vector.tensor_tensor(TTr[g], ident4, NT[g], op).then_inc(INV["inv_start"], 1)
            for n, size in enumerate(LEVELS):
                for g in range(2):
                    if n:
                        eng.wait_ge(INV["inv_summed" if x_shares else "inv_x"], 10 * u + 2 * (n - 1) + g + 1)
                    else:
                        eng.wait_ge(INV["inv_start"], 2 * u + g + 1)
                    nc.vector.tensor_tensor(NT[g], LT[g], four(const(f"level{size}")), ALU.mult)\
                        .then_inc(INV["inv_masked"], 1)
                for g in range(2):
                    eng.wait_ge(INV["inv_summed"], 10 * u + 2 * n + g + 1)
                    if n < len(LEVELS) - 1:
                        nc.vector.tensor_tensor(T[g], T[g], bank4(3 * g + 1), op).then_inc(steps.sem, 1)
                        steps.n += 1
                        STEPS_DONE[steps.name] = steps.n
                    nc.vector.tensor_tensor(TTr[g], TTr[g], bank4(3 * g + 2), op)\
                        .then_inc(INV["inv_updated"], 1)

        def inverse_scalar(eng, u, T, X):
            for g in range(2):
                eng.wait_ge(INV["inv_turned"], 2 * u + g + 1)
                nc.scalar.activation(T[g], bank4(3 * g + 1), ACT.Copy).then_inc(INV["inv_copied"], 1)
            for n in range(len(LEVELS)):
                for g in range(2):
                    eng.wait_ge(INV["inv_x"], 10 * u + 2 * n + g + 1)
                    nc.scalar.activation(X[g], bank4(3 * g), ACT.Copy).then_inc(INV["inv_x_copied"], 1)

        def inverse_tensor(eng, u, T, TTr, NT, X):
            for g in range(2):
                eng.wait_ge(INV["inv_start"], 2 * u + g + 1)
                for h in range(4):
                    mm = nc.tensor.transpose(bank4(3 * g + 1)[:, h, :], TTr[g][:, h, :], const("ident"))
                mm.then_inc(INV["inv_turned"], 1)
            for n in range(len(LEVELS)):
                for g in range(2):
                    eng.wait_ge(INV["inv_masked"], 10 * u + 2 * n + g + 1)
                    if n:
                        eng.wait_ge(INV["inv_updated"], 10 * u + 2 * (n - 1) + g + 1)
                    else:
                        eng.wait_ge(INV["inv_copied"], 2 * u + g + 1)
                    for h in range(4):
                        mm = nc.tensor.matmul(bank4(3 * g)[:, h, :], NT[g][:, h, :], T[g][:, h, :], start=True, stop=True)
                    mm.then_inc(INV["inv_x"], 1)
                for g in range(2):
                    eng.wait_ge(INV["inv_x_copied"], 10 * u + 2 * n + g + 1)
                    for h in range(4):
                        if n < len(LEVELS) - 1:
                            nc.tensor.matmul(bank4(3 * g + 1)[:, h, :], TTr[g][:, h, :], X[g][:, h, :], start=True, stop=True)
                    for h in range(4):
                        mm = nc.tensor.matmul(bank4(3 * g + 2)[:, h, :], X[g][:, h, :], TTr[g][:, h, :], start=True, stop=True)
                    mm.then_inc(INV["inv_summed"], 1)

        def four(m):
            return m.rearrange("p (a n) -> p a n", a=1).broadcast_to((P, 4, m.shape[1]))

        def bank4(b):
            return psum[:, b, :].rearrange("p (a n) -> p a n", a=4)

        def bank2(b):
            return psum[:, b, :].rearrange("p (a n) -> p a n", a=2)

        bank_read = {6: s("bank_read6"), 7: s("bank_read7")}
        PROJ = {}
        inv0 = {"rwkv": 1 if ("mix1", 0) in STAGES else 0}
        for c_, name_ in enumerate(names):
            if name_[0] in ("w_in", "hy_w_in", "rw"):
                PROJ[name_] = len(PROJ)

        def proj_bank(name):
            return 6 + PROJ[name] % 2

        def project(eng, name, form, **kw):
            c, q = CH[name], PROJ[name]
            eng.wait_ge(low_made, c + 1)
            if q >= 2:
                eng.wait_ge(bank_read[6 + q % 2], q // 2)
            form(c % SPLIT, 6 + q % 2, **kw).then_inc(chunk_used, 1)

        def projected(eng, name):
            eng.wait_ge(chunk_used, CH[name] + 1)

        def read(ins, name):
            return ins.then_inc(bank_read[proj_bank(name)], 1)

        def add_out(eng, kind):
            for j in range(4):
                name = (kind, 0, j)
                projected(eng, name)
                xs = x[:, :, j * 256:(j + 1) * 256]
                nc.vector.tensor_tensor(xs, xs, bank2(6 + j % 2), ALU.add).then_inc(x_ready, 1)

        def out_tensor(eng, kind, ready, count):
            eng.wait_ge(ready, count)
            for j in range(4):
                c = CH[(kind, 0, j)]
                eng.wait_ge(low_made, c + 1)
                if j < 2:
                    eng.wait_ge(bank_read[6 + j], sum(1 for n_, q_ in PROJ.items() if CH[n_] < c and q_ % 2 == j))
                else:
                    eng.wait_ge(x_ready, x_base[kind] + j - 1)
                tokens_out(c % SPLIT, 6 + j % 2).then_inc(chunk_used, 1)

        cin = area(0, 12, 260)
        sq = area(3120, 8, 256)
        rs = area(5168, 8, 256)
        Dm = [area(0 + 512 * g, 4, P) for g in range(2)]
        NTm = Dm
        LTm = [area(1024 + 512 * g, 4, P) for g in range(2)]
        ATm = [area(2048 + 512 * g, 4, P) for g in range(2)]
        Tm = [area(3072 + 512 * g, 4, P) for g in range(2)]
        TTm = [area(4096 + 512 * g, 4, P) for g in range(2)]
        Xm = [area(5120 + 512 * g, 4, P) for g in range(2)]
        ngB = Xm
        qkv = area(7216, 12, 256)
        ktok = area(10288, 2, 512)
        vtok = area(11312, 2, 512)
        zg = area(12336, 2, 512)
        va = area(13360, 2, 512)
        yraw = area(14384, 4, 256)
        wsT = area(15408, 8, P)
        ws = area(16432, 8, P)
        Om = area(16432, 2, 512)
        lnp = area(17456, 2, 512)
        gbias = area(18480, 4, P)
        sm = area(18992, 256)
        Rm = area(19248, 4, P)
        Wb = area(19760, 2, 512)
        Sm = area(20784, 4, P)
        OQ = area(21296, 4, P)
        osq = area(21808, 2, 512)
        dnn = area(22832, P)
        alog = area(22960, 8)

        ba_y, ba_abs, ba_beta, ba_g, ba_l = (sm[:, 8 * k:8 * k + 8] for k in range(5))
        ex = sm[:, 40:72].rearrange("p (m k h) -> p m k h", m=2, k=4)
        neg_eg = sm[:, 72:80]
        bd = sm[:, 80:88]
        lnst = sm[:, 96:108]
        mv = sm[:, 108:112]
        lnr = sm[:, 112:116]
        osum = sm[:, 120:128]
        ort = sm[:, 128:136]
        orr = sm[:, 136:144]
        ealog = sm[:, 144:148]
        spl = sm[:, 152:160]
        mh = lambda v: v.rearrange("p (m h) -> p m h", m=2)
        QKV = {6: 4, 7: 6, 4: 0, 5: 2, 8: 8, 9: 10}

        def mix1_scalar(eng, highs, st):
            n, stage = norm_of[st], STAGES.index(st)
            eng.wait_ge(x_ready, 4 * stage)
            eng.dma_start(ws, rows["gm_w_s"].rearrange("g i j -> i g j")).then_inc(s("m1_loaded"), 16)
            eng.dma_start(lnp[:, 0, :], rows["gm_ln_g"].partition_broadcast(P)).then_inc(s("m1_loaded"), 16)
            eng.dma_start(lnp[:, 1, :], rows["gm_ln_b"].partition_broadcast(P)).then_inc(s("m1_loaded"), 16)
            eng.dma_start(gbias, rows["gm_bias"]).then_inc(s("m1_loaded"), 16)
            eng.dma_start(dnn, rows["dn_norm"].partition_broadcast(P)).then_inc(s("m1_loaded"), 16)
            eng.dma_start(alog, rows["gates"].partition_broadcast(P)).then_inc(s("m1_loaded"), 16)
            norm_scalar(eng, n, CH[("w_in", 0, 12)] - 1, stage)
            highs.upto(CH[("w_in", 0, 12)] + 2)
            steps = Steps(eng, "act_step")
            projected(eng, ("w_in", 0, 12))
            eng.wait_ge(s("m1_y"), 1)
            read(nc.scalar.activation(mh(ba_beta), bank2(proj_bank(("w_in", 0, 12)))[:, :, 0:4], ACT.Sigmoid),
                 ("w_in", 0, 12))
            steps(nc.scalar.activation(ba_abs, ba_y, ACT.Abs))
            eng.wait_ge(S["m1_loaded"], 96)
            nc.scalar.activation(ealog, alog[:, 0:4], ACT.Exp).then_inc(s("m1_sp"), 1)
            steps(nc.scalar.activation(ba_abs, ba_abs, ACT.Exp, scale=-1.0))
            nc.scalar.activation(ba_l, ba_abs, ACT.Ln, bias=stat[:, 62:63]).then_inc(s("m1_sp"), 1)

            def conv_in(j):
                name = ("w_in", 0, j)
                highs.upto(CH[name] + 2)
                projected(eng, name)
                t = QKV[j]
                if j == 6:
                    eng.wait_ge(s("m1_pads"), 1)
                read(nc.scalar.activation(cin[:, t:t + 2, 3:259], bank2(proj_bank(name)), ACT.Copy), name)

            def silu(j, order):
                t = QKV[j]
                eng.wait_ge(s("m1_conv"), order + 1)
                nc.scalar.activation(qkv[:, t:t + 2, :], qkv[:, t:t + 2, :], ACT.Silu).then_inc(s("m1_silu"), 1)
                if t < 8:
                    eng.wait_ge(S["m1_silu"], order + 1)
                    nc.scalar.activation(sq[:, t:t + 2, :], qkv[:, t:t + 2, :], ACT.Square).then_inc(s("m1_sq"), 1)

            for order, j in enumerate((6, 7, 4, 5, 8, 9)):
                conv_in(j)
                if order:
                    silu((6, 7, 4, 5, 8, 9)[order - 1], order - 1)
            silu(9, 5)
            for j in (10, 11):
                name = ("w_in", 0, j)
                highs.upto(CH[name] + 2)
                projected(eng, name)
                zc = zg[:, :, (j - 10) * 256:(j - 10) * 256 + 256]
                nc.scalar.activation(zc, bank2(proj_bank(name)), ACT.Silu).then_inc(bank_read[proj_bank(name)], 1)
            for j in (2, 3):
                name = ("w_in", 0, j)
                highs.upto(CH[name] + 2)
                projected(eng, name)
                nc.scalar.activation(va[:, :, (j - 2) * 256:(j - 2) * 256 + 256], bank2(proj_bank(name)),
                                     ACT.Gelu_apprx_tanh).then_inc(bank_read[proj_bank(name)], 1)
            for j in (0, 1):
                name = ("w_in", 0, j)
                highs.upto(CH[name] + 2)
                projected(eng, name)
                nc.scalar.activation(yraw[:, 2 * j:2 * j + 2, :], bank2(proj_bank(name)),
                                     ACT.Gelu_apprx_tanh).then_inc(bank_read[proj_bank(name)], 1)
            highs.upto(CH[("w_in", 0, 1)] + 3)
            for b in range(4):
                eng.wait_ge(s("m1_sums"), b + 1)
                nc.scalar.activation(rs[:, 2 * b:2 * b + 2, :], bank2(b), ACT.Sqrt, scale=float(P) if b < 2 else 1.0,
                                     bias=stat[:, 61:62] if b < 2 else stat[:, 63:64]).then_inc(s("m1_root"), 1)
            eng.wait_ge(s("m1_var"), 1)
            nc.scalar.activation(lnr[:, 0:2], mv.rearrange("p (m k) -> p m k", m=2)[:, :, 1], ACT.Sqrt,
                                 bias=stat[:, 63:64]).then_inc(s("m1_lnroot"), 1)
            for k, dst in enumerate((ktok[:, 0, :], ktok[:, 1, :], vtok[:, 0, :], vtok[:, 1, :])):
                eng.wait_ge(s("m1_kvturned"), k + 1)
                nc.scalar.activation(dst, psum[:, k, :], ACT.Copy).then_inc(s("m1_kvtok"), 1)
            eng.wait_ge(s("m1_gsums"), 1)
            nc.scalar.activation(ex, psum[:, 5, 0:32].rearrange("p (m k h) -> p m k h", m=2, k=4), ACT.Exp)\
                .then_inc(s("m1_ex"), 1)
            for m in range(2):
                eng.wait_ge(s("m1_dlog"), m + 1)
                nc.scalar.activation(Dm[m], Dm[m], ACT.Exp).then_inc(s("m1_dexp"), 1)
            inverse_scalar(eng, 0, Tm, Xm)
            for c in range(4):
                r = slice((c % 2) * 64, (c % 2) * 64 + 64)
                eng.wait_ge(s("m1_ks"), c + 1)
                if c:
                    eng.wait_ge(s("m1_o"), c)
                for h in range(4):
                    nc.scalar.activation(OQ[r, h, :], psum[r, 1, h * P:(h + 1) * P], ACT.Copy,
                                         scale=ex[r, c // 2, 0, h:h + 1]).then_inc(s("m1_oq"), 1)
            for m in range(2):
                eng.wait_ge(s("m1_o"), 2 * m + 2)
                nc.scalar.activation(osq[:, m, :], Om[:, m, :], ACT.Square).then_inc(s("m1_osq"), 1)
            eng.wait_ge(s("m1_osum"), 2)
            nc.scalar.activation(ort, osum, ACT.Sqrt, scale=1.0 / P, bias=stat[:, 63:64]).then_inc(s("m1_oroot"), 1)
            eng.wait_ge(s("m1_gated"), 2)
            eng.wait_ge(chunk_used, CH[("w_in", 0, 1)] + 1)
            nc.scalar.activation(hhi[:, 0:4, :], yraw, ACT.Copy).then_inc(s("m1_yhi"), 1)
            for b in range(2):
                eng.wait_ge(s("m1_oturned"), b + 1)
                nc.scalar.activation(hhi[:, 4 + 2 * b:6 + 2 * b, :], bank2(b), ACT.Copy).then_inc(s("m1_yhi"), 1)
            for j in range(4):
                highs.upto(CH[("w_out", 0, j)] + 3)

        def mix1_vector(eng, st):
            norm_vector(eng, norm_of[st])
            steps = Steps(eng, "dve_step")
            eng.wait_ge(chunk_used, CH[("w_in", 0, 12)] + 1)
            eng.wait_ge(s("m1_loaded"), 96)
            nc.vector.tensor_tensor(mh(ba_y), bank2(proj_bank(("w_in", 0, 12)))[:, :, 4:8],
                                    alog[:, 4:8].rearrange("p (a h) -> p a h", a=1).broadcast_to((P, 2, 4)), ALU.add)\
                .then_inc(s("m1_y"), 1)
            nc.vector.memset(cin[:, :, 0:3], 0.0).then_inc(s("m1_pads"), 1)
            eng.wait_ge(S["m1_y"], 1)
            steps(nc.vector.tensor_scalar(spl, ba_y, 0.0, None, ALU.max))
            eng.wait_ge(s("m1_sp"), 2)
            steps(nc.vector.tensor_tensor(spl, spl, ba_l, ALU.add))
            nc.vector.scalar_tensor_tensor(out=mh(ba_g), in0=mh(spl), scalar=-1.0,
                                           in1=ealog.rearrange("p (a h) -> p a h", a=1).broadcast_to((P, 2, 4)),
                                           op0=ALU.mult, op1=ALU.mult).then_inc(s("m1_g"), 1)
            nc.vector.memset(Rm, 0.0).then_inc(s("m1_zero"), 1)
            nc.vector.memset(Wb, 0.0).then_inc(S["m1_zero"], 1)
            nc.vector.memset(Sm, 0.0).then_inc(S["m1_zero"], 1)
            for b in range(2):
                eng.wait_ge(s("m1_wturned"), b + 1)
                nc.vector.tensor_tensor(wsT[:, 4 * b:4 * b + 4, :], bank4(4 + b), four(const("gm_mask")), ALU.mult)\
                    .then_inc(s("m1_wsT"), 1)
            for order, j in enumerate((6, 7, 4, 5, 8, 9)):
                name = ("w_in", 0, j)
                eng.wait_ge(bank_read[proj_bank(name)], PROJ[name] // 2 + 1)
                for t in (QKV[j], QKV[j] + 1):
                    w = lambda k: vec[:, VEC_AT["conv"] + 12 * k + t:VEC_AT["conv"] + 12 * k + t + 1]
                    steps(nc.vector.tensor_scalar(qkv[:, t, :], cin[:, t, 3:259], w(3), None, ALU.mult))
                    for k in (2, 1, 0):
                        ins = nc.vector.scalar_tensor_tensor(out=qkv[:, t, :], in0=cin[:, t, k:k + 256], scalar=w(k),
                                                             in1=qkv[:, t, :], op0=ALU.mult, op1=ALU.add)
                        if k:
                            steps(ins)
                    if t == QKV[j]:
                        steps(ins)
                ins.then_inc(s("m1_conv"), 1)
            eng.wait_ge(bank_read[proj_bank(("w_in", 0, 2))], PROJ[("w_in", 0, 2)] // 2 + 1)
            eng.wait_ge(bank_read[proj_bank(("w_in", 0, 3))], PROJ[("w_in", 0, 3)] // 2 + 1)
            for m in range(2):
                steps(nc.vector.bn_stats(lnst[:, 6 * m:6 * m + 6], va[:, m, :]))
            steps(nc.vector.bn_aggr(mv[:, 0:2], lnst[:, 0:6]))
            nc.vector.bn_aggr(mv[:, 2:4], lnst[:, 6:12]).then_inc(s("m1_var"), 1)
            for b in range(4):
                eng.wait_ge(s("m1_root"), b + 1)
                steps(nc.vector.reciprocal(rs[:, 2 * b:2 * b + 2, :], rs[:, 2 * b:2 * b + 2, :]))
                nc.vector.tensor_tensor(qkv[:, 2 * b:2 * b + 2, :], qkv[:, 2 * b:2 * b + 2, :], rs[:, 2 * b:2 * b + 2, :],
                                        ALU.mult).then_inc(s("m1_unit"), 1)
            eng.wait_ge(s("m1_lnroot"), 1)
            steps(nc.vector.reciprocal(lnr[:, 2:4], lnr[:, 0:2]))
            for m in range(2):
                steps(nc.vector.tensor_scalar(va[:, m, :], va[:, m, :], mv[:, 2 * m:2 * m + 1], lnr[:, 2 + m:3 + m],
                                              ALU.subtract, ALU.mult))
            for k, op in enumerate((ALU.mult, ALU.add)):
                ins = nc.vector.tensor_tensor(va, va, lnp[:, k:k + 1, :].broadcast_to((P, 2, 512)), op)
                if k == 0:
                    steps(ins)
            ins.then_inc(s("m1_ln"), 1)
            eng.wait_ge(S["m1_g"], 1)
            eng.wait_ge(S["m1_unit"], 4)
            for m in range(2):
                nc.vector.tensor_scalar(ngB[m], mh(ba_g)[:, m, :].rearrange("p (h a) -> p h a", a=1).broadcast_to((P, 4, P)),
                                        -1.0, None, ALU.mult).then_inc(s("m1_ngB"), 1)
            eng.wait_ge(s("m1_ex"), 1)
            nc.vector.tensor_scalar(mh(neg_eg), ex[:, :, 0, :], -1.0, None, ALU.mult).then_inc(s("m1_bd"), 1)
            eng.wait_ge(bank_read[proj_bank(("w_in", 0, 12))], PROJ[("w_in", 0, 12)] // 2 + 1)
            nc.vector.tensor_tensor(mh(bd), mh(ba_beta), ex[:, :, 1, :], ALU.mult).then_inc(s("m1_bd"), 1)
            for m in range(2):
                eng.wait_ge(s("m1_dpsum"), m + 1)
                nc.vector.tensor_scalar(Dm[m], bank4(m), 0.0, None, ALU.min).then_inc(s("m1_dlog"), 1)
            over = lambda v: v.rearrange("p (h a) -> p h a", a=1).broadcast_to((P, 4, P))
            for m in range(2):
                eng.wait_ge(s("m1_dexp"), m + 1)
                steps(nc.vector.tensor_tensor(Dm[m], Dm[m], four(const("upto")), ALU.mult))
                steps(nc.vector.tensor_tensor(Dm[m], Dm[m], over(mh(ba_beta)[:, m, :]), ALU.mult))
                eng.wait_ge(s("m1_kk"), m + 1)
                steps(nc.vector.tensor_tensor(LTm[m], bank4(m), Dm[m], ALU.mult))
                steps(nc.vector.tensor_tensor(ATm[m], bank4(2 + m), Dm[m], ALU.mult))
            eng.wait_ge(s("m1_kvtok"), 4)
            eng.wait_ge(S["m1_bd"], 2)
            for m in range(2):
                kt4 = ktok[:, m, :].rearrange("p (h d) -> p h d", h=4)
                nc.vector.tensor_tensor(kt4, kt4, over(mh(bd)[:, m, :]), ALU.mult).then_inc(s("m1_kd"), 1)
            inverse_vector(eng, 0, steps, LTm, Tm, TTm, NTm, four(const("ident")))
            for m in range(2):
                eng.wait_ge(s("m1_mixed"), m + 1)
                steps(nc.vector.tensor_tensor(osq[:, m, :].rearrange("p (a n) -> p a n", a=4), bank4(4 + m), gbias, ALU.add))
                ys = yraw[:, :, m * P:(m + 1) * P]
                nc.vector.tensor_tensor(ys, ys, osq[:, m, :].rearrange("p (a n) -> p a n", a=4), ALU.mult)\
                    .then_inc(s("m1_gated"), 1)
            steps(nc.vector.tensor_tensor(zg.rearrange("p m (h d) -> p (m h) d", h=4), zg.rearrange("p m (h d) -> p (m h) d", h=4),
                                          dnn.rearrange("p (a d) -> p a d", a=1).broadcast_to((P, 8, P)), ALU.mult))
            eng.wait_ge(S["m1_zero"], 3)
            for c in range(4):
                m, r = c // 2, slice((c % 2) * 64, (c % 2) * 64 + 64)
                eng.wait_ge(s("m1_ks"), c + 1)
                for h in range(4):
                    nc.vector.scalar_tensor_tensor(out=Rm[r, h, :], in0=psum[r, 0, h * P:(h + 1) * P],
                                                   scalar=neg_eg[r, 4 * m + h:4 * m + h + 1],
                                                   in1=vtok[r, m, h * P:(h + 1) * P], op0=ALU.mult, op1=ALU.add)\
                        .then_inc(s("m1_r"), 1)
                eng.wait_ge(s("m1_w"), c + 1)
                nc.vector.tensor_copy(Wb[r, c % 2, :], psum[r, 2, :]).then_inc(s("m1_wb"), 1)
                if c < 3:
                    eng.wait_ge(s("m1_spsum"), c + 1)
                    for h in range(4):
                        nc.vector.scalar_tensor_tensor(out=Sm[:, h, :], in0=Sm[:, h, :], scalar=ex[:, m, 2 + c % 2, h:h + 1],
                                                       in1=psum[:, 4, h * P:(h + 1) * P], op0=ALU.mult, op1=ALU.add)\
                            .then_inc(s("m1_s"), 1)
                eng.wait_ge(s("m1_opsum"), c + 1)
                eng.wait_ge(s("m1_oq"), 4 * c + 4)
                nc.vector.tensor_tensor(Om[r, m, :], psum[r, 3, :], OQ[r, :, :].rearrange("p h d -> p (h d)"), ALU.add)\
                    .then_inc(s("m1_o"), 1)
            for m in range(2):
                eng.wait_ge(s("m1_osq"), m + 1)
                nc.vector.tensor_reduce(osum[:, 4 * m:4 * m + 4], osq[:, m, :].rearrange("p (h d) -> p h d", h=4), AX_X, ALU.add)\
                    .then_inc(s("m1_osum"), 1)
            eng.wait_ge(s("m1_oroot"), 1)
            steps(nc.vector.reciprocal(orr, ort))
            for m in range(2):
                o4 = Om[:, m, :].rearrange("p (h d) -> p h d", h=4)
                steps(nc.vector.tensor_tensor(o4, o4, over(orr[:, 4 * m:4 * m + 4]), ALU.mult))
                nc.vector.tensor_tensor(Om[:, m, :], Om[:, m, :], zg[:, m, :], ALU.mult).then_inc(s("m1_on"), 1)
            eng.wait_ge(s("m1_yhi"), 1)
            nc.vector.tensor_tensor(hlo[:, 0:4, :], yraw, hhi[:, 0:4, :].bitcast(F32), ALU.subtract).then_inc(s("m1_ylo"), 1)
            for b in range(2):
                eng.wait_ge(S["m1_yhi"], b + 2)
                nc.vector.tensor_tensor(hlo[:, 4 + 2 * b:6 + 2 * b, :], bank2(b), hhi[:, 4 + 2 * b:6 + 2 * b, :].bitcast(F32),
                                        ALU.subtract).then_inc(s("m1_ylo"), 1)
            add_out(eng, "w_out")

        def mix1_tensor(eng, st):
            norm_tensor(eng, norm_of[st])
            eng.wait_ge(s("m1_loaded"), 96)
            for b in range(2):
                for g in range(4):
                    mm = nc.tensor.transpose(bank4(4 + b)[:, g, :], ws[:, 4 * b + g, :], const("ident"))
                mm.then_inc(s("m1_wturned"), 1)
            eng.wait_ge(S["h_low"], 8 * norm_of[st] + 8)
            project(eng, ("w_in", 0, 12), tokens_out, n=8)
            for j in (6, 7, 4, 5, 8, 9):
                project(eng, ("w_in", 0, j), columns_out)
            for j in (10, 11, 2, 3):
                project(eng, ("w_in", 0, j), tokens_out)
            for j in (0, 1):
                project(eng, ("w_in", 0, j), columns_out)
            eng.wait_ge(s("m1_sq"), 4)
            for b in range(4):
                nc.tensor.matmul(psum[:, b, :], const("ones"), sq[:, 2 * b:2 * b + 2, :], start=True, stop=True)\
                    .then_inc(s("m1_sums"), 1)
            eng.wait_ge(s("m1_g"), 1)
            eng.wait_ge(s("m1_wsT"), 2)
            for m in range(2):
                for k, mat in enumerate(("upto", "after", "chunk0", "chunk1")):
                    mm = nc.tensor.matmul(psum[:, 5, 16 * m + 4 * k:16 * m + 4 * k + 4], const(mat), mh(ba_g)[:, m, :],
                                          start=True, stop=True)
            mm.then_inc(s("m1_gsums"), 1)
            eng.wait_ge(s("m1_unit"), 4)
            eng.wait_ge(s("m1_silu"), 6)
            for k, (t0, m) in enumerate(((4, 0), (4, 1), (8, 0), (8, 1))):
                eng.wait_ge(s("m1_root"), 4)
                for h in range(4):
                    mm = nc.tensor.transpose(bank4(k)[:, h, :], qkv[:, t0 + h, m * P:(m + 1) * P], const("ident"))
                mm.then_inc(s("m1_kvturned"), 1)
            eng.wait_ge(s("m1_ngB"), 2)
            for m in range(2):
                eng.wait_ge(s("m1_kvtok"), m + 1)
                nc.tensor.matmul(bank4(m), const("upto"), ngB[m], start=True, stop=False)
                for h in range(4):
                    mm = nc.tensor.matmul(bank4(m)[:, h, :], ngB[m][:, h, :], const("neg_upto"), start=False, stop=h == 3)
                mm.then_inc(s("m1_dpsum"), 1)
            for m in range(2):
                eng.wait_ge(s("m1_dlog"), m + 1)
                eng.wait_ge(s("m1_kvtok"), 3 + m)
                for h in range(4):
                    nc.tensor.matmul(bank4(m)[:, h, :], qkv[:, 4 + h, m * P:(m + 1) * P], qkv[:, 4 + h, m * P:(m + 1) * P],
                                     start=True, stop=True)
                for h in range(4):
                    mm = nc.tensor.matmul(bank4(2 + m)[:, h, :], qkv[:, 4 + h, m * P:(m + 1) * P],
                                          qkv[:, h, m * P:(m + 1) * P], start=True, stop=True)
                mm.then_inc(s("m1_kk"), 1)
            inverse_tensor(eng, 0, Tm, TTm, NTm, Xm)
            eng.wait_ge(s("m1_ln"), 1)
            eng.wait_ge(INV["inv_updated"], 10)
            for m in range(2):
                for g in range(8):
                    p0 = (g % 2) * 64
                    mm = nc.tensor.matmul(psum[p0:p0 + 64, 4 + m, (g // 2) * P:(g // 2) * P + P], va[:, m, g * 64:g * 64 + 64],
                                          wsT[:, g, :], start=True, stop=True)
                mm.then_inc(s("m1_mixed"), 1)
            for c in range(4):
                m, tok = c // 2, slice((c // 2) * P, (c // 2) * P + P)
                if c == 0:
                    eng.wait_ge(s("m1_zero"), 3)
                    eng.wait_ge(s("m1_gated"), 2)
                else:
                    eng.wait_ge(s("m1_s"), 4 * c)
                    eng.wait_ge(s("m1_oq"), 4 * c)
                for h in range(4):
                    nc.tensor.matmul(bank4(0)[:, h, :], qkv[:, 4 + h, tok], Sm[:, h, :], start=True, stop=True)
                for h in range(4):
                    mm = nc.tensor.matmul(bank4(1)[:, h, :], qkv[:, h, tok], Sm[:, h, :], start=True, stop=True)
                mm.then_inc(s("m1_ks"), 1)
                eng.wait_ge(s("m1_r"), 4 * c + 4)
                for h in range(4):
                    mm = nc.tensor.matmul(bank4(2)[:, h, :], TTm[m][:, h, :], Rm[:, h, :], start=True, stop=True)
                mm.then_inc(s("m1_w"), 1)
                eng.wait_ge(s("m1_wb"), c + 1)
                eng.wait_ge(s("m1_kd"), 2)
                if c < 3:
                    for h in range(4):
                        mm = nc.tensor.matmul(bank4(4)[:, h, :], ktok[:, m, h * P:(h + 1) * P],
                                              Wb[:, c % 2, h * P:(h + 1) * P], start=True, stop=True)
                    mm.then_inc(s("m1_spsum"), 1)
                if c:
                    eng.wait_ge(s("m1_o"), c)
                for h in range(4):
                    mm = nc.tensor.matmul(bank4(3)[:, h, :], ATm[m][:, h, :], Wb[:, c % 2, h * P:(h + 1) * P],
                                          start=True, stop=True)
                mm.then_inc(s("m1_opsum"), 1)
            eng.wait_ge(s("m1_on"), 2)
            for b in range(2):
                for k in range(2):
                    for m in range(2):
                        mm = nc.tensor.transpose(psum[:, b, k * 256 + m * P:k * 256 + m * P + P],
                                                 Om[:, m, (2 * b + k) * P:(2 * b + k) * P + P], const("ident"))
                mm.then_inc(s("m1_oturned"), 1)
            out_tensor(eng, "w_out", s("m1_ylo"), 3)

        rsq = area(2048, TT, D)
        fin = area(4096, D)

        def rms_scalar(eng, stage):
            eng.wait_ge(x_ready, 4 * stage)
            eng.dma_start(fin, rows["final_norm"].partition_broadcast(P)).then_inc(s("fin_loaded"), 16)
            for m in range(TT):
                nc.scalar.activation(rsq[:, m, :], x[:, m, :], ACT.Square, scale=1.0 / 32, accum_out=stat[:, 8 + m:9 + m])\
                    .then_inc(s("fin_squares"), 1)
            eng.wait_ge(S["fin_squares"], 2)
            nc.scalar.activation(stat[:, 10:12], stat[:, 8:10], ACT.Sqrt, bias=stat[:, 63:64]).then_inc(s("fin_root"), 1)

        def rms_vector(eng):
            eng.wait_ge(s("fin_root"), 1)
            nc.vector.reciprocal(stat[:, 12:14], stat[:, 10:12]).then_inc(s("fin_scale"), 1)
            eng.wait_ge(S["fin_scale"], 1)
            eng.wait_ge(s("fin_loaded"), 16)
            for m in range(TT):
                for half in range(2):
                    xs = x[:, m, half * 512:half * 512 + 512]
                    nc.vector.scalar_tensor_tensor(out=xs, in0=xs, scalar=stat[:, 12 + m:13 + m],
                                                   in1=fin[:, half * 512:half * 512 + 512], op0=ALU.mult, op1=ALU.mult)\
                        .then_inc(x_ready, 1)

        fqk = area(0, 8, 256)
        fsq = area(2048, 8, 256)
        frs = area(4096, 8, 256)
        nlfB = area(6144, 2, 8 * P)
        fv = area(8192, 2, 512)
        fog = area(9216, 2, 512)
        U = area(10240, 4, 272)
        WA = area(11328, 4, 272)
        WB = area(12416, 4, 272)
        pooled = area(13504, 4, 256)
        pw = area(14528, 4, P)
        FL = area(15040, 2, 512)
        FP = area(16064, 2, 512)
        FT = area(17088, 2, 512)
        yo = area(18112, 2, 512)
        sf = area(19136, 256)
        fb, f_y, f_abs, f_l, f_n = (sf[:, 16 * k:16 * k + 16] for k in range(5))
        fmax, fneg = sf[:, 80:104], sf[:, 104:128]
        fsum, frec = sf[:, 128:144], sf[:, 144:160]
        fpart = sf[:, 160:176]
        UNITS = [(0, [p, p + 2, p + 4, p + 6]) for p in range(2)] + \
                [(1, [p + 4 * k, p + 4 * k + 2]) for k in range(2) for p in range(2)]
        mh8 = lambda v: v.rearrange("p (m h) -> p m h", m=2)

        def fox_scalar(eng, highs, st):
            n, stage = norm_of[st], STAGES.index(st)
            eng.wait_ge(x_ready, 4 * stage)
            eng.dma_start(pw, rows["pool_w"].rearrange("g c d -> c g d")).then_inc(s("m2_loaded"), 16)
            eng.dma_start(fb[:, 0:8], rows["f_bias"].partition_broadcast(P)).then_inc(s("m2_loaded"), 16)
            norm_scalar(eng, n, CH[("hy_w_in", 0, 8)] - 1, stage)
            steps = Steps(eng, "act_step")
            N = lambda j: ("hy_w_in", 0, j)

            def ready(j):
                highs.upto(CH[N(j)] + 2)
                projected(eng, N(j))

            highs.upto(CH[N(8)] + 2)
            eng.wait_ge(s("m2_y"), 1)
            steps(nc.scalar.activation(f_abs, f_y, ACT.Abs))
            steps(nc.scalar.activation(f_abs, f_abs, ACT.Exp, scale=-1.0))
            nc.scalar.activation(f_l, f_abs, ACT.Ln, bias=stat[:, 62:63]).then_inc(s("m2_l"), 1)
            for k, j in enumerate((0, 1, 2, 3)):
                ready(j)
                b = proj_bank(N(j))
                nc.scalar.activation(fqk[:, 2 * k:2 * k + 2, :], bank2(b), ACT.Copy).then_inc(s("m2_qk"), 1)
                read(nc.scalar.activation(fsq[:, 2 * k:2 * k + 2, :], bank2(b), ACT.Square), N(j))
            for j in (4, 5):
                ready(j)
                read(nc.scalar.activation(fv[:, :, (j - 4) * 256:(j - 4) * 256 + 256], bank2(proj_bank(N(j))), ACT.Copy), N(j))
            for b in range(4):
                eng.wait_ge(s("m2_sums"), b + 1)
                nc.scalar.activation(frs[:, 2 * b:2 * b + 2, :], bank2(b), ACT.Sqrt, scale=1.0 if b < 2 else 1.0 / 64,
                                     bias=stat[:, 60:61] if b < 2 else stat[:, 63:64]).then_inc(s("m2_root"), 1)
            eng.wait_ge(s("m2_pads"), 3)
            for j in (9, 10):
                ready(j)
                read(nc.scalar.activation(U[:, 2 * (j - 9):2 * (j - 9) + 2, 16:272], bank2(proj_bank(N(j))), ACT.Copy), N(j))
            for j in (6, 7):
                ready(j)
                read(nc.scalar.activation(fog[:, :, (j - 6) * 256:(j - 6) * 256 + 256], bank2(proj_bank(N(j))), ACT.Sigmoid),
                     N(j))
            highs.upto(CH[N(7)] + 3)
            for u, (m, heads) in enumerate(UNITS):
                keys = P * (m + 1)
                eng.wait_ge(s("m2_neg"), u + 1)
                if u >= 2:
                    eng.wait_ge(s("m2_pturned"), u - 1)
                for k, h in enumerate(heads):
                    nc.scalar.activation(FP[:, u % 2, k * keys:(k + 1) * keys], FL[:, u % 2, k * keys:(k + 1) * keys], ACT.Exp,
                                         bias=fneg[:, 4 * u + k:4 * u + k + 1], accum_out=fsum[:, 8 * m + h:8 * m + h + 1])\
                        .then_inc(s("m2_p"), 1)
                eng.wait_ge(s("m2_pturned"), u + 1)
                if u >= 2:
                    eng.wait_ge(s("m2_pv"), u - 1)
                nc.scalar.activation(FT[:, u % 2, :], psum[:, 2 + u % 2, :], ACT.Copy).then_inc(s("m2_pt"), 1)
            eng.wait_ge(chunk_used, CH[N(7)] + 1)
            for b in range(2):
                eng.wait_ge(s("m2_pooled"), b + 1)
                for g in (2 * b, 2 * b + 1):
                    nc.scalar.activation(hhi[:, 4 + g, :], bank2(b)[:, g % 2, :], ACT.Copy,
                                         scale=vec[:, VEC_AT["pool_scale"] + g:VEC_AT["pool_scale"] + g + 1])\
                        .then_inc(s("m2_yhi"), 1)
            for b in range(2):
                eng.wait_ge(s("m2_oturned"), b + 1)
                nc.scalar.activation(hhi[:, 2 * b:2 * b + 2, :], bank2(2 + b), ACT.Copy).then_inc(s("m2_yhi"), 1)
            for j in range(4):
                highs.upto(CH[("hy_w_out", 0, j)] + 3)

        def fox_vector(eng, st):
            norm_vector(eng, norm_of[st])
            steps = Steps(eng, "dve_step")
            N = lambda j: ("hy_w_in", 0, j)
            projected(eng, N(8))
            eng.wait_ge(s("m2_loaded"), 32)
            nc.vector.tensor_tensor(mh8(f_y), bank2(proj_bank(N(8)))[:, :, 0:8],
                                    fb[:, 0:8].rearrange("p (a h) -> p a h", a=1).broadcast_to((P, 2, 8)), ALU.add)\
                .then_inc(s("m2_y"), 1)
            eng.wait_ge(S["m2_y"], 1)
            read(nc.vector.tensor_scalar(f_n, f_y, -1.0, 0.0, ALU.mult, ALU.max), N(8))
            for t in (U, WA, WB):
                nc.vector.memset(t[:, :, 0:16], 0.0).then_inc(s("m2_pads"), 1)
            eng.wait_ge(s("m2_l"), 1)
            eng.wait_ge(bank_read[proj_bank(N(8))], PROJ[N(8)] // 2 + 1)
            steps(nc.vector.tensor_tensor(f_n, f_n, f_l, ALU.add))
            for m in range(2):
                nc.vector.tensor_scalar(nlfB[:, m, :].rearrange("p (h a) -> p h a", h=8),
                                        f_n[:, 8 * m:8 * m + 8].rearrange("p (h a) -> p h a", a=1).broadcast_to((P, 8, P)),
                                        1.0, None, ALU.mult).then_inc(s("m2_nlfB"), 1)
            for b in range(4):
                eng.wait_ge(s("m2_root"), b + 1)
                eng.wait_ge(s("m2_qk"), b + 1)
                t = slice(2 * b, 2 * b + 2)
                steps(nc.vector.reciprocal(frs[:, t, :], frs[:, t, :]))
                gain = VEC_AT["q_gain" if b < 2 else "k_gain"]
                nc.vector.scalar_tensor_tensor(out=fqk[:, t, :], in0=fqk[:, t, :], scalar=vec[:, gain:gain + 1],
                                               in1=frs[:, t, :], op0=ALU.mult, op1=ALU.mult).then_inc(s("m2_unit"), 1)
            for j in (9, 10):
                eng.wait_ge(bank_read[proj_bank(N(j))], PROJ[N(j)] // 2 + 1)
            eng.wait_ge(S["m2_pads"], 3)
            src = U
            for g0, dst in enumerate((WA, WB, WA, WB)):
                back = 2 ** g0
                steps(nc.vector.tensor_tensor(dst[:, g0:4, 16:272], src[:, g0:4, 16:272], src[:, g0:4, 16 - back:272 - back],
                                              ALU.add))
                src = dst
            for g, t in enumerate((WA, WB, WA, WB)):
                inv = const("pool", 64)[:, 16 * g:16 * g + 16]
                nc.vector.scalar_tensor_tensor(out=pooled[:, g, 16:256], in0=t[:, g, 32:272], scalar=1.0 / 2 ** (g + 1),
                                               in1=U[:, g, 32:272], op0=ALU.mult, op1=ALU.subtract).then_inc(s("m2_pool"), 1)
                steps(nc.vector.tensor_tensor(t[:, g, 16:32], t[:, g, 16:32], inv, ALU.mult))
                nc.vector.tensor_tensor(pooled[:, g, 0:16], t[:, g, 16:32], U[:, g, 16:32], ALU.subtract)\
                    .then_inc(S["m2_pool"], 1)
            def logits(u):
                m, heads = UNITS[u]
                nh, keys = len(heads), P * (m + 1)
                eng.wait_ge(s("m2_logits"), u + 1)
                if u >= 2:
                    eng.wait_ge(s("m2_p"), sum(len(x_[1]) for x_ in UNITS[:u - 1]))
                L3 = FL[:, u % 2, :].rearrange("p (h k) -> p h k", h=nh)
                mask = const("causal") if m == 0 else const("zero_causal", 256)
                mask = mask.rearrange("p (a k) -> p a k", a=1).broadcast_to((P, nh, keys))
                nc.vector.tensor_tensor(L3, psum[:, u % 2, :].rearrange("p (h k) -> p h k", h=nh), mask, ALU.add)\
                    .then_inc(s("m2_masked"), 1)
                eng.wait_ge(S["m2_masked"], u + 1)
                steps(nc.vector.tensor_reduce(fmax[:, 4 * u:4 * u + nh], L3, AX_X, ALU.max))
                nc.vector.tensor_scalar(fneg[:, 4 * u:4 * u + nh], fmax[:, 4 * u:4 * u + nh], -1.0, None, ALU.mult)\
                    .then_inc(s("m2_neg"), 1)

            for u in range(6):
                logits(u)
            for m in range(2):
                eng.wait_ge(s("m2_pv"), 2 if m == 0 else 6)
                steps(nc.vector.reciprocal(frec[:, 8 * m:8 * m + 8], fsum[:, 8 * m:8 * m + 8]))
                y3 = yo[:, m, :].rearrange("p (h d) -> p h d", h=8)
                steps(nc.vector.tensor_tensor(y3, psum[:, 4 + m, :].rearrange("p (h d) -> p h d", h=8),
                                              frec[:, 8 * m:8 * m + 8].rearrange("p (h a) -> p h a", a=1).broadcast_to((P, 8, 64)),
                                              ALU.mult))
                nc.vector.tensor_tensor(yo[:, m, :], yo[:, m, :], fog[:, m, :], ALU.mult).then_inc(s("m2_yo"), 1)
            for b in range(2):
                eng.wait_ge(s("m2_yhi"), 2 * b + 2)
                for g in (2 * b, 2 * b + 1):
                    nc.vector.scalar_tensor_tensor(out=hlo[:, 4 + g, :], in0=bank2(b)[:, g % 2, :],
                                                   scalar=vec[:, VEC_AT["pool_scale"] + g:VEC_AT["pool_scale"] + g + 1],
                                                   in1=hhi[:, 4 + g, :].bitcast(F32), op0=ALU.mult, op1=ALU.subtract)\
                        .then_inc(s("m2_ylo"), 1)
            for b in range(2):
                eng.wait_ge(s("m2_yhi"), 5 + b)
                nc.vector.tensor_tensor(hlo[:, 2 * b:2 * b + 2, :], bank2(2 + b), hhi[:, 2 * b:2 * b + 2, :].bitcast(F32),
                                        ALU.subtract).then_inc(s("m2_ylo"), 1)
            add_out(eng, "hy_w_out")

        def fox_tensor(eng, st):
            N = lambda j: ("hy_w_in", 0, j)
            norm_tensor(eng, norm_of[st])
            eng.wait_ge(S["h_low"], 8 * norm_of[st] + 8)
            project(eng, N(8), tokens_out, n=8)
            for j in (0, 1, 2, 3):
                project(eng, N(j), columns_out)
            for j in (4, 5):
                project(eng, N(j), tokens_out)
            for b in range(4):
                eng.wait_ge(bank_read[proj_bank(N(b))], PROJ[N(b)] // 2 + 1)
                nc.tensor.matmul(psum[:, b, :], const("same64"), fsq[:, 2 * b:2 * b + 2, :], start=True, stop=True)\
                    .then_inc(s("m2_sums"), 1)
            for j in (9, 10):
                project(eng, N(j), columns_out)
            for j in (6, 7):
                project(eng, N(j), tokens_out)
            eng.wait_ge(s("m2_unit"), 4)
            eng.wait_ge(s("m2_nlfB"), 2)

            def logits(u):
                m, heads = UNITS[u]
                keys = P * (m + 1)
                if u >= 2:
                    eng.wait_ge(s("m2_masked"), u - 1)
                for k, h in enumerate(heads):
                    o = psum[:, u % 2, k * keys:(k + 1) * keys]
                    r, t = slice((h % 2) * 64, (h % 2) * 64 + 64), h // 2
                    nc.tensor.matmul(o, fqk[r, t, m * P:(m + 1) * P], fqk[r, 4 + t, 0:keys], start=True, stop=False)
                    mm = nc.tensor.matmul(o, nlfB[:, 0, h * P:(h + 1) * P], const("upto_all", keys), start=False, stop=m == 0)
                    if m == 1:
                        mm = nc.tensor.matmul(o[:, P:2 * P], nlfB[:, 1, h * P:(h + 1) * P], const("upto_all"), start=False,
                                              stop=True)
                mm.then_inc(s("m2_logits"), 1)

            def values(u):
                m, heads = UNITS[u]
                eng.wait_ge(s("m2_pt"), u + 1)
                for k, h in enumerate(heads):
                    for t in range(m + 1):
                        mm = nc.tensor.matmul(psum[:, 4 + m, h * 64:h * 64 + 64],
                                              FT[:, u % 2, (k * (m + 1) + t) * P:(k * (m + 1) + t + 1) * P],
                                              fv[:, t, h * 64:h * 64 + 64], start=t == 0, stop=t == m)
                mm.then_inc(s("m2_pv"), 1)

            logits(0)
            for u, (m, heads) in enumerate(UNITS):
                if u < 5:
                    logits(u + 1)
                eng.wait_ge(s("m2_p"), sum(len(x_[1]) for x_ in UNITS[:u + 1]))
                if u >= 2:
                    eng.wait_ge(s("m2_pt"), u - 1)
                for k in range(4):
                    mm = nc.tensor.transpose(bank4(2 + u % 2)[:, k, :], FP[:, u % 2, k * P:(k + 1) * P], const("ident"))
                mm.then_inc(s("m2_pturned"), 1)
                if u:
                    values(u - 1)
            values(5)
            eng.wait_ge(s("m2_pool"), 8)
            eng.wait_ge(s("m2_masked"), 6)
            eng.wait_ge(s("m2_loaded"), 32)
            for b in range(2):
                for g in (2 * b, 2 * b + 1):
                    mm = nc.tensor.matmul(bank2(b)[:, g % 2, :], pw[:, g, :], pooled[:, g, :], start=True, stop=True)
                mm.then_inc(s("m2_pooled"), 1)
            eng.wait_ge(s("m2_yo"), 2)
            eng.wait_ge(s("m2_pt"), 6)
            for b in range(2):
                for k in range(2):
                    for m in range(2):
                        mm = nc.tensor.transpose(psum[:, 2 + b, k * 256 + m * P:k * 256 + m * P + P],
                                                 yo[:, m, (2 * b + k) * P:(2 * b + k) * P + P], const("ident"))
                mm.then_inc(s("m2_oturned"), 1)
            out_tensor(eng, "hy_w_out", s("m2_ylo"), 6)

        DECAY = float(np.exp(-0.5))
        ar = area(0, 2, 8 * 256).rearrange("p s (k t) -> p s k t", k=8)
        kk = ar[:, 0, :, :]
        rr = ar[:, 1, :, :]
        kx = area(4096, 8, 256)
        sw = area(6144, 8, 256)
        aa = area(8192, 8, 256)
        vt = area(10240, 2, D)
        s8 = area(12288, 8, 256)
        s9 = area(14336, 8, 256)
        ht = area(16384, 8, 257)
        bkT = area(6144, 2, 8 * P).rearrange("p s (k t) -> p s k t", k=8)
        bk = area(14336, 2, D)
        T7 = [area(12288 + 512 * g, 4, P) for g in range(2)]
        TT7 = [area(13312 + 512 * g, 4, P) for g in range(2)]
        AB = [area(16384 + 1024 * g, 4, 256).rearrange("p a (s n) -> p a s n", s=2) for g in range(2)]
        AK = [area(18432 + 1024 * g, 4, 256).rearrange("p a (s n) -> p a s n", s=2) for g in range(2)]
        NT7 = [area(20480 + 512 * g, 4, P) for g in range(2)]
        R7 = area(20480, 4, P)
        U7 = area(20992, 4, P)
        Z = area(21504, 8, P)
        s3m = area(22528, 512)
        pc = s3m[:, 0:32].rearrange("p (k c) -> p k c", k=8)
        bonus = s3m[:, 32:64]
        gsum, gmean, gvar, groot, gscale = (s3m[:, 64 + 32 * k:96 + 32 * k] for k in range(5))
        Y = x
        yt = area(0, 8, 256)
        wa_hi, wa_lo = ahi[:, 0, 0, :], alo[:, 0, 0, :]
        gm_hi, gm_lo = ahi[:, 1, 0, :], alo[:, 1, 0, :]
        gt_hi, gt_lo = ahi[:, 1, 1, :], alo[:, 1, 1, :]
        lw = area(12288 + 8192, 3, 256)
        V_AT = lambda name, k: vec[:, VEC_AT[name] + k:VEC_AT[name] + k + 1]
        VARIANTS = (1, 4, 5, 0, 2, 3)
        RW = lambda j: ("rw", 0, j)
        L0, L1, L2 = (CH.get(("lora", 0, j)) for j in range(3))
        PASSES = [(m, q) for m in range(2) for q in range(2)]

        def z_steps(w, hh):
            return 5 * sum(1 for v_ in range(2 * w + hh) if 2 * PASSES[v_ // 2][0] + v_ % 2 < 3)

        def variant_used(eng, v):
            if v in (1, 2):
                eng.wait_ge(s("rw_first"), v)
            if v == 3:
                eng.wait_ge(s("rw_first"), 4)
            if v == 4:
                eng.wait_ge(chunk_used, CH[RW(3)] + 1)
            if v == 5:
                eng.wait_ge(chunk_used, CH[RW(7)] + 1)

        def rwkv_scalar(eng, highs, st):
            n, stage = norm_of[st], STAGES.index(st)
            eng.wait_ge(x_ready, 4 * stage)
            eng.wait_ge(S["rms_scale"], 2 * n)
            for m in range(TT):
                nc.scalar.activation(junk[:, m, :], x[:, m, :], ACT.Square, scale=1.0 / 32, accum_out=stat[:, m:m + 1])\
                    .then_inc(S["rms_squares"], 1)
            eng.wait_ge(S["rms_squares"], 2 * (n + 1))
            nc.scalar.activation(stat[:, 2:4], stat[:, 0:2], ACT.Sqrt, bias=stat[:, 63:64]).then_inc(S["rms_root"], 1)
            eng.wait_ge(S["rows_scaled"], 2 * n + 2)
            eng.dma_start(kept_x, x[:, :, :].rearrange("p m d -> p (m d)")).then_inc(s("x_kept"), 16)
            for b in range(4):
                eng.wait_ge(S["turned"], 4 * n + b + 1)
                for k in (2 * b, 2 * b + 1):
                    nc.scalar.activation(ht[:, k, 1:257], psum[:, b, (k % 2) * 256:(k % 2) * 256 + 256], ACT.Copy,
                                         scale=V_AT(NORMS[n], k)).then_inc(S["h_high"], 1)
            highs.upto(L0 + 2)

            def high_variant(v):
                variant_used(eng, v)
                for b in range(4):
                    eng.wait_ge(s("rw_mixed"), 8 * v + 2 * b + 2)
                    nc.scalar.activation(hhi[:, 2 * b:2 * b + 2, :], s9[:, 2 * b:2 * b + 2, :], ACT.Copy)\
                        .then_inc(s("rw_xhi"), 1)

            eng.wait_ge(chunk_used, L0)
            for v in range(3):
                high_variant(v)
            eng.wait_ge(s("rw_first"), 2)
            nc.scalar.activation(lw[0:64, 0, :], psum[0:64, 0, 0:256], ACT.Tanh).then_inc(s("rw_lw"), 1)
            nc.scalar.activation(lw[64:128, 0, :], psum[64:128, 0, 256:512], ACT.Copy).then_inc(s("rw_lw"), 1)
            eng.wait_ge(s("rw_lw"), 2)
            nc.scalar.activation(wa_hi, lw[:, 0, :], ACT.Copy).then_inc(s("rw_lwhi"), 1)
            eng.wait_ge(s("rw_first"), 4)
            nc.scalar.activation(lw[:, 1, :], psum[:, 1, 0:256], ACT.Sigmoid).then_inc(S["rw_lw"], 1)
            nc.scalar.activation(lw[0:32, 2, :], psum[0:32, 1, 256:512], ACT.Sigmoid).then_inc(S["rw_lw"], 1)
            eng.wait_ge(S["rw_lw"], 4)
            nc.scalar.activation(gm_hi, lw[:, 1, :], ACT.Copy).then_inc(S["rw_lwhi"], 1)
            nc.scalar.activation(gt_hi[0:32], lw[0:32, 2, :], ACT.Copy).then_inc(S["rw_lwhi"], 1)
            for k in range(8):
                if k % 2 == 0:
                    eng.wait_ge(s("rw_second"), k // 2 + 1)
                b = (k // 2) % 2
                nc.scalar.activation(sw[:, k, :], bank2(2 + b)[:, k % 2, :], ACT.Sigmoid, bias=V_AT("w0", k)).then_inc(s("rw_sig"), 1)
                nc.scalar.activation(aa[:, k, :], bank2(4 + b)[:, k % 2, :], ACT.Sigmoid, bias=V_AT("a0", k)).then_inc(s("rw_sig"), 1)
            for v, dst in ((3, rr), (4, kx), (5, vt)):
                high_variant(v)
                for j in range(4):
                    name = RW(4 * (v - 3) + j)
                    highs.upto(CH[name] + 2)
                    projected(eng, name)
                    o = vt[:, :, j * 256:(j + 1) * 256] if v == 5 else dst[:, 2 * j:2 * j + 2, :]
                    read(nc.scalar.activation(o, bank2(proj_bank(name)), ACT.Copy), name)
            eng.wait_ge(s("rw_kk"), 8)
            nc.scalar.activation(s8, kk, ACT.Square).then_inc(s("rw_sq"), 1)
            highs.upto(CH[RW(11)] + 3)
            eng.wait_ge(s("rw_xlo"), 24)
            for b in range(4):
                eng.wait_ge(s("rw_sums"), b + 1)
                nc.scalar.activation(s9[:, 2 * b:2 * b + 2, :], bank2(b), ACT.Sqrt).then_inc(s("rw_root"), 1)
            eng.wait_ge(s("rw_before"), 1)
            nc.scalar.activation(sw, sw, ACT.Exp, scale=-DECAY).then_inc(s("rw_pm"), 1)
            eng.wait_ge(s("rw_bonus"), 1)
            nc.scalar.activation(s8, s9, ACT.Exp, scale=DECAY).then_inc(s("rw_pinv"), 1)
            eng.wait_ge(s("rw_pinv"), 1)
            nc.scalar.activation(s9, s9, ACT.Exp, scale=-DECAY).then_inc(s("rw_p"), 1)
            eng.wait_ge(s("x_kept"), 16)
            for w, (m, q) in enumerate(PASSES):
                if q == 0:
                    for b in range(4):
                        eng.wait_ge(s("rw_bkturned"), 4 * m + b + 1)
                        nc.scalar.activation(bk[:, b // 2, (b % 2) * 512:(b % 2) * 512 + 512], psum[:, 2 + b, :], ACT.Copy)\
                            .then_inc(s("rw_bk"), 1)
                inverse_scalar(eng, w + inv0["rwkv"], T7, NT7)
                for hh in range(2):
                    c = 2 * w + hh
                    eng.wait_ge(s("rw_usum"), c + 1)
                    nc.scalar.activation(R7, bank4(0), ACT.Copy).then_inc(s("rw_r"), 1)
                    eng.wait_ge(s("rw_u"), c + 1)
                    r = slice(hh * 64, hh * 64 + 64)
                    nc.scalar.activation(U7[r], bank4(1)[r], ACT.Copy).then_inc(s("rw_ub"), 1)
                    eng.wait_ge(s("rw_ysum"), c + 1)
                    nc.scalar.activation(Y[r, m, q * 512:(q + 1) * 512], psum[r, 2, :], ACT.Copy).then_inc(s("rw_y"), 1)
            for m in range(2):
                eng.wait_ge(s("rw_centred"), m + 1)
                nc.scalar.activation(area(12288, 2, D)[:, m, :], Y[:, m, :], ACT.Square).then_inc(s("rw_ysq"), 1)
            eng.wait_ge(s("rw_gvar"), 2)
            nc.scalar.activation(groot, gvar, ACT.Sqrt, scale=1.0 / 64, bias=stat[:, 59:60]).then_inc(s("rw_groot"), 1)
            for b in range(4):
                eng.wait_ge(s("rw_out"), b + 1)
                for k in (2 * b, 2 * b + 1):
                    nc.scalar.activation(yt[:, k, :], bank2(b % 2)[:, k % 2, :], ACT.Identity, scale=V_AT("ln_w", k),
                                         bias=V_AT("ln_b", k)).then_inc(s("rw_yt"), 1)
                if b == 3:
                    eng.wait_ge(s("rw_out"), 4)
                    eng.dma_start(x[:, :, :].rearrange("p m d -> p (m d)"), kept_x).then_inc(s("x_back"), 16)
                eng.wait_ge(s("rw_gated"), b + 1)
                nc.scalar.activation(hhi[:, 2 * b:2 * b + 2, :], yt[:, 2 * b:2 * b + 2, :], ACT.Copy).then_inc(s("rw_yhi"), 1)
            for j in range(4):
                highs.upto(CH[("rw_o", 0, j)] + 3)

        def rwkv_vector(eng, st):
            n = norm_of[st]
            steps = Steps(eng, "dve_step")
            eng.wait_ge(S["rms_root"], n + 1)
            nc.vector.reciprocal(stat[:, 4:6], stat[:, 2:4]).then_inc(S["rms_scale"], 1)
            eng.wait_ge(S["rms_scale"], 2 * n + 1)
            for m in range(TT):
                nc.vector.tensor_scalar(xn[:, m, :], x[:, m, :], stat[:, 4 + m:5 + m], None, ALU.mult)\
                    .then_inc(S["rows_scaled"], 1)
            steps(nc.vector.memset(ht[:, :, 0:1], 0.0))
            steps(nc.vector.memset(Z, 0.0))
            for b in range(4):
                eng.wait_ge(S["h_high"], 8 * n + 2 * b + 2)
                for k in (2 * b, 2 * b + 1):
                    nc.vector.tensor_tensor(s8[:, k, :], ht[:, k, 0:256], ht[:, k, 1:257], ALU.subtract)\
                        .then_inc(S["h_low"], 1)
            eng.wait_ge(S["h_low"], 8 * n + 8)
            nc.vector.tensor_copy(stat[:, 6:7], stat[:, 5:6]).then_inc(S["rms_scale"], 1)
            eng.wait_ge(S["rms_scale"], 2 * n + 2)

            def variant(v):
                if v:
                    eng.wait_ge(s("rw_xlo"), 4 * v)
                for k in range(8):
                    mu = VEC_AT["mu"] + 8 * VARIANTS[v] + k
                    nc.vector.scalar_tensor_tensor(out=s9[:, k, :], in0=s8[:, k, :], scalar=vec[:, mu:mu + 1],
                                                   in1=ht[:, k, 1:257], op0=ALU.mult, op1=ALU.add).then_inc(s("rw_mixed"), 1)
                for b in range(4):
                    eng.wait_ge(s("rw_xhi"), 4 * v + b + 1)
                    k = slice(2 * b, 2 * b + 2)
                    nc.vector.tensor_tensor(hlo[:, k, :], s9[:, k, :], hhi[:, k, :].bitcast(F32), ALU.subtract)\
                        .then_inc(s("rw_xlo"), 1)

            for v in range(3):
                variant(v)
            eng.wait_ge(s("rw_lwhi"), 1)
            nc.vector.tensor_tensor(wa_lo, lw[:, 0, :], wa_hi.bitcast(F32), ALU.subtract).then_inc(s("rw_lwlo"), 1)
            eng.wait_ge(S["rw_lwhi"], 3)
            nc.vector.tensor_tensor(gm_lo, lw[:, 1, :], gm_hi.bitcast(F32), ALU.subtract).then_inc(S["rw_lwlo"], 1)
            nc.vector.tensor_tensor(gt_lo[0:32], lw[0:32, 2, :], gt_hi[0:32].bitcast(F32), ALU.subtract).then_inc(S["rw_lwlo"], 1)
            for v in range(3, 6):
                variant(v)
            for j in range(4, 8):
                eng.wait_ge(bank_read[proj_bank(RW(j))], PROJ[RW(j)] // 2 + 1)
            for k in range(8):
                nc.vector.tensor_scalar(kk[:, k, :], kx[:, k, :], V_AT("k_k", k), None, ALU.mult).then_inc(s("rw_kk"), 1)
            for b in range(4):
                eng.wait_ge(s("rw_root"), b + 1)
                k = slice(2 * b, 2 * b + 2)
                steps(nc.vector.tensor_scalar(s9[:, k, :], s9[:, k, :], 1e-12, None, ALU.max))
                steps(nc.vector.reciprocal(s9[:, k, :], s9[:, k, :]))
                steps(nc.vector.tensor_tensor(kk[:, k, :], kk[:, k, :], s9[:, k, :], ALU.mult))
            eng.wait_ge(s("rw_sums"), 4)
            eng.wait_ge(s("rw_sig"), 16)
            for k in range(8):
                ins = nc.vector.tensor_scalar(s8[:, k, :], aa[:, k, :], 1.0, V_AT("k_a", k), ALU.subtract, ALU.mult)
                steps(ins)
            steps(nc.vector.scalar_tensor_tensor(out=kx, in0=s8, scalar=1.0, in1=kx, op0=ALU.add, op1=ALU.mult))
            for j in range(0, 4):
                eng.wait_ge(bank_read[proj_bank(RW(j))], PROJ[RW(j)] // 2 + 1)
            for k in range(8):
                nc.vector.scalar_tensor_tensor(out=s8[:, k, :], in0=rr[:, k, :], scalar=V_AT("r_k", k), in1=kx[:, k, :],
                                               op0=ALU.mult, op1=ALU.mult).then_inc(s("rw_rk"), 1)
            for k in range(8):
                steps(nc.vector.tensor_tensor_scan(s9[:, k, :], const("restart", TOK), sw[:, k, :], 0.0, ALU.mult, ALU.add))
            nc.vector.tensor_tensor(sw, s9, sw, ALU.subtract).then_inc(s("rw_before"), 1)
            eng.wait_ge(s("rw_bonus_sum"), 1)
            nc.vector.tensor_copy(bonus, psum[:, 4, 0:32]).then_inc(s("rw_bonus"), 1)
            steps(nc.vector.tensor_tensor(aa, aa, kk, ALU.mult))
            eng.wait_ge(s("rw_pm"), 1)
            steps(nc.vector.scalar_tensor_tensor(out=kk, in0=kk, scalar=-1.0, in1=sw, op0=ALU.mult, op1=ALU.mult))
            eng.wait_ge(s("rw_pinv"), 1)
            steps(nc.vector.tensor_tensor(aa, aa, s8, ALU.mult))
            steps(nc.vector.tensor_tensor(kx, kx, s8, ALU.mult))
            eng.wait_ge(s("rw_p"), 1)
            nc.vector.tensor_tensor(rr, rr, s9, ALU.mult).then_inc(s("rw_ready"), 1)
            steps(nc.vector.tensor_copy(pc, s9.rearrange("p k (c t) -> p k c t", c=4)[:, :, :, 63]))
            eng.wait_ge(S["rw_ready"], 1)

            def to_tokens(m):
                if m:
                    eng.wait_ge(s("rw_bkturned"), 4 * m)
                pcb = pc[:, :, 2 * m:2 * m + 2].rearrange("p k (c a) -> p k c a", a=1).broadcast_to((P, 8, 2, 64))
                for i_, src in enumerate((aa, kx)):
                    nc.vector.tensor_tensor(bkT[:, i_, :, :].rearrange("p k (c t) -> p k c t", c=2),
                                            src[:, :, m * P:(m + 1) * P].rearrange("p k (c t) -> p k c t", c=2), pcb, ALU.mult)\
                        .then_inc(s("rw_bkT"), 1)

            both = const("before", 256).rearrange("p (a n) -> p a n", a=1).broadcast_to((P, 2, 256))
            for w, (m, q) in enumerate(PASSES):
                if q == 0:
                    to_tokens(m)
                for g in range(2):
                    for i_, dst in enumerate((AB[g], AK[g])):
                        for half in range(2):
                            eng.wait_ge(s("rw_scores"), 8 * w + 4 * g + 2 * i_ + half + 1)
                            nc.vector.tensor_tensor(dst[:, 2 * half:2 * half + 2, :, :].rearrange("p a s n -> p a (s n)"),
                                                    bank2(4 * g + 2 * i_ + half), both, ALU.mult).then_inc(s("rw_masked"), 1)
                eng.wait_ge(S["rw_masked"], 8 * w + 8)
                inverse_vector(eng, w + inv0["rwkv"], steps, [AB[g][:, :, 0, :] for g in range(2)], T7, TT7, NT7,
                               four(const("ident")), ALU.add, True)
                for hh in range(2):
                    c, z0 = 2 * m + hh, z_steps(w, hh)
                    if c < 3:
                        eng.wait_ge(s("rw_zsum"), z0 // 5 + 1)
                        if hh == 1:
                            eng.wait_ge(s("rw_z"), z0)
                        Zt = T7[0]
                        nc.vector.tensor_tensor(Zt, bank4(3), four(const("same64")), ALU.mult).then_inc(s("rw_z"), 1)
                        eng.wait_ge(s("rw_z"), z0 + 1)
                        eng.wait_ge(s("rw_ysum"), 2 * w + hh + 1)
                        for k in range(4):
                            t = 4 * q + k
                            nc.vector.scalar_tensor_tensor(out=Z[:, t, :], in0=Z[:, t, :], scalar=pc[:, t, c:c + 1],
                                                           in1=Zt[:, k, :], op0=ALU.mult, op1=ALU.add).then_inc(s("rw_z"), 1)
            over64 = lambda v: v.rearrange("p (h a) -> p h a", a=1).broadcast_to((P, 16, 64))
            eng.wait_ge(s("rw_y"), 8)
            for m in range(2):
                y3 = Y[:, m, :].rearrange("p (h d) -> p h d", h=16)
                hs = slice(16 * m, 16 * m + 16)
                steps(nc.vector.tensor_reduce(gsum[:, hs], y3, AX_X, ALU.add))
                steps(nc.vector.tensor_scalar(gmean[:, hs], gsum[:, hs], 1.0 / 64, None, ALU.mult))
                nc.vector.tensor_tensor(y3, y3, over64(gmean[:, hs]), ALU.subtract).then_inc(s("rw_centred"), 1)
            for m in range(2):
                v3 = vt[:, m, :].rearrange("p (h d) -> p h d", h=16)
                nc.vector.tensor_tensor(v3, v3, over64(bonus[:, 16 * m:16 * m + 16]), ALU.mult).then_inc(s("rw_bv"), 1)
            for m in range(2):
                eng.wait_ge(s("rw_ysq"), m + 1)
                nc.vector.tensor_reduce(gvar[:, 16 * m:16 * m + 16],
                                        area(12288, 2, D)[:, m, :].rearrange("p (h d) -> p h d", h=16), AX_X, ALU.add)\
                    .then_inc(s("rw_gvar"), 1)
            eng.wait_ge(s("rw_groot"), 1)
            steps(nc.vector.reciprocal(gscale, groot))
            for m in range(2):
                y3 = Y[:, m, :].rearrange("p (h d) -> p h d", h=16)
                nc.vector.tensor_tensor(y3, y3, over64(gscale[:, 16 * m:16 * m + 16]), ALU.mult).then_inc(s("rw_yn"), 1)
            for b in range(4):
                k = slice(2 * b, 2 * b + 2)
                eng.wait_ge(s("rw_yt"), 2 * b + 2)
                steps(nc.vector.tensor_tensor(yt[:, k, :], yt[:, k, :], bank2(2 + b % 2), ALU.add))
                nc.vector.tensor_tensor(yt[:, k, :], yt[:, k, :], bank2(4 + b % 2), ALU.mult).then_inc(s("rw_gated"), 1)
            for b in range(4):
                k = slice(2 * b, 2 * b + 2)
                eng.wait_ge(s("rw_yhi"), b + 1)
                nc.vector.tensor_tensor(hlo[:, k, :], yt[:, k, :], hhi[:, k, :].bitcast(F32), ALU.subtract)\
                    .then_inc(s("rw_ylo"), 1)
            eng.wait_ge(s("x_back"), 16)
            add_out(eng, "rw_o")

        def rwkv_tensor(eng, st):
            n = norm_of[st]
            norm_tensor(eng, n)
            eng.wait_ge(low_made, L0 + 1)

            def first(v, bank, half, slot, at, width, stride):
                rows_ = width
                for k in range(KT):
                    if k % 2 == 0:
                        eng.wait_ge(s("rw_xlo"), 4 * v + k // 2 + 1)
                    w = (slice(None), slot, slice(at + k * stride, at + k * stride + width))
                    mm = three_passes(psum[0:rows_, bank, half * 256:half * 256 + 256], whi[w], wlo[w], hhi[:, k, :],
                                      hlo[:, k, :], True, k == 0, k == KT - 1)
                return mm

            first(0, 0, 0, L0 % SPLIT, 0, P, 256).then_inc(s("rw_first"), 1)
            first(1, 0, 1, L0 % SPLIT, 0, P, 256).then_inc(s("rw_first"), 1)
            first(2, 1, 0, L0 % SPLIT, P, P, 256).then_inc(s("rw_first"), 1)
            eng.wait_ge(S["rw_first"], 3)
            nc.tensor.matmul(psum[0:1, 7, 0:2], const("ident")[:, 0:1], const("ident")[:, 0:2], start=True, stop=True)\
                .then_inc(chunk_used, 1)
            eng.wait_ge(low_made, L1 + 1)
            first(2, 1, 1, L1 % SPLIT, D, 32, 32).then_inc(s("rw_first"), 1)
            eng.wait_ge(s("rw_lwlo"), 1)
            for b in range(4):
                if b >= 2:
                    eng.wait_ge(s("rw_sig"), 4 * (b - 1))
                for base, lo_, hi_ in ((2, 0, 64), (4, 64, 128)):
                    for k in (2 * b, 2 * b + 1):
                        w = (slice(lo_, hi_), L1 % SPLIT, slice(k * P, k * P + P))
                        mm = three_passes(bank2(base + b % 2)[:, k % 2, :], whi[w], wlo[w], wa_hi[lo_:hi_], wa_lo[lo_:hi_],
                                          True, True, True)
                mm.then_inc(s("rw_second"), 1)
            nc.tensor.matmul(psum[0:1, 7, 0:2], const("ident")[:, 0:1], const("ident")[:, 0:2], start=True, stop=True)\
                .then_inc(chunk_used, 1)
            for v in range(3, 6):
                eng.wait_ge(s("rw_xlo"), 4 * v + 4)
                for j in range(4):
                    project(eng, RW(4 * (v - 3) + j), tokens_out if v == 5 else columns_out)
            eng.wait_ge(s("rw_sq"), 1)
            eng.wait_ge(s("rw_sig"), 16)
            for b in range(4):
                nc.tensor.matmul(psum[:, b, :], const("same64"), s8[:, 2 * b:2 * b + 2, :], start=True, stop=True)\
                    .then_inc(s("rw_sums"), 1)
            eng.wait_ge(s("rw_rk"), 8)
            for m in range(2):
                for k in range(8):
                    mm = nc.tensor.matmul(psum[:, 4, 16 * m + 2 * k:16 * m + 2 * k + 2], s8[:, k, m * P:(m + 1) * P],
                                          const("same64")[:, 0:P:64], start=True, stop=True)
            mm.then_inc(s("rw_bonus_sum"), 1)
            eng.wait_ge(s("rw_root"), 4)
            eng.wait_ge(s("rw_bonus"), 1)
            eng.wait_ge(s("rw_ready"), 1)
            for w, (m, q) in enumerate(PASSES):
                if q == 0:
                    eng.wait_ge(s("rw_bkT"), 2 * m + 2)
                    if w:
                        eng.wait_ge(s("rw_y"), 2 * w)
                        eng.wait_ge(s("rw_z"), z_steps(w, 0))
                    for b in range(4):
                        for k in range(4):
                            mm = nc.tensor.transpose(bank4(2 + b)[:, k, :], bkT[:, b // 2, 4 * (b % 2) + k, :], const("ident"))
                        mm.then_inc(s("rw_bkturned"), 1)
                if w:
                    eng.wait_ge(s("rw_y"), 2 * w)
                    eng.wait_ge(s("rw_z"), z_steps(w, 0))
                tok = slice(m * P, (m + 1) * P)
                for g in range(2):
                    r = slice(64 * g, 64 * g + 64)
                    for i_, src in enumerate((aa, kx)):
                        for half in range(2):
                            b = 4 * g + 2 * i_ + half
                            if b >= 2 and b <= 5:
                                eng.wait_ge(s("rw_bk"), 4 * m + b - 1)
                            for k in range(2):
                                t = 4 * q + 2 * half + k
                                mm = nc.tensor.matmul(bank2(b)[:, k, :], src[r, t, tok], ar[r, :, t, tok],
                                                      start=True, stop=True)
                            mm.then_inc(s("rw_scores"), 1)
                eng.wait_ge(s("rw_masked"), 8 * w + 8)
                inverse_tensor(eng, w + inv0["rwkv"], T7, TT7, NT7, NT7)
                for hh in range(2):
                    c, r = 2 * w + hh, slice(hh * 64, hh * 64 + 64)
                    if hh == 0:
                        eng.wait_ge(INV["inv_updated"], 10 * (w + inv0["rwkv"]) + 10)
                    else:
                        eng.wait_ge(s("rw_z"), z_steps(w, 1))
                    for k in range(4):
                        nc.tensor.matmul(bank4(0)[:, k, :], kk[:, 4 * q + k, tok], Z[:, 4 * q + k, :], start=True, stop=False)
                        for p in range(2):
                            col = (4 * q + k) * P + p * 64
                            mm = nc.tensor.matmul(bank4(0)[:, k, p * 64:p * 64 + 64], AK[p][:, k, 0, :], vt[:, m, col:col + 64],
                                                  start=False, stop=p == 1)
                    mm.then_inc(s("rw_usum"), 1)
                    eng.wait_ge(s("rw_r"), c + 1)
                    for k in range(4):
                        for p in range(2):
                            mm = nc.tensor.matmul(bank4(1)[:, k, p * 64:p * 64 + 64], TT7[p][:, k, :],
                                                  R7[:, k, p * 64:p * 64 + 64], start=True, stop=True)
                    mm.then_inc(s("rw_u"), 1)
                    eng.wait_ge(s("rw_ub"), c + 1)
                    if 2 * m + hh < 3:
                        for k in range(4):
                            t = 4 * q + k
                            nc.tensor.matmul(bank4(3)[:, k, :], bk[r, 0, t * P:(t + 1) * P], U7[r, k, :], start=True, stop=False)
                            mm = nc.tensor.matmul(bank4(3)[:, k, :], bk[r, 1, t * P:(t + 1) * P], vt[r, m, t * P:(t + 1) * P],
                                                  start=False, stop=True)
                        mm.then_inc(s("rw_zsum"), 1)
                    if hh:
                        eng.wait_ge(s("rw_y"), c)
                    for k in range(4):
                        nc.tensor.matmul(bank4(2)[:, k, :], rr[:, 4 * q + k, tok], Z[:, 4 * q + k, :], start=True, stop=False)
                        for p in range(2):
                            col = (4 * q + k) * P + p * 64
                            o = bank4(2)[:, k, p * 64:p * 64 + 64]
                            nc.tensor.matmul(o, AK[p][:, k, 1, :], vt[:, m, col:col + 64], start=False, stop=False)
                            mm = nc.tensor.matmul(o, AB[p][r, k, 1, :], U7[r, k, p * 64:p * 64 + 64], start=False, stop=p == 1)
                    mm.then_inc(s("rw_ysum"), 1)
            eng.wait_ge(s("rw_yn"), 2)
            eng.wait_ge(s("rw_bv"), 2)
            eng.wait_ge(s("rw_y"), 8)
            eng.wait_ge(low_made, L2 + 1)
            eng.wait_ge(s("rw_lwlo"), 3)
            for b in range(4):
                if b >= 2:
                    eng.wait_ge(s("rw_gated"), b - 1)
                for base, src in ((0, Y), (2, vt)):
                    for k in range(2):
                        for m in range(2):
                            nc.tensor.transpose(psum[:, base + b % 2, k * 256 + m * P:k * 256 + m * P + P],
                                                src[:, m, (2 * b + k) * P:(2 * b + k + 1) * P], const("ident"))
                for k in range(2):
                    o = bank2(4 + b % 2)[:, k, :]
                    at = (2 * b + k) * P
                    w = (slice(None), L2 % SPLIT, slice(at, at + P))
                    three_passes(o, whi[w], wlo[w], gm_hi, gm_lo, True, True, False)
                    w = (slice(0, 32), L2 % SPLIT, slice(D + at, D + at + P))
                    mm = three_passes(o, whi[w], wlo[w], gt_hi[0:32], gt_lo[0:32], True, False, True)
                mm.then_inc(s("rw_out"), 1)
            nc.tensor.matmul(psum[0:1, 6, 0:2], const("ident")[:, 0:1], const("ident")[:, 0:2], start=True, stop=True)\
                .then_inc(chunk_used, 1)
            out_tensor(eng, "rw_o", s("rw_ylo"), 4)

        block = ctx.enter_context(nc.Block())

        @block.sync
        def _(sp):
            sp.dma_start(x[:, :, :], x_in.rearrange("(m p) d -> p m d", p=P)).then_inc(S["x_loaded"], 16)
            sp.dma_start(con[:, :], consts).then_inc(S["const_loaded"], 16)
            sp.dma_start(vec[:, :], vectors).then_inc(S["const_loaded"], 16)
            for c in range(RAW):
                sp.dma_start(raw[:, c, :], stream[c]).then_inc(raw_loaded[c], 16)
            with sp.Fori(1, NCH // RAW) as i:
                for r in range(RAW):
                    sp.wait_ge(low_made, 3 * i + (r - 2))
                    sp.dma_start(raw[:, r, :], stream[bass.ds(3 * i + r, 1), :, :].rearrange("a p n -> p (a n)"))\
                        .then_inc(raw_loaded[r], 16)
            for c in range(NCH // RAW * RAW, NCH):
                sp.wait_ge(low_made, c - 2)
                sp.dma_start(raw[:, c % RAW, :], stream[c]).then_inc(raw_loaded[c % RAW], 16)
            sp.wait_ge(x_ready, 4 * len(STAGES))
            sp.dma_start(out.rearrange("(m p) d -> p m d", p=P), x[:, :, :]).then_inc(S["stored"], 16)
            sp.wait_ge(S["stored"], 16)

        @block.gpsimd
        def _(pool):
            def low(c, i=None):
                slot = c % SPLIT
                pool.wait_ge(high_made, c + 1 if i is None else c + 1 + 3 * i)
                nc.gpsimd.tensor_tensor(wlo[:, slot, :], raw[:, c % RAW, :], whi[:, slot, :].bitcast(F32), ALU.subtract)\
                    .then_inc(low_made, 1)
            with pool.Fori(0, NCH // 3) as i:
                for r in range(3):
                    low(r, i)
            for c in range(NCH // 3 * 3, NCH):
                low(c)

        @block.scalar
        def _(act_eng):
            highs = Highs(act_eng)
            highs.upto(2)
            act_eng.wait_ge(S["const_loaded"], 32)
            act_eng.wait_ge(S["eps_ready"], 5)
            for k, st in enumerate(STAGES):
                if st[0] == "ffn":
                    norm_scalar(act_eng, norm_of[st], firsts[k] - 1 if k else None, k)
                    ffn_scalar(act_eng, st[1], highs)
                if st[0] == "mix1":
                    mix1_scalar(act_eng, highs, st)
                if st[0] == "rms":
                    rms_scalar(act_eng, k)
                if st[0] == "fox":
                    fox_scalar(act_eng, highs, st)
                if st[0] == "rwkv":
                    rwkv_scalar(act_eng, highs, st)

        @block.vector
        def _(dve):
            nc.vector.memset(stat[:, 63:64], EPS).then_inc(S["eps_ready"], 1)
            nc.vector.memset(stat[:, 62:63], 1.0).then_inc(S["eps_ready"], 1)
            nc.vector.memset(stat[:, 61:62], P * EPS).then_inc(S["eps_ready"], 1)
            nc.vector.memset(stat[:, 60:61], 64 * EPS).then_inc(S["eps_ready"], 1)
            nc.vector.memset(stat[:, 59:60], 64e-5).then_inc(S["eps_ready"], 1)
            dve.wait_ge(S["x_loaded"], 16)
            dve.wait_ge(S["const_loaded"], 32)
            for st in STAGES:
                if st[0] == "mix1":
                    mix1_vector(dve, st)
                if st[0] == "rms":
                    rms_vector(dve)
                if st[0] == "fox":
                    fox_vector(dve, st)
                if st[0] == "rwkv":
                    rwkv_vector(dve, st)
                if st[0] == "ffn":
                    norm_vector(dve, norm_of[st])
                    ffn_vector(dve, st[1], 0.5 if st[1] < 2 else 1.0)

        @block.tensor
        def _(pe):
            pe.wait_ge(S["const_loaded"], 32)
            for st in STAGES:
                if st[0] == "mix1":
                    mix1_tensor(pe, st)
                if st[0] == "fox":
                    fox_tensor(pe, st)
                if st[0] == "rwkv":
                    rwkv_tensor(pe, st)
                if st[0] == "ffn":
                    norm_tensor(pe, norm_of[st])
                    ffn_tensor(pe, st[1], norm_of[st])


def kernel(**inputs):
    import concourse.bacc as bacc
    from concourse.bass_utils import run_bass_kernel_spmd

    a = {k: np.asarray(v) for k, v in inputs.items()}
    names = stream_plan(STAGES)
    stream = np.stack([lay_out_chunk(n, a) for n in names])
    rows = {"gm_w_s": a["gm_w_s"][0], "gm_ln_g": a["gm_ln_g"][0], "gm_ln_b": a["gm_ln_b"][0],
            "gm_bias": np.repeat(a["gm_b_s"][0].reshape(4, 2, P), 64, axis=1).transpose(1, 0, 2),
            "dn_norm": a["dn_norm"][0], "gates": np.concatenate([a["dn_a_log"][0], a["dn_dt_bias"][0]]),
            "final_norm": a["final_norm"], "pool_w": a["hy_pool_w_2"][0], "f_bias": a["hy_f_bias_2"][0]}
    rows = {k: np.ascontiguousarray(v) for k, v in rows.items()}
    arrays = {"stream": stream, "consts": CONSTS, "vectors": lay_out_vectors(a), "x_in": a["x"].reshape(TOK, D), **rows}
    nc = bacc.Bacc("TRN2", target_bir_lowering=False, num_devices=1)
    h = {k: nc.dram_tensor(k, v.shape, mybir.dt.from_np(v.dtype), kind="ExternalInput").ap() for k, v in arrays.items()}
    out = nc.dram_tensor("out", (TOK, D), F32, kind="ExternalOutput").ap()
    build(nc, h["stream"], h["consts"], h["vectors"], h["x_in"], {k: h[k] for k in rows},
          nc.dram_tensor("kept_x", (P, TT * D), F32, kind="Internal").ap(), out)
    r = run_bass_kernel_spmd(nc, [arrays], core_ids=[0])
    return r.results[0]["out"].reshape(1, TOK, D)
```

```python
from contextlib import ExitStack

import numpy as np

import concourse.bass as bass
from concourse import mybir

P = 128
TOK = 256
TT = TOK // P
D = 1024
KT = D // P
FF = 2816
GROUPS = FF // 256
CHUNK_COLS = 2048
RAW = 3
SPLIT = 3
EPS = 1e-6

F32 = mybir.dt.float32
F32R = mybir.dt.float32r
ALU = mybir.AluOpType
ACT = mybir.ActivationFunctionType
AX_X = mybir.AxisListType.X


def ffn_chunks(f):
    names = [("gate", f, 0), ("up", f, 0)]
    for g in range(1, GROUPS):
        names += [("gate", f, g), ("up", f, g), ("down", f, g - 1)]
    return names + [("down", f, GROUPS - 1)]


def stream_plan(stages):
    names = []
    for s in stages:
        if s[0] == "ffn":
            names += ffn_chunks(s[1])
        if s[0] == "mix1":
            names += [("w_in", 0, j) for j in MIX1_ORDER] + [("w_out", 0, j) for j in range(4)]
        if s[0] == "fox":
            names += [("hy_w_in", 0, j) for j in FOX_ORDER] + [("hy_w_out", 0, j) for j in range(4)]
        if s[0] == "rwkv":
            names += RWKV_ORDER
    return names


MIX1_ORDER = [12, 6, 7, 4, 5, 8, 9, 2, 3, 0, 1, 10, 11]
FOX_ORDER = [8, 0, 1, 2, 3, 4, 5, 9, 10, 6, 7]
RWKV_ORDER = [("lora", 0, 0), ("lora", 0, 1)] + [("rw", 0, j) for j in (4, 5, 6, 7, 0, 1, 2, 3, 8, 9, 10, 11)] + \
    [("lora", 0, 2)] + \
    [("rw_o", 0, j) for j in range(4)]
STAGES = [("ffn", 0), ("mix1", 0), ("ffn", 1), ("rms", 0), ("fox", 0), ("ffn", 2), ("rwkv", 0), ("ffn", 3)]


def col_chunk(w, c0, n=256):
    part = w[:, c0:c0 + n]
    if part.shape[1] < 256:
        part = np.concatenate([part, np.zeros((w.shape[0], 256 - part.shape[1]), w.dtype)], 1)
    return part.reshape(KT, P, 256).transpose(1, 0, 2).reshape(P, CHUNK_COLS)


def row_chunk(w, g):
    return w[g * 256:(g + 1) * 256].reshape(2, P, D).transpose(1, 0, 2).reshape(P, CHUNK_COLS)


def lay_out_chunk(name, a):
    kind, f, j = name
    ffn = {0: ("ffn1_w_gate", "ffn1_w_up", "ffn1_w_down", 0), 1: ("ffn2_w_gate", "ffn2_w_up", "ffn2_w_down", 0),
           2: ("ffn_w_gate_2", "ffn_w_up_2", "ffn_w_down_2", 0), 3: ("ffn_w_gate_2", "ffn_w_up_2", "ffn_w_down_2", 1)}
    if kind in ("gate", "up", "down"):
        w = a[ffn[f][("gate", "up", "down").index(kind)]][ffn[f][3]]
        return row_chunk(w, j) if kind == "down" else col_chunk(w, j * 256)
    if kind == "rw":
        return col_chunk(a[("rw_w_r_2", "rw_w_k_2", "rw_w_v_2")[j // 4]][0], (j % 4) * 256)
    if kind == "rw_o":
        return col_chunk(a["rw_w_o_2"][0], j * 256)
    if kind == "lora":
        g1, g2 = a["rw_g1_2"][0], a["rw_g2_2"][0]
        if j == 0:
            return col_chunk(np.concatenate([a["rw_w1_2"][0], a["rw_a1_2"][0], g1[:, :P]], 1), 0)
        if j == 1:
            tail = g1[:, P:].reshape(KT, P, 32).transpose(1, 0, 2).reshape(P, 256)
            top = np.concatenate([a["rw_w2_2"][0], a["rw_a2_2"][0]], 0)
            return np.concatenate([top, tail, np.zeros((P, 768), g1.dtype)], 1)
        return np.concatenate([g2[:P], np.concatenate([g2[P:], np.zeros((96, D), g2.dtype)], 0)], 1)
    if kind == "hy_w_in":
        return col_chunk(a["hy_w_in_2"][0], *{8: (2048, 8), 9: (2056,), 10: (2312,)}.get(j, (j * 256,)))
    return col_chunk(a[{"w_in": "w_in", "w_out": "w_out", "hy_w_in": "hy_w_in_2", "hy_w_out": "hy_w_out_2"}[kind]][0], j * 256)


def shape_constants():
    i = np.arange(P)[None, :]
    j = np.arange(P)[:, None]
    same = (i // 64) == (j // 64)
    parts = {
        "ident": i == j,
        "before": (j < i) & same,
        "upto": (j <= i) & same,
        "neg_upto": -1.0 * ((j <= i) & same),
        "after": (j > i) & same,
        "chunk0": (j < 64) & (i >= 0),
        "chunk1": (j >= 64) & (i >= 0),
        "upto_all": j <= i,
        "ones": (i >= 0) & (j >= 0),
        "same64": same,
        "gm_mask": ~((j >= 64) & (i < 64)),
    }
    parts["level1"] = (i // 2 == j // 2) & (i % 2 == 1) & (j % 2 == 0)
    for s in (2, 4, 8, 16, 32):
        parts[f"level{s}"] = (i // (2 * s) == j // (2 * s)) & ((j // s) % 2 == 1) & ((i // s) % 2 == 0)
    cols, at = [], {}
    n = 0
    for name, m in parts.items():
        at[name] = n
        cols.append(np.asarray(m).astype(np.float32))
        n += P
    at["zero_causal"] = n
    n += P
    at["causal"] = n
    cols.append(np.zeros((P, P), np.float32))
    cols.append(np.where(i > j, np.float32(-1e30), np.float32(0)).astype(np.float32))
    n += P
    at["pool"] = n
    t = np.arange(16)
    pool = np.concatenate([1.0 / np.minimum(t + 1, w) for w in (2, 4, 8, 16)]).astype(np.float32)
    cols.append(np.broadcast_to(pool, (P, 64)))
    n += 64
    at["restart"] = n
    cols.append(np.broadcast_to((np.arange(TOK) % 64 != 0).astype(np.float32), (P, TOK)))
    n += TOK
    return np.ascontiguousarray(np.concatenate(cols, 1)), at


CONSTS, CONST_AT = shape_constants()

VEC = [("ffn1_norm", 8), ("mix_norm", 8), ("ffn2_norm", 8), ("mix_norm_2a", 8), ("ffn_norm_2a", 8),
       ("mix_norm_2b", 8), ("ffn_norm_2b", 8), ("conv", 48), ("pool_scale", 4), ("q_gain", 1), ("k_gain", 1),
       ("mu", 48), ("w0", 8), ("a0", 8), ("k_k", 8), ("k_a", 8), ("r_k", 8), ("ln_w", 8), ("ln_b", 8)]
VEC_AT = {}
_n = 0
for _name, _w in VEC:
    VEC_AT[_name] = _n
    _n += _w
VEC_COLS = _n


def lay_out_vectors(a):
    cm = lambda v: v.reshape(-1, P).T
    twice = lambda v: np.concatenate([v, v]).reshape(1, P).T
    parts = [cm(a["ffn1_norm"][0]), cm(a["mix_norm"][0]), cm(a["ffn2_norm"][0]), cm(a["mix_norm_2"][0]),
             cm(a["ffn_norm_2"][0]), cm(a["mix_norm_2"][1]), cm(a["ffn_norm_2"][1]),
             np.concatenate([cm(a["dn_conv_w"][0, k]) for k in range(4)], 1),
             cm(a["hy_pool_scale_2"][0]), twice(a["hy_q_gain_2"][0]), twice(a["hy_k_gain_2"][0]),
             np.concatenate([cm(a["rw_mu_2"][0, k]) for k in range(6)], 1),
             cm(a["rw_w0_2"][0]), cm(a["rw_a0_2"][0]), cm(a["rw_k_k_2"][0]), cm(a["rw_k_a_2"][0]),
             cm(a["rw_r_k_2"][0]), cm(a["rw_ln_w_2"][0]), cm(a["rw_ln_b_2"][0])]
    return np.ascontiguousarray(np.concatenate(parts, 1))


def build(nc, stream, consts, vectors, x_in, rows, kept_x, out):
    names = stream_plan(STAGES)
    CH = {name: c for c, name in enumerate(names)}
    NCH = len(names)
    ctx = ExitStack()
    with ctx:
        def sb(name, shape, dt=F32):
            return ctx.enter_context(nc.sbuf_tensor(name, shape, dt))

        def sem(name):
            return ctx.enter_context(nc.semaphore(name))

        raw = sb("raw", [P, RAW, CHUNK_COLS])
        whi = sb("whi", [P, SPLIT, CHUNK_COLS], F32R)
        wlo = sb("wlo", [P, SPLIT, CHUNK_COLS], F32R)
        hhi = sb("hhi", [P, KT, TOK], F32R)
        hlo = sb("hlo", [P, KT, TOK], F32R)
        ahi = sb("ahi", [P, 2, 2, TOK], F32R)
        alo = sb("alo", [P, 2, 2, TOK], F32R)
        x = sb("x", [P, TT, D])
        con = sb("con", [P, CONSTS.shape[1]])
        vec = sb("vec", [P, VEC_COLS])
        stat = sb("stat", [P, 64])
        ARENA = 23360
        arena = sb("arena", [P, ARENA])
        psum = ctx.enter_context(nc.psum_tensor("psum", [P, 8, 512], F32))

        def const(name, n=P):
            return con[:, CONST_AT[name]:CONST_AT[name] + n]

        def area(at, *shape):
            n = int(np.prod(shape))
            assert at + n <= ARENA, (at, shape)
            v = arena[:, at:at + n]
            if len(shape) == 2:
                v = v.rearrange("p (a b) -> p a b", a=shape[0])
            if len(shape) == 3:
                v = v.rearrange("p (a b c) -> p a b c", a=shape[0], b=shape[1])
            return v

        xn = area(0, TT, D)
        junk = area(2048, TT, D)
        sg = area(4096, 2, 512)
        act = area(5120, 2, 512)

        S = {}

        def s(name):
            if name not in S:
                S[name] = sem(name)
            return S[name]

        raw_loaded = [sem(f"raw_loaded{i}") for i in range(RAW)]
        for n in ("high_made", "low_made", "chunk_used", "const_loaded", "x_loaded", "stored",
                  "x_ready", "rms_squares", "rms_root", "rms_scale", "rows_scaled", "turned", "h_high", "h_low",
                  "act_step", "dve_step", "eps_ready"):
            s(n)
        x_ready = S["x_ready"]
        high_made, low_made, chunk_used = S["high_made"], S["low_made"], S["chunk_used"]

        STEPS_DONE = {}

        class Steps:

            def __init__(self, eng, name):
                self.eng, self.sem, self.n = eng, s(name), STEPS_DONE.get(name, 0)
                self.name = name

            def __call__(self, ins):
                ins.then_inc(self.sem, 1)
                self.n += 1
                STEPS_DONE[self.name] = self.n
                self.eng.wait_ge(self.sem, self.n)

        def high(eng, c, i=None):
            loaded, used, slot = 16 * (c // RAW + 1), c - SPLIT + 1, c % SPLIT
            eng.wait_ge(raw_loaded[c % RAW], loaded if i is None else loaded + 32 * i)
            if used > 0:
                eng.wait_ge(chunk_used, used if i is None else used + 6 * i)
            nc.scalar.activation(whi[:, slot, :], raw[:, c % RAW, :], ACT.Copy).then_inc(high_made, 1)

        x_base, bank_reads_before = {}, {}
        for k_, st_ in enumerate(STAGES):
            kind_ = {"mix1": "w_out", "fox": "hy_w_out", "rwkv": "rw_o"}.get(st_[0])
            if kind_:
                x_base[kind_] = 4 * k_

        norm_of, last_use, n = {}, {}, 0
        for st in STAGES:
            if st[0] != "rms":
                norm_of[st] = n
                n += 1
        firsts = [CH.get(("gate", st[1], 0)) for st in STAGES]

        class Highs:

            def __init__(self, eng):
                self.eng, self.next = eng, 0

            def upto(self, c):
                while self.next <= min(c, NCH - 1):
                    high(self.eng, self.next)
                    self.next += 1

        def three_passes(out, w_hi, w_lo, h_hi, h_lo, weights_stand, start, stop):
            if weights_stand:
                nc.tensor.matmul(out, w_hi, h_hi, start=start, stop=False)
                nc.tensor.matmul(out, w_hi, h_lo, start=False, stop=False)
                return nc.tensor.matmul(out, w_lo, h_hi, start=False, stop=stop)
            nc.tensor.matmul(out, h_hi, w_hi, start=start, stop=False)
            nc.tensor.matmul(out, h_hi, w_lo, start=False, stop=False)
            return nc.tensor.matmul(out, h_lo, w_hi, start=False, stop=stop)

        def columns_out(slot, bank, hi=hhi, lo=hlo, halves=(0, 1)):
            for j in halves:
                for k in range(KT):
                    w = (slice(None), slot, slice(k * 256 + j * P, k * 256 + j * P + P))
                    mm = three_passes(psum[:, bank, j * 256:(j + 1) * 256], whi[w], wlo[w], hi[:, k, :], lo[:, k, :],
                                      True, k == 0, k == KT - 1)
            return mm

        def tokens_out(slot, bank, hi=hhi, lo=hlo, n=256, halves=(0, 1)):
            for m in halves:
                for k in range(KT):
                    w = (slice(None), slot, slice(k * 256, k * 256 + n))
                    t = (slice(None), k, slice(m * P, m * P + P))
                    mm = three_passes(psum[:, bank, m * 256:m * 256 + n], whi[w], wlo[w], hi[t], lo[t],
                                      False, k == 0, k == KT - 1)
            return mm

        NORMS = ["ffn1_norm", "mix_norm", "ffn2_norm", "mix_norm_2a", "ffn_norm_2a", "mix_norm_2b", "ffn_norm_2b"]

        def norm_scalar(eng, n, last_use, stage):
            if n == 0:
                eng.wait_ge(S["x_loaded"], 16)
            else:
                eng.wait_ge(x_ready, 4 * stage)
                eng.wait_ge(S["rms_scale"], 2 * n)
            for m in range(TT):
                nc.scalar.activation(junk[:, m, :], x[:, m, :], ACT.Square, scale=1.0 / 32, accum_out=stat[:, m:m + 1])\
                    .then_inc(S["rms_squares"], 1)
            eng.wait_ge(S["rms_squares"], 2 * (n + 1))
            nc.scalar.activation(stat[:, 2:4], stat[:, 0:2], ACT.Sqrt, bias=stat[:, 63:64]).then_inc(S["rms_root"], 1)
            if last_use is not None:
                eng.wait_ge(chunk_used, last_use + 1)
            gain = VEC_AT[NORMS[n]]
            for b in range(4):
                eng.wait_ge(S["turned"], 4 * n + b + 1)
                for k in (2 * b, 2 * b + 1):
                    nc.scalar.activation(hhi[:, k, :], psum[:, b, (k % 2) * 256:(k % 2) * 256 + 256], ACT.Copy,
                                         scale=vec[:, gain + k:gain + k + 1]).then_inc(S["h_high"], 1)

        def norm_vector(eng, n):
            eng.wait_ge(S["rms_root"], n + 1)
            nc.vector.reciprocal(stat[:, 4:6], stat[:, 2:4]).then_inc(S["rms_scale"], 1)
            eng.wait_ge(S["rms_scale"], 2 * n + 1)
            for m in range(TT):
                nc.vector.tensor_scalar(xn[:, m, :], x[:, m, :], stat[:, 4 + m:5 + m], None, ALU.mult)\
                    .then_inc(S["rows_scaled"], 1)
            gain = VEC_AT[NORMS[n]]
            for b in range(4):
                for k in (2 * b, 2 * b + 1):
                    eng.wait_ge(S["h_high"], 8 * n + 2 * b + 2)
                    ins = nc.vector.scalar_tensor_tensor(
                        out=hlo[:, k, :], in0=psum[:, b, (k % 2) * 256:(k % 2) * 256 + 256],
                        scalar=vec[:, gain + k:gain + k + 1], in1=hhi[:, k, :].bitcast(F32),
                        op0=ALU.mult, op1=ALU.subtract)
                    ins.then_inc(S["h_low"], 1)
            eng.wait_ge(S["h_low"], 8 * n + 8)
            nc.vector.tensor_copy(stat[:, 6:7], stat[:, 5:6]).then_inc(S["rms_scale"], 1)

        def norm_tensor(eng, n):
            for b in range(4):
                if n:
                    eng.wait_ge(S["h_low"], 8 * n)
                for k in (2 * b, 2 * b + 1):
                    for m in range(TT):
                        eng.wait_ge(S["rows_scaled"], 2 * n + m + 1)
                        at = (k % 2) * 256 + m * P
                        mm = nc.tensor.transpose(psum[:, b, at:at + P], xn[:, m, k * P:(k + 1) * P], const("ident"))
                mm.then_inc(S["turned"], 1)

        def ffn_tensor(eng, f, n):
            product, act_low = s("ffn_product"), s("ffn_act_low")
            c0 = CH[("gate", f, 0)]

            def step(kind, c, g, start=False, stop=False, i=None):
                b, slot, more = g % 2, c % SPLIT, lambda v, k: v if i is None else v + k * i
                eng.wait_ge(low_made, more(c + 1, 6))
                if kind == "gate":
                    if g >= 2:
                        eng.wait_ge(product, GROUPS * f + more(g - 1, 2))
                    columns_out(slot, b).then_inc(chunk_used, 1)
                if kind == "up":
                    columns_out(slot, 2 + b).then_inc(chunk_used, 1)
                if kind == "down":
                    eng.wait_ge(act_low, GROUPS * f + more(g + 1, 2))
                    for m in range(TT):
                        for half in range(2):
                            for j in range(2):
                                t = (slice(None), b, j, slice(m * P, m * P + P))
                                w = (slice(None), slot, slice(j * D + half * 512, j * D + half * 512 + 512))
                                mm = three_passes(psum[:, 4 + 2 * m + half, :], whi[w], wlo[w], ahi[t], alo[t],
                                                  False, start and j == 0, stop and j == 1)
                    mm.then_inc(chunk_used, 1)

            def group(c, g, start=False, i=None):
                step("gate", c, g, i=i)
                step("up", c + 1, g, i=i)
                step("down", c + 2, g - 1, start=start, i=i)

            eng.wait_ge(S["h_low"], 8 * n + 8)
            step("gate", c0, 0)
            step("up", c0 + 1, 0)
            group(c0 + 2, 1, start=True)
            group(c0 + 5, 2)
            with eng.Fori(0, (GROUPS - 3) // 2) as i:
                group(c0 + 8, 3, i=i)
                group(c0 + 11, 4, i=i)
            step("down", c0 + 32, GROUPS - 1, stop=True)

        def ffn_scalar(eng, f, highs):
            silu_done, act_high, product = s("ffn_silu_done"), s("ffn_act_high"), s("ffn_product")
            c0 = CH[("gate", f, 0)]

            def silu(c, g, i=None):
                more = lambda v, k: v if i is None else v + k * i
                eng.wait_ge(chunk_used, more(c + 1, 6))
                if g >= 2:
                    eng.wait_ge(product, GROUPS * f + more(g - 1, 2))
                nc.scalar.activation(sg[:, g % 2, :], psum[:, g % 2, :], ACT.Silu).then_inc(silu_done, 1)

            def act_highs(c, g, i=None):
                more = lambda v, k: v if i is None else v + k * i
                eng.wait_ge(product, GROUPS * f + more(g + 1, 2))
                if g >= 2:
                    eng.wait_ge(chunk_used, more(c, 6))
                b = g % 2
                nc.scalar.activation(ahi[:, b, :, :], act[:, b, :].rearrange("p (a b) -> p a b", a=2), ACT.Copy)\
                    .then_inc(act_high, 1)

            def group(c, g, i=None):
                if i is None:
                    highs.upto(c + 3)
                else:
                    high(eng, c + 3, i)
                silu(c, g, i)
                if i is None:
                    highs.upto(c + 4)
                else:
                    high(eng, c + 4, i)
                act_highs(c, g, i)
                if i is None:
                    highs.upto(c + 5)
                else:
                    high(eng, c + 5, i)

            highs.upto(c0 + 2)
            silu(c0, 0)
            highs.upto(c0 + 3)
            act_highs(c0, 0)
            highs.upto(c0 + 4)
            group(c0 + 2, 1)
            group(c0 + 5, 2)
            with eng.Fori(0, (GROUPS - 5) // 2) as i:
                group(c0 + 8, 3, i)
                group(c0 + 11, 4, i)
            highs.next = c0 + 8 + 3 * (GROUPS - 5) + 3
            group(c0 + 26, 9)
            group(c0 + 29, 10)

        def ffn_vector(eng, f, factor):
            silu_done, act_high, act_low = s("ffn_silu_done"), s("ffn_act_high"), s("ffn_act_low")
            product = s("ffn_product")
            c0 = CH[("gate", f, 0)]

            def group(c, g, i=None):
                more = lambda v, k: v if i is None else v + k * i
                b = g % 2
                eng.wait_ge(silu_done, GROUPS * f + more(g + 1, 2))
                eng.wait_ge(chunk_used, more(c + 2, 6))
                if g >= 2:
                    eng.wait_ge(act_low, GROUPS * f + more(g - 1, 2))
                nc.vector.tensor_tensor(act[:, b, :], sg[:, b, :], psum[:, 2 + b, :], ALU.mult).then_inc(product, 1)
                eng.wait_ge(act_high, GROUPS * f + more(g + 1, 2))
                flat = lambda t: t[:, b, :, :].rearrange("p a b -> p (a b)")
                nc.vector.tensor_tensor(flat(alo), act[:, b, :], flat(ahi).bitcast(F32), ALU.subtract)\
                    .then_inc(act_low, 1)

            group(c0, 0)
            group(c0 + 2, 1)
            group(c0 + 5, 2)
            with eng.Fori(0, (GROUPS - 3) // 2) as i:
                group(c0 + 8, 3, i)
                group(c0 + 11, 4, i)
            eng.wait_ge(chunk_used, c0 + 33)
            for m in range(TT):
                for half in range(2):
                    xs = x[:, m, half * 512:half * 512 + 512]
                    nc.vector.scalar_tensor_tensor(out=xs, in0=psum[:, 4 + 2 * m + half, :], scalar=factor, in1=xs,
                                                   op0=ALU.mult, op1=ALU.add).then_inc(x_ready, 1)

        LEVELS = (2, 4, 8, 16, 32)
        for n_ in ("inv_start", "inv_turned", "inv_copied", "inv_x", "inv_masked", "inv_summed", "inv_updated"):
            s(n_)
        INV = {k: S[k] for k in S if k.startswith("inv_")}

        def inverse_start(steps, LT, TTr, op):
            for g in range(2):
                steps(nc.vector.tensor_tensor(TTr[g], LT[g], four(const("level1")), ALU.mult))
                nc.vector.tensor_tensor(TTr[g], four(const("ident")), TTr[g], op).then_inc(INV["inv_start"], 1)

        def inverse_level_vector(eng, u, n, T, TTr, X, op):
            for g in range(2):
                eng.wait_ge(INV["inv_x"], 10 * u + 2 * n + g + 1)
                nc.vector.tensor_tensor(X[g], bank4(2 * g), four(const(f"level{LEVELS[n]}")), ALU.mult)\
                    .then_inc(INV["inv_masked"], 1)
            for g in range(2):
                eng.wait_ge(INV["inv_summed"], 10 * u + 2 * n + g + 1)
                if n < len(LEVELS) - 1:
                    nc.vector.tensor_tensor(T[g], T[g], bank4(2 * g), op)
                nc.vector.tensor_tensor(TTr[g], TTr[g], bank4(2 * g + 1), op).then_inc(INV["inv_updated"], 1)

        def inverse_scalar(eng, u, T):
            for g in range(2):
                eng.wait_ge(INV["inv_turned"], 2 * u + g + 1)
                nc.scalar.activation(T[g], bank4(2 * g), ACT.Copy).then_inc(INV["inv_copied"], 1)

        def inverse_turn_tensor(eng, u, TTr):
            for g in range(2):
                eng.wait_ge(INV["inv_start"], 2 * u + g + 1)
                for h in range(4):
                    mm = nc.tensor.transpose(bank4(2 * g)[:, h, :], TTr[g][:, h, :], const("ident"))
                mm.then_inc(INV["inv_turned"], 1)

        def inverse_x_tensor(eng, u, n, LT, T):
            for g in range(2):
                if n:
                    eng.wait_ge(INV["inv_updated"], 10 * u + 2 * (n - 1) + g + 1)
                else:
                    eng.wait_ge(INV["inv_copied"], 2 * u + g + 1)
                for h in range(4):
                    mm = nc.tensor.matmul(bank4(2 * g)[:, h, :], LT[g][:, h, :], T[g][:, h, :], start=True, stop=True)
                mm.then_inc(INV["inv_x"], 1)

        def inverse_tx_tensor(eng, u, n, TTr, X):
            for g in range(2):
                eng.wait_ge(INV["inv_masked"], 10 * u + 2 * n + g + 1)
                if n < len(LEVELS) - 1:
                    for h in range(4):
                        nc.tensor.matmul(bank4(2 * g)[:, h, :], TTr[g][:, h, :], X[g][:, h, :], start=True, stop=True)
                for h in range(4):
                    mm = nc.tensor.matmul(bank4(2 * g + 1)[:, h, :], X[g][:, h, :], TTr[g][:, h, :], start=True, stop=True)
                mm.then_inc(INV["inv_summed"], 1)

        def four(m):
            return m.rearrange("p (a n) -> p a n", a=1).broadcast_to((P, 4, m.shape[1]))

        def bank4(b):
            return psum[:, b, :].rearrange("p (a n) -> p a n", a=4)

        def bank2(b):
            return psum[:, b, :].rearrange("p (a n) -> p a n", a=2)

        bank_read = {6: s("bank_read6"), 7: s("bank_read7")}
        PROJ = {}
        inv0 = {"rwkv": 1 if ("mix1", 0) in STAGES else 0}
        for c_, name_ in enumerate(names):
            if name_[0] in ("w_in", "hy_w_in", "rw"):
                PROJ[name_] = len(PROJ)

        def proj_bank(name):
            return 6 + PROJ[name] % 2

        def project(eng, name, form, **kw):
            c, q = CH[name], PROJ[name]
            eng.wait_ge(low_made, c + 1)
            if q >= 2:
                eng.wait_ge(bank_read[6 + q % 2], q // 2)
            form(c % SPLIT, 6 + q % 2, **kw).then_inc(chunk_used, 1)

        def project_half(eng, name, form, half):
            c, q = CH[name], PROJ[name]
            if half == 0:
                eng.wait_ge(low_made, c + 1)
                eng.wait_ge(bank_read[6 + q % 2], q // 2)
            mm = form(c % SPLIT, 6 + q % 2, halves=(half,))
            if half == 1:
                mm.then_inc(chunk_used, 1)

        def projected(eng, name):
            eng.wait_ge(chunk_used, CH[name] + 1)

        def read(ins, name):
            return ins.then_inc(bank_read[proj_bank(name)], 1)

        def add_out(eng, kind):
            for j in range(4):
                name = (kind, 0, j)
                projected(eng, name)
                xs = x[:, :, j * 256:(j + 1) * 256]
                nc.vector.tensor_tensor(xs, xs, bank2(6 + j % 2), ALU.add).then_inc(x_ready, 1)

        def out_tensor(eng, kind, ready, count):
            eng.wait_ge(ready, count)
            for j in range(4):
                c = CH[(kind, 0, j)]
                eng.wait_ge(low_made, c + 1)
                if j < 2:
                    eng.wait_ge(bank_read[6 + j], sum(1 for n_, q_ in PROJ.items() if CH[n_] < c and q_ % 2 == j))
                else:
                    eng.wait_ge(x_ready, x_base[kind] + j - 1)
                tokens_out(c % SPLIT, 6 + j % 2).then_inc(chunk_used, 1)

        cin = area(0, 12, 260)
        sq = area(3120, 8, 256)
        rs = area(5168, 8, 256)
        Dm = [area(0 + 512 * g, 4, P) for g in range(2)]
        LTm = [area(1024 + 512 * g, 4, P) for g in range(2)]
        ATm = [area(2048 + 512 * g, 4, P) for g in range(2)]
        Tm = [area(3072 + 512 * g, 4, P) for g in range(2)]
        TTm = [area(4096 + 512 * g, 4, P) for g in range(2)]
        Xm = [area(5120 + 512 * g, 4, P) for g in range(2)]
        ngB = [area(21296 + 512 * g, 4, P) for g in range(2)]
        qkv = area(7216, 12, 256)
        ktok = area(10288, 2, 512)
        vtok = area(11312, 2, 512)
        zg = area(12336, 2, 512)
        va = area(13360, 2, 512)
        yraw = area(14384, 4, 256)
        wsT = area(15408, 8, P)
        ws = area(16432, 8, P)
        Om = area(16432, 2, 512)
        lnp = area(17456, 2, 512)
        gbias = area(18480, 4, P)
        sm = area(18992, 256)
        Rm = area(19248, 4, P)
        Wb = area(19760, 2, 512)
        Sm = area(20784, 4, P)
        OQ = area(21296, 4, P)
        osq = area(21808, 2, 512)
        dnn = area(22832, P)
        alog = area(22960, 8)

        ba_y, ba_abs, ba_beta, ba_g, ba_l = (sm[:, 8 * k:8 * k + 8] for k in range(5))
        ex = sm[:, 40:72].rearrange("p (m k h) -> p m k h", m=2, k=4)
        neg_eg = sm[:, 72:80]
        bd = sm[:, 80:88]
        lnst = sm[:, 96:108]
        mv = sm[:, 108:112]
        lnr = sm[:, 112:116]
        osum = sm[:, 120:128]
        ort = sm[:, 128:136]
        orr = sm[:, 136:144]
        ealog = sm[:, 144:148]
        spl = sm[:, 152:160]
        mh = lambda v: v.rearrange("p (m h) -> p m h", m=2)
        KV_BANKS = (2, 3, 4, 0)
        DLOG_BANKS = (1, 5)
        QKV = {6: 4, 7: 6, 4: 0, 5: 2, 8: 8, 9: 10}

        def mix1_scalar(eng, highs, st):
            n, stage = norm_of[st], STAGES.index(st)
            eng.wait_ge(x_ready, 4 * stage)
            eng.dma_start(ws, rows["gm_w_s"].rearrange("g i j -> i g j")).then_inc(s("m1_loaded"), 16)
            eng.dma_start(lnp[:, 0, :], rows["gm_ln_g"].partition_broadcast(P)).then_inc(s("m1_loaded"), 16)
            eng.dma_start(lnp[:, 1, :], rows["gm_ln_b"].partition_broadcast(P)).then_inc(s("m1_loaded"), 16)
            eng.dma_start(gbias, rows["gm_bias"]).then_inc(s("m1_loaded"), 16)
            eng.dma_start(dnn, rows["dn_norm"].partition_broadcast(P)).then_inc(s("m1_loaded"), 16)
            eng.dma_start(alog, rows["gates"].partition_broadcast(P)).then_inc(s("m1_loaded"), 16)
            norm_scalar(eng, n, CH[("w_in", 0, 12)] - 1, stage)
            highs.upto(CH[("w_in", 0, 12)] + 2)
            steps = Steps(eng, "act_step")
            projected(eng, ("w_in", 0, 12))
            eng.wait_ge(s("m1_y"), 1)
            read(nc.scalar.activation(mh(ba_beta), bank2(proj_bank(("w_in", 0, 12)))[:, :, 0:4], ACT.Sigmoid),
                 ("w_in", 0, 12))
            steps(nc.scalar.activation(ba_abs, ba_y, ACT.Abs))
            eng.wait_ge(S["m1_loaded"], 96)
            nc.scalar.activation(ealog, alog[:, 0:4], ACT.Exp).then_inc(s("m1_sp"), 1)
            steps(nc.scalar.activation(ba_abs, ba_abs, ACT.Exp, scale=-1.0))
            nc.scalar.activation(ba_l, ba_abs, ACT.Ln, bias=stat[:, 62:63]).then_inc(s("m1_sp"), 1)

            def conv_in(j):
                name = ("w_in", 0, j)
                highs.upto(CH[name] + 2)
                projected(eng, name)
                t = QKV[j]
                if j == 6:
                    eng.wait_ge(s("m1_pads"), 1)
                read(nc.scalar.activation(cin[:, t:t + 2, 3:259], bank2(proj_bank(name)), ACT.Copy), name)

            def silu(j, order):
                t = QKV[j]
                eng.wait_ge(s("m1_conv"), order + 1)
                nc.scalar.activation(qkv[:, t:t + 2, :], qkv[:, t:t + 2, :], ACT.Silu).then_inc(s("m1_silu"), 1)
                if t < 8:
                    eng.wait_ge(S["m1_silu"], order + 1)
                    nc.scalar.activation(sq[:, t:t + 2, :], qkv[:, t:t + 2, :], ACT.Square).then_inc(s("m1_sq"), 1)

            def root(b, count):
                eng.wait_ge(s("m1_sums"), count)
                nc.scalar.activation(rs[:, 2 * b:2 * b + 2, :], bank2(b), ACT.Sqrt, scale=float(P) if b < 2 else 1.0,
                                     bias=stat[:, 61:62] if b < 2 else stat[:, 63:64]).then_inc(s("m1_root"), 1)

            for order, j in enumerate((6, 7, 4, 5, 8, 9)):
                conv_in(j)
                if order:
                    silu((6, 7, 4, 5, 8, 9)[order - 1], order - 1)
                if j == 5:
                    root(2, 1)
                    root(3, 2)
            silu(9, 5)
            root(0, 3)
            root(1, 4)
            eng.wait_ge(s("m1_gsums"), 1)
            nc.scalar.activation(ex, psum[:, 5, 0:32].rearrange("p (m k h) -> p m k h", m=2, k=4), ACT.Exp)\
                .then_inc(s("m1_ex"), 1)

            def gelu(j, to):
                name = ("w_in", 0, j)
                highs.upto(CH[name] + 2)
                projected(eng, name)
                read(nc.scalar.activation(to, bank2(proj_bank(name)), ACT.Gelu_apprx_tanh), name)
                highs.upto(CH[name] + 3)

            gelu(2, va[:, :, 0:256])
            for k, dst in enumerate((ktok[:, 0, :], ktok[:, 1, :], vtok[:, 0, :], vtok[:, 1, :])):
                eng.wait_ge(s("m1_kvturned"), k + 1)
                nc.scalar.activation(dst, psum[:, KV_BANKS[k], :], ACT.Copy).then_inc(s("m1_kvtok"), 1)
            for m in range(2):
                eng.wait_ge(s("m1_dlog"), m + 1)
                nc.scalar.activation(Dm[m], Dm[m], ACT.Exp).then_inc(s("m1_dexp"), 1)
            gelu(3, va[:, :, 256:512])
            inverse_scalar(eng, 0, Tm)
            gelu(0, yraw[:, 0:2, :])
            eng.wait_ge(s("m1_var"), 1)
            nc.scalar.activation(lnr[:, 0:2], mv.rearrange("p (m k) -> p m k", m=2)[:, :, 1], ACT.Sqrt,
                                 bias=stat[:, 63:64]).then_inc(s("m1_lnroot"), 1)
            gelu(1, yraw[:, 2:4, :])
            for c in range(4):
                r = slice((c % 2) * 64, (c % 2) * 64 + 64)
                eng.wait_ge(s("m1_ks"), c + 1)
                if c:
                    eng.wait_ge(s("m1_o"), c)
                for h in range(4):
                    nc.scalar.activation(OQ[r, h, :], psum[r, 1, h * P:(h + 1) * P], ACT.Copy,
                                         scale=ex[r, c // 2, 0, h:h + 1]).then_inc(s("m1_oq"), 1)
                if c % 2:
                    j = 10 + c // 2
                    name = ("w_in", 0, j)
                    projected(eng, name)
                    zc = zg[:, :, (j - 10) * 256:(j - 10) * 256 + 256]
                    read(nc.scalar.activation(zc, bank2(proj_bank(name)), ACT.Silu), name)
                    highs.upto(CH[name] + 3)
            for m in range(2):
                eng.wait_ge(s("m1_o"), 2 * m + 2)
                nc.scalar.activation(osq[:, m, :], Om[:, m, :], ACT.Square).then_inc(s("m1_osq"), 1)
            eng.wait_ge(s("m1_osum"), 2)
            nc.scalar.activation(ort, osum, ACT.Sqrt, scale=1.0 / P, bias=stat[:, 63:64]).then_inc(s("m1_oroot"), 1)
            eng.wait_ge(s("m1_gated"), 2)
            eng.wait_ge(chunk_used, CH[("w_in", 0, 11)] + 1)
            nc.scalar.activation(hhi[:, 0:4, :], yraw, ACT.Copy).then_inc(s("m1_yhi"), 1)
            for b in range(2):
                eng.wait_ge(s("m1_oturned"), b + 1)
                nc.scalar.activation(hhi[:, 4 + 2 * b:6 + 2 * b, :], bank2(b), ACT.Copy).then_inc(s("m1_yhi"), 1)
            for j in range(4):
                highs.upto(CH[("w_out", 0, j)] + 3)

        def mix1_vector(eng, st):
            norm_vector(eng, norm_of[st])
            steps = Steps(eng, "dve_step")
            eng.wait_ge(chunk_used, CH[("w_in", 0, 12)] + 1)
            eng.wait_ge(s("m1_loaded"), 96)
            nc.vector.tensor_tensor(mh(ba_y), bank2(proj_bank(("w_in", 0, 12)))[:, :, 4:8],
                                    alog[:, 4:8].rearrange("p (a h) -> p a h", a=1).broadcast_to((P, 2, 4)), ALU.add)\
                .then_inc(s("m1_y"), 1)
            nc.vector.memset(cin[:, :, 0:3], 0.0).then_inc(s("m1_pads"), 1)
            eng.wait_ge(S["m1_y"], 1)
            steps(nc.vector.tensor_scalar(spl, ba_y, 0.0, None, ALU.max))
            eng.wait_ge(s("m1_sp"), 2)
            steps(nc.vector.tensor_tensor(spl, spl, ba_l, ALU.add))
            nc.vector.scalar_tensor_tensor(out=mh(ba_g), in0=mh(spl), scalar=-1.0,
                                           in1=ealog.rearrange("p (a h) -> p a h", a=1).broadcast_to((P, 2, 4)),
                                           op0=ALU.mult, op1=ALU.mult).then_inc(s("m1_g"), 1)
            nc.vector.memset(Rm, 0.0).then_inc(s("m1_zero"), 1)
            nc.vector.memset(Wb, 0.0).then_inc(S["m1_zero"], 1)
            nc.vector.memset(Sm, 0.0).then_inc(S["m1_zero"], 1)
            for b in range(2):
                eng.wait_ge(s("m1_wturned"), b + 1)
                nc.vector.tensor_tensor(wsT[:, 4 * b:4 * b + 4, :], bank4(4 + b), four(const("gm_mask")), ALU.mult)\
                    .then_inc(s("m1_wsT"), 1)
            eng.wait_ge(S["m1_g"], 1)
            for m in range(2):
                nc.vector.tensor_scalar(ngB[m], mh(ba_g)[:, m, :].rearrange("p (h a) -> p h a", a=1).broadcast_to((P, 4, P)),
                                        -1.0, None, ALU.mult).then_inc(s("m1_ngB"), 1)

            def conv(j):
                name = ("w_in", 0, j)
                eng.wait_ge(bank_read[proj_bank(name)], PROJ[name] // 2 + 1)
                t0 = QKV[j]
                tap = lambda k, t: vec[:, VEC_AT["conv"] + 12 * k + t:VEC_AT["conv"] + 12 * k + t + 1]
                for k in (3, 2, 1, 0):
                    for t in (t0, t0 + 1):
                        if k == 3:
                            ins = nc.vector.tensor_scalar(qkv[:, t, :], cin[:, t, 3:259], tap(3, t), None, ALU.mult)
                        else:
                            ins = nc.vector.scalar_tensor_tensor(out=qkv[:, t, :], in0=cin[:, t, k:k + 256], scalar=tap(k, t),
                                                                 in1=qkv[:, t, :], op0=ALU.mult, op1=ALU.add)
                    if k:
                        steps(ins)
                ins.then_inc(s("m1_conv"), 1)

            def unit(b, count):
                eng.wait_ge(s("m1_root"), count)
                eng.wait_ge(s("m1_sq"), 2 if b >= 2 else 4)
                steps(nc.vector.reciprocal(rs[:, 2 * b:2 * b + 2, :], rs[:, 2 * b:2 * b + 2, :]))
                nc.vector.tensor_tensor(qkv[:, 2 * b:2 * b + 2, :], qkv[:, 2 * b:2 * b + 2, :], rs[:, 2 * b:2 * b + 2, :],
                                        ALU.mult).then_inc(s("m1_unit"), 1)

            conv(6)
            conv(7)
            conv(4)
            conv(5)
            unit(2, 1)
            conv(8)
            unit(3, 2)
            conv(9)
            unit(0, 3)
            unit(1, 4)
            eng.wait_ge(s("m1_ex"), 1)
            nc.vector.tensor_scalar(mh(neg_eg), ex[:, :, 0, :], -1.0, None, ALU.mult).then_inc(s("m1_bd"), 1)
            eng.wait_ge(bank_read[proj_bank(("w_in", 0, 12))], PROJ[("w_in", 0, 12)] // 2 + 1)
            nc.vector.tensor_tensor(mh(bd), mh(ba_beta), ex[:, :, 1, :], ALU.mult).then_inc(s("m1_bd"), 1)
            eng.wait_ge(s("m1_conv"), 6)
            for m in range(2):
                eng.wait_ge(s("m1_dpsum"), m + 1)
                nc.vector.tensor_scalar(Dm[m], bank4(DLOG_BANKS[m]), 0.0, None, ALU.min).then_inc(s("m1_dlog"), 1)
            over = lambda v: v.rearrange("p (h a) -> p h a", a=1).broadcast_to((P, 4, P))
            for m in range(2):
                eng.wait_ge(s("m1_dexp"), m + 1)
                steps(nc.vector.tensor_tensor(Dm[m], Dm[m], four(const("upto")), ALU.mult))
                steps(nc.vector.tensor_tensor(Dm[m], Dm[m], over(mh(ba_beta)[:, m, :]), ALU.mult))
            for m in range(2):
                eng.wait_ge(s("m1_kk"), m + 1)
                nc.vector.tensor_tensor(LTm[m], bank4(m), Dm[m], ALU.mult)
                steps(nc.vector.tensor_tensor(ATm[m], bank4(2 + m), Dm[m], ALU.mult))
            eng.wait_ge(S["m1_unit"], 4)
            inverse_start(steps, LTm, TTm, ALU.subtract)
            eng.wait_ge(s("m1_kvtok"), 4)
            eng.wait_ge(S["m1_bd"], 2)
            for m in range(2):
                kt4 = ktok[:, m, :].rearrange("p (h d) -> p h d", h=4)
                nc.vector.tensor_tensor(kt4, kt4, over(mh(bd)[:, m, :]), ALU.mult).then_inc(s("m1_kd"), 1)
            inverse_level_vector(eng, 0, 0, Tm, TTm, Xm, ALU.subtract)
            eng.wait_ge(bank_read[proj_bank(("w_in", 0, 2))], PROJ[("w_in", 0, 2)] // 2 + 1)
            eng.wait_ge(bank_read[proj_bank(("w_in", 0, 3))], PROJ[("w_in", 0, 3)] // 2 + 1)
            for m in range(2):
                steps(nc.vector.bn_stats(lnst[:, 6 * m:6 * m + 6], va[:, m, :]))
            steps(nc.vector.bn_aggr(mv[:, 0:2], lnst[:, 0:6]))
            nc.vector.bn_aggr(mv[:, 2:4], lnst[:, 6:12]).then_inc(s("m1_var"), 1)
            inverse_level_vector(eng, 0, 1, Tm, TTm, Xm, ALU.subtract)
            eng.wait_ge(s("m1_lnroot"), 1)
            steps(nc.vector.reciprocal(lnr[:, 2:4], lnr[:, 0:2]))
            for m in range(2):
                steps(nc.vector.tensor_scalar(va[:, m, :], va[:, m, :], mv[:, 2 * m:2 * m + 1], lnr[:, 2 + m:3 + m],
                                              ALU.subtract, ALU.mult))
            for k, op in enumerate((ALU.mult, ALU.add)):
                ins = nc.vector.tensor_tensor(va, va, lnp[:, k:k + 1, :].broadcast_to((P, 2, 512)), op)
                if k == 0:
                    steps(ins)
            ins.then_inc(s("m1_ln"), 1)
            for n in range(2, len(LEVELS)):
                inverse_level_vector(eng, 0, n, Tm, TTm, Xm, ALU.subtract)
            for j in (0, 1):
                eng.wait_ge(bank_read[proj_bank(("w_in", 0, j))], PROJ[("w_in", 0, j)] // 2 + 1)
            for m in range(2):
                eng.wait_ge(s("m1_mixed"), m + 1)
                steps(nc.vector.tensor_tensor(osq[:, m, :].rearrange("p (a n) -> p a n", a=4), bank4(4 + m), gbias, ALU.add))
                ys = yraw[:, :, m * P:(m + 1) * P]
                nc.vector.tensor_tensor(ys, ys, osq[:, m, :].rearrange("p (a n) -> p a n", a=4), ALU.mult)\
                    .then_inc(s("m1_gated"), 1)
            eng.wait_ge(S["m1_zero"], 3)
            for c in range(4):
                m, r = c // 2, slice((c % 2) * 64, (c % 2) * 64 + 64)
                eng.wait_ge(s("m1_ks"), c + 1)
                for h in range(4):
                    nc.vector.scalar_tensor_tensor(out=Rm[r, h, :], in0=psum[r, 0, h * P:(h + 1) * P],
                                                   scalar=neg_eg[r, 4 * m + h:4 * m + h + 1],
                                                   in1=vtok[r, m, h * P:(h + 1) * P], op0=ALU.mult, op1=ALU.add)\
                        .then_inc(s("m1_r"), 1)
                eng.wait_ge(s("m1_w"), c + 1)
                nc.vector.tensor_copy(Wb[r, c % 2, :], psum[r, 2, :]).then_inc(s("m1_wb"), 1)
                if c < 3:
                    eng.wait_ge(s("m1_spsum"), c + 1)
                    for h in range(4):
                        nc.vector.scalar_tensor_tensor(out=Sm[:, h, :], in0=Sm[:, h, :], scalar=ex[:, m, 2 + c % 2, h:h + 1],
                                                       in1=psum[:, 4, h * P:(h + 1) * P], op0=ALU.mult, op1=ALU.add)\
                            .then_inc(s("m1_s"), 1)
                eng.wait_ge(s("m1_opsum"), c + 1)
                eng.wait_ge(s("m1_oq"), 4 * c + 4)
                nc.vector.tensor_tensor(Om[r, m, :], psum[r, 3, :], OQ[r, :, :].rearrange("p h d -> p (h d)"), ALU.add)\
                    .then_inc(s("m1_o"), 1)
            for j in (10, 11):
                eng.wait_ge(bank_read[proj_bank(("w_in", 0, j))], PROJ[("w_in", 0, j)] // 2 + 1)
            steps(nc.vector.tensor_tensor(zg.rearrange("p m (h d) -> p (m h) d", h=4), zg.rearrange("p m (h d) -> p (m h) d", h=4),
                                          dnn.rearrange("p (a d) -> p a d", a=1).broadcast_to((P, 8, P)), ALU.mult))
            for m in range(2):
                eng.wait_ge(s("m1_osq"), m + 1)
                nc.vector.tensor_reduce(osum[:, 4 * m:4 * m + 4], osq[:, m, :].rearrange("p (h d) -> p h d", h=4), AX_X, ALU.add)\
                    .then_inc(s("m1_osum"), 1)
            eng.wait_ge(s("m1_oroot"), 1)
            steps(nc.vector.reciprocal(orr, ort))
            for m in range(2):
                o4 = Om[:, m, :].rearrange("p (h d) -> p h d", h=4)
                steps(nc.vector.tensor_tensor(o4, o4, over(orr[:, 4 * m:4 * m + 4]), ALU.mult))
                nc.vector.tensor_tensor(Om[:, m, :], Om[:, m, :], zg[:, m, :], ALU.mult).then_inc(s("m1_on"), 1)
            eng.wait_ge(s("m1_yhi"), 1)
            nc.vector.tensor_tensor(hlo[:, 0:4, :], yraw, hhi[:, 0:4, :].bitcast(F32), ALU.subtract).then_inc(s("m1_ylo"), 1)
            for b in range(2):
                eng.wait_ge(S["m1_yhi"], b + 2)
                nc.vector.tensor_tensor(hlo[:, 4 + 2 * b:6 + 2 * b, :], bank2(b), hhi[:, 4 + 2 * b:6 + 2 * b, :].bitcast(F32),
                                        ALU.subtract).then_inc(s("m1_ylo"), 1)
            add_out(eng, "w_out")

        def mix1_tensor(eng, st):
            norm_tensor(eng, norm_of[st])
            eng.wait_ge(s("m1_loaded"), 96)
            for b in range(2):
                for g in range(4):
                    mm = nc.tensor.transpose(bank4(4 + b)[:, g, :], ws[:, 4 * b + g, :], const("ident"))
                mm.then_inc(s("m1_wturned"), 1)
            eng.wait_ge(S["h_low"], 8 * norm_of[st] + 8)
            project(eng, ("w_in", 0, 12), tokens_out, n=8)
            def square_sums(b):
                eng.wait_ge(s("m1_sq"), 2 if b >= 2 else 4)
                nc.tensor.matmul(psum[:, b, :], const("ones"), sq[:, 2 * b:2 * b + 2, :], start=True, stop=True)\
                    .then_inc(s("m1_sums"), 1)

            for j in (6, 7, 4, 5):
                project(eng, ("w_in", 0, j), columns_out)
            square_sums(2)
            square_sums(3)
            for j in (8, 9):
                project(eng, ("w_in", 0, j), columns_out)
            square_sums(0)
            square_sums(1)
            eng.wait_ge(s("m1_g"), 1)
            eng.wait_ge(s("m1_wsT"), 2)
            for m in range(2):
                for k, mat in enumerate(("upto", "after", "chunk0", "chunk1")):
                    mm = nc.tensor.matmul(psum[:, 5, 16 * m + 4 * k:16 * m + 4 * k + 4], const(mat), mh(ba_g)[:, m, :],
                                          start=True, stop=True)
            mm.then_inc(s("m1_gsums"), 1)
            project(eng, ("w_in", 0, 2), tokens_out)
            eng.wait_ge(s("m1_root"), 4)
            eng.wait_ge(s("m1_unit"), 2)
            eng.wait_ge(s("m1_silu"), 6)
            for k, (t0, m) in enumerate(((4, 0), (4, 1), (8, 0), (8, 1))):
                for h in range(4):
                    mm = nc.tensor.transpose(bank4(KV_BANKS[k])[:, h, :], qkv[:, t0 + h, m * P:(m + 1) * P], const("ident"))
                mm.then_inc(s("m1_kvturned"), 1)
            eng.wait_ge(s("m1_ngB"), 2)
            eng.wait_ge(s("m1_ex"), 1)
            for m in range(2):
                b = DLOG_BANKS[m]
                nc.tensor.matmul(bank4(b), const("upto"), ngB[m], start=True, stop=False)
                for h in range(4):
                    mm = nc.tensor.matmul(bank4(b)[:, h, :], ngB[m][:, h, :], const("neg_upto"), start=False, stop=h == 3)
                mm.then_inc(s("m1_dpsum"), 1)
            project(eng, ("w_in", 0, 3), tokens_out)
            eng.wait_ge(s("m1_unit"), 4)
            eng.wait_ge(s("m1_kvtok"), 4)
            for m in range(2):
                eng.wait_ge(s("m1_dlog"), m + 1)
                for h in range(4):
                    nc.tensor.matmul(bank4(m)[:, h, :], qkv[:, 4 + h, m * P:(m + 1) * P], qkv[:, 4 + h, m * P:(m + 1) * P],
                                     start=True, stop=True)
                for h in range(4):
                    mm = nc.tensor.matmul(bank4(2 + m)[:, h, :], qkv[:, 4 + h, m * P:(m + 1) * P],
                                          qkv[:, h, m * P:(m + 1) * P], start=True, stop=True)
                mm.then_inc(s("m1_kk"), 1)

            def mixed(m):
                eng.wait_ge(s("m1_ln"), 1)
                for g in range(8):
                    p0 = (g % 2) * 64
                    mm = nc.tensor.matmul(psum[p0:p0 + 64, 4 + m, (g // 2) * P:(g // 2) * P + P], va[:, m, g * 64:g * 64 + 64],
                                          wsT[:, g, :], start=True, stop=True)
                mm.then_inc(s("m1_mixed"), 1)

            inverse_turn_tensor(eng, 0, TTm)
            for n in range(len(LEVELS)):
                inverse_x_tensor(eng, 0, n, LTm, Tm)
                if n < 2:
                    project_half(eng, ("w_in", 0, n), columns_out, 0)
                if n == 3:
                    mixed(0)
                inverse_tx_tensor(eng, 0, n, TTm, Xm)
                if n < 2:
                    project_half(eng, ("w_in", 0, n), columns_out, 1)
                if n == 3:
                    mixed(1)
            eng.wait_ge(INV["inv_updated"], 10)
            for c in range(4):
                m, tok = c // 2, slice((c // 2) * P, (c // 2) * P + P)
                if c == 0:
                    eng.wait_ge(s("m1_zero"), 3)
                else:
                    eng.wait_ge(s("m1_s"), 4 * c)
                    eng.wait_ge(s("m1_oq"), 4 * c)
                for h in range(4):
                    nc.tensor.matmul(bank4(0)[:, h, :], qkv[:, 4 + h, tok], Sm[:, h, :], start=True, stop=True)
                for h in range(4):
                    mm = nc.tensor.matmul(bank4(1)[:, h, :], qkv[:, h, tok], Sm[:, h, :], start=True, stop=True)
                mm.then_inc(s("m1_ks"), 1)
                project_half(eng, ("w_in", 0, 10 + c // 2), tokens_out, c % 2)
                eng.wait_ge(s("m1_r"), 4 * c + 4)
                for h in range(4):
                    mm = nc.tensor.matmul(bank4(2)[:, h, :], TTm[m][:, h, :], Rm[:, h, :], start=True, stop=True)
                mm.then_inc(s("m1_w"), 1)
                eng.wait_ge(s("m1_wb"), c + 1)
                eng.wait_ge(s("m1_kd"), 2)
                if c == 0:
                    eng.wait_ge(s("m1_gated"), 2)
                if c < 3:
                    for h in range(4):
                        mm = nc.tensor.matmul(bank4(4)[:, h, :], ktok[:, m, h * P:(h + 1) * P],
                                              Wb[:, c % 2, h * P:(h + 1) * P], start=True, stop=True)
                    mm.then_inc(s("m1_spsum"), 1)
                if c:
                    eng.wait_ge(s("m1_o"), c)
                for h in range(4):
                    mm = nc.tensor.matmul(bank4(3)[:, h, :], ATm[m][:, h, :], Wb[:, c % 2, h * P:(h + 1) * P],
                                          start=True, stop=True)
                mm.then_inc(s("m1_opsum"), 1)
            eng.wait_ge(s("m1_on"), 2)
            for b in range(2):
                for k in range(2):
                    for m in range(2):
                        mm = nc.tensor.transpose(psum[:, b, k * 256 + m * P:k * 256 + m * P + P],
                                                 Om[:, m, (2 * b + k) * P:(2 * b + k) * P + P], const("ident"))
                mm.then_inc(s("m1_oturned"), 1)
            out_tensor(eng, "w_out", s("m1_ylo"), 3)

        rsq = area(2048, TT, D)
        fin = area(4096, D)

        def rms_scalar(eng, stage):
            eng.wait_ge(x_ready, 4 * stage)
            eng.dma_start(fin, rows["final_norm"].partition_broadcast(P)).then_inc(s("fin_loaded"), 16)
            for m in range(TT):
                nc.scalar.activation(rsq[:, m, :], x[:, m, :], ACT.Square, scale=1.0 / 32, accum_out=stat[:, 8 + m:9 + m])\
                    .then_inc(s("fin_squares"), 1)
            eng.wait_ge(S["fin_squares"], 2)
            nc.scalar.activation(stat[:, 10:12], stat[:, 8:10], ACT.Sqrt, bias=stat[:, 63:64]).then_inc(s("fin_root"), 1)

        def rms_vector(eng):
            eng.wait_ge(s("fin_root"), 1)
            nc.vector.reciprocal(stat[:, 12:14], stat[:, 10:12]).then_inc(s("fin_scale"), 1)
            eng.wait_ge(S["fin_scale"], 1)
            eng.wait_ge(s("fin_loaded"), 16)
            for m in range(TT):
                for half in range(2):
                    xs = x[:, m, half * 512:half * 512 + 512]
                    nc.vector.scalar_tensor_tensor(out=xs, in0=xs, scalar=stat[:, 12 + m:13 + m],
                                                   in1=fin[:, half * 512:half * 512 + 512], op0=ALU.mult, op1=ALU.mult)\
                        .then_inc(x_ready, 1)

        fqk = area(0, 8, 256)
        fsq = area(2048, 8, 256)
        frs = area(4096, 8, 256)
        nlfB = area(6144, 2, 8 * P)
        fv = area(8192, 2, 512)
        fog = area(9216, 2, 512)
        U = area(10240, 4, 272)
        WA = area(11328, 4, 272)
        WB = area(12416, 4, 272)
        pooled = area(13504, 4, 256)
        pw = area(14528, 4, P)
        FL = area(15040, 2, 512)
        FP = area(16064, 2, 512)
        FT = area(17088, 2, 512)
        yo = area(18112, 2, 512)
        sf = area(19136, 256)
        fb, f_y, f_abs, f_l, f_n = (sf[:, 16 * k:16 * k + 16] for k in range(5))
        fmax, fneg = sf[:, 80:104], sf[:, 104:128]
        fsum, frec = sf[:, 128:144], sf[:, 144:160]
        fpart = sf[:, 160:176]
        UNITS = [(0, [p, p + 2, p + 4, p + 6]) for p in range(2)] + \
                [(1, [p + 4 * k, p + 4 * k + 2]) for k in range(2) for p in range(2)]
        mh8 = lambda v: v.rearrange("p (m h) -> p m h", m=2)

        def fox_scalar(eng, highs, st):
            n, stage = norm_of[st], STAGES.index(st)
            eng.wait_ge(x_ready, 4 * stage)
            eng.dma_start(pw, rows["pool_w"].rearrange("g c d -> c g d")).then_inc(s("m2_loaded"), 16)
            eng.dma_start(fb[:, 0:8], rows["f_bias"].partition_broadcast(P)).then_inc(s("m2_loaded"), 16)
            norm_scalar(eng, n, CH[("hy_w_in", 0, 8)] - 1, stage)
            steps = Steps(eng, "act_step")
            N = lambda j: ("hy_w_in", 0, j)

            def ready(j):
                highs.upto(CH[N(j)] + 2)
                projected(eng, N(j))

            highs.upto(CH[N(8)] + 2)
            eng.wait_ge(s("m2_y"), 1)
            steps(nc.scalar.activation(f_abs, f_y, ACT.Abs))
            steps(nc.scalar.activation(f_abs, f_abs, ACT.Exp, scale=-1.0))
            nc.scalar.activation(f_l, f_abs, ACT.Ln, bias=stat[:, 62:63]).then_inc(s("m2_l"), 1)
            for k, j in enumerate((0, 1, 2, 3)):
                ready(j)
                b = proj_bank(N(j))
                nc.scalar.activation(fqk[:, 2 * k:2 * k + 2, :], bank2(b), ACT.Copy).then_inc(s("m2_qk"), 1)
                read(nc.scalar.activation(fsq[:, 2 * k:2 * k + 2, :], bank2(b), ACT.Square), N(j))
            for j in (4, 5):
                ready(j)
                read(nc.scalar.activation(fv[:, :, (j - 4) * 256:(j - 4) * 256 + 256], bank2(proj_bank(N(j))), ACT.Copy), N(j))
            for b in range(4):
                eng.wait_ge(s("m2_sums"), b + 1)
                nc.scalar.activation(frs[:, 2 * b:2 * b + 2, :], bank2(b), ACT.Sqrt, scale=1.0 if b < 2 else 1.0 / 64,
                                     bias=stat[:, 60:61] if b < 2 else stat[:, 63:64]).then_inc(s("m2_root"), 1)
            eng.wait_ge(s("m2_pads"), 3)
            for j in (9, 10):
                ready(j)
                read(nc.scalar.activation(U[:, 2 * (j - 9):2 * (j - 9) + 2, 16:272], bank2(proj_bank(N(j))), ACT.Copy), N(j))
            for j in (6, 7):
                ready(j)
                read(nc.scalar.activation(fog[:, :, (j - 6) * 256:(j - 6) * 256 + 256], bank2(proj_bank(N(j))), ACT.Sigmoid),
                     N(j))
            highs.upto(CH[N(7)] + 3)
            for u, (m, heads) in enumerate(UNITS):
                keys = P * (m + 1)
                eng.wait_ge(s("m2_neg"), u + 1)
                if u >= 2:
                    eng.wait_ge(s("m2_pturned"), u - 1)
                for k, h in enumerate(heads):
                    nc.scalar.activation(FP[:, u % 2, k * keys:(k + 1) * keys], FL[:, u % 2, k * keys:(k + 1) * keys], ACT.Exp,
                                         bias=fneg[:, 4 * u + k:4 * u + k + 1], accum_out=fsum[:, 8 * m + h:8 * m + h + 1])\
                        .then_inc(s("m2_p"), 1)
                eng.wait_ge(s("m2_pturned"), u + 1)
                if u >= 2:
                    eng.wait_ge(s("m2_pv"), u - 1)
                nc.scalar.activation(FT[:, u % 2, :], psum[:, 2 + u % 2, :], ACT.Copy).then_inc(s("m2_pt"), 1)
            eng.wait_ge(chunk_used, CH[N(7)] + 1)
            for b in range(2):
                eng.wait_ge(s("m2_pooled"), b + 1)
                for g in (2 * b, 2 * b + 1):
                    nc.scalar.activation(hhi[:, 4 + g, :], bank2(b)[:, g % 2, :], ACT.Copy,
                                         scale=vec[:, VEC_AT["pool_scale"] + g:VEC_AT["pool_scale"] + g + 1])\
                        .then_inc(s("m2_yhi"), 1)
            for b in range(2):
                eng.wait_ge(s("m2_oturned"), b + 1)
                nc.scalar.activation(hhi[:, 2 * b:2 * b + 2, :], bank2(2 + b), ACT.Copy).then_inc(s("m2_yhi"), 1)
            for j in range(4):
                highs.upto(CH[("hy_w_out", 0, j)] + 3)

        def fox_vector(eng, st):
            norm_vector(eng, norm_of[st])
            steps = Steps(eng, "dve_step")
            N = lambda j: ("hy_w_in", 0, j)
            projected(eng, N(8))
            eng.wait_ge(s("m2_loaded"), 32)
            nc.vector.tensor_tensor(mh8(f_y), bank2(proj_bank(N(8)))[:, :, 0:8],
                                    fb[:, 0:8].rearrange("p (a h) -> p a h", a=1).broadcast_to((P, 2, 8)), ALU.add)\
                .then_inc(s("m2_y"), 1)
            eng.wait_ge(S["m2_y"], 1)
            read(nc.vector.tensor_scalar(f_n, f_y, -1.0, 0.0, ALU.mult, ALU.max), N(8))
            for t in (U, WA, WB):
                nc.vector.memset(t[:, :, 0:16], 0.0).then_inc(s("m2_pads"), 1)
            eng.wait_ge(s("m2_l"), 1)
            eng.wait_ge(bank_read[proj_bank(N(8))], PROJ[N(8)] // 2 + 1)
            steps(nc.vector.tensor_tensor(f_n, f_n, f_l, ALU.add))
            for m in range(2):
                nc.vector.tensor_scalar(nlfB[:, m, :].rearrange("p (h a) -> p h a", h=8),
                                        f_n[:, 8 * m:8 * m + 8].rearrange("p (h a) -> p h a", a=1).broadcast_to((P, 8, P)),
                                        1.0, None, ALU.mult).then_inc(s("m2_nlfB"), 1)
            for b in range(4):
                eng.wait_ge(s("m2_root"), b + 1)
                eng.wait_ge(s("m2_qk"), b + 1)
                t = slice(2 * b, 2 * b + 2)
                steps(nc.vector.reciprocal(frs[:, t, :], frs[:, t, :]))
                gain = VEC_AT["q_gain" if b < 2 else "k_gain"]
                nc.vector.scalar_tensor_tensor(out=fqk[:, t, :], in0=fqk[:, t, :], scalar=vec[:, gain:gain + 1],
                                               in1=frs[:, t, :], op0=ALU.mult, op1=ALU.mult).then_inc(s("m2_unit"), 1)
            for j in (9, 10):
                eng.wait_ge(bank_read[proj_bank(N(j))], PROJ[N(j)] // 2 + 1)
            eng.wait_ge(S["m2_pads"], 3)
            src = U
            for g0, dst in enumerate((WA, WB, WA, WB)):
                back = 2 ** g0
                steps(nc.vector.tensor_tensor(dst[:, g0:4, 16:272], src[:, g0:4, 16:272], src[:, g0:4, 16 - back:272 - back],
                                              ALU.add))
                src = dst
            for g, t in enumerate((WA, WB, WA, WB)):
                inv = const("pool", 64)[:, 16 * g:16 * g + 16]
                nc.vector.scalar_tensor_tensor(out=pooled[:, g, 16:256], in0=t[:, g, 32:272], scalar=1.0 / 2 ** (g + 1),
                                               in1=U[:, g, 32:272], op0=ALU.mult, op1=ALU.subtract).then_inc(s("m2_pool"), 1)
                steps(nc.vector.tensor_tensor(t[:, g, 16:32], t[:, g, 16:32], inv, ALU.mult))
                nc.vector.tensor_tensor(pooled[:, g, 0:16], t[:, g, 16:32], U[:, g, 16:32], ALU.subtract)\
                    .then_inc(S["m2_pool"], 1)
            def logits(u):
                m, heads = UNITS[u]
                nh, keys = len(heads), P * (m + 1)
                eng.wait_ge(s("m2_logits"), u + 1)
                if u >= 2:
                    eng.wait_ge(s("m2_p"), sum(len(x_[1]) for x_ in UNITS[:u - 1]))
                L3 = FL[:, u % 2, :].rearrange("p (h k) -> p h k", h=nh)
                mask = const("causal") if m == 0 else const("zero_causal", 256)
                mask = mask.rearrange("p (a k) -> p a k", a=1).broadcast_to((P, nh, keys))
                nc.vector.tensor_tensor(L3, psum[:, u % 2, :].rearrange("p (h k) -> p h k", h=nh), mask, ALU.add)\
                    .then_inc(s("m2_masked"), 1)
                eng.wait_ge(S["m2_masked"], u + 1)
                steps(nc.vector.tensor_reduce(fmax[:, 4 * u:4 * u + nh], L3, AX_X, ALU.max))
                nc.vector.tensor_scalar(fneg[:, 4 * u:4 * u + nh], fmax[:, 4 * u:4 * u + nh], -1.0, None, ALU.mult)\
                    .then_inc(s("m2_neg"), 1)

            for u in range(6):
                logits(u)
            for m in range(2):
                eng.wait_ge(s("m2_pv"), 2 if m == 0 else 6)
                steps(nc.vector.reciprocal(frec[:, 8 * m:8 * m + 8], fsum[:, 8 * m:8 * m + 8]))
                y3 = yo[:, m, :].rearrange("p (h d) -> p h d", h=8)
                steps(nc.vector.tensor_tensor(y3, psum[:, 4 + m, :].rearrange("p (h d) -> p h d", h=8),
                                              frec[:, 8 * m:8 * m + 8].rearrange("p (h a) -> p h a", a=1).broadcast_to((P, 8, 64)),
                                              ALU.mult))
                nc.vector.tensor_tensor(yo[:, m, :], yo[:, m, :], fog[:, m, :], ALU.mult).then_inc(s("m2_yo"), 1)
            for b in range(2):
                eng.wait_ge(s("m2_yhi"), 2 * b + 2)
                for g in (2 * b, 2 * b + 1):
                    nc.vector.scalar_tensor_tensor(out=hlo[:, 4 + g, :], in0=bank2(b)[:, g % 2, :],
                                                   scalar=vec[:, VEC_AT["pool_scale"] + g:VEC_AT["pool_scale"] + g + 1],
                                                   in1=hhi[:, 4 + g, :].bitcast(F32), op0=ALU.mult, op1=ALU.subtract)\
                        .then_inc(s("m2_ylo"), 1)
            for b in range(2):
                eng.wait_ge(s("m2_yhi"), 5 + b)
                nc.vector.tensor_tensor(hlo[:, 2 * b:2 * b + 2, :], bank2(2 + b), hhi[:, 2 * b:2 * b + 2, :].bitcast(F32),
                                        ALU.subtract).then_inc(s("m2_ylo"), 1)
            add_out(eng, "hy_w_out")

        def fox_tensor(eng, st):
            N = lambda j: ("hy_w_in", 0, j)
            norm_tensor(eng, norm_of[st])
            eng.wait_ge(S["h_low"], 8 * norm_of[st] + 8)
            project(eng, N(8), tokens_out, n=8)
            for j in (0, 1, 2, 3):
                project(eng, N(j), columns_out)
            for j in (4, 5):
                project(eng, N(j), tokens_out)
            for b in range(4):
                eng.wait_ge(bank_read[proj_bank(N(b))], PROJ[N(b)] // 2 + 1)
                nc.tensor.matmul(psum[:, b, :], const("same64"), fsq[:, 2 * b:2 * b + 2, :], start=True, stop=True)\
                    .then_inc(s("m2_sums"), 1)
            for j in (9, 10):
                project(eng, N(j), columns_out)
            for j in (6, 7):
                project(eng, N(j), tokens_out)
            eng.wait_ge(s("m2_unit"), 4)
            eng.wait_ge(s("m2_nlfB"), 2)

            def logits(u):
                m, heads = UNITS[u]
                keys = P * (m + 1)
                if u >= 2:
                    eng.wait_ge(s("m2_masked"), u - 1)
                for k, h in enumerate(heads):
                    o = psum[:, u % 2, k * keys:(k + 1) * keys]
                    r, t = slice((h % 2) * 64, (h % 2) * 64 + 64), h // 2
                    nc.tensor.matmul(o, fqk[r, t, m * P:(m + 1) * P], fqk[r, 4 + t, 0:keys], start=True, stop=False)
                    mm = nc.tensor.matmul(o, nlfB[:, 0, h * P:(h + 1) * P], const("upto_all", keys), start=False, stop=m == 0)
                    if m == 1:
                        mm = nc.tensor.matmul(o[:, P:2 * P], nlfB[:, 1, h * P:(h + 1) * P], const("upto_all"), start=False,
                                              stop=True)
                mm.then_inc(s("m2_logits"), 1)

            def values(u):
                m, heads = UNITS[u]
                eng.wait_ge(s("m2_pt"), u + 1)
                for k, h in enumerate(heads):
                    for t in range(m + 1):
                        mm = nc.tensor.matmul(psum[:, 4 + m, h * 64:h * 64 + 64],
                                              FT[:, u % 2, (k * (m + 1) + t) * P:(k * (m + 1) + t + 1) * P],
                                              fv[:, t, h * 64:h * 64 + 64], start=t == 0, stop=t == m)
                mm.then_inc(s("m2_pv"), 1)

            logits(0)
            for u, (m, heads) in enumerate(UNITS):
                if u < 5:
                    logits(u + 1)
                eng.wait_ge(s("m2_p"), sum(len(x_[1]) for x_ in UNITS[:u + 1]))
                if u >= 2:
                    eng.wait_ge(s("m2_pt"), u - 1)
                for k in range(4):
                    mm = nc.tensor.transpose(bank4(2 + u % 2)[:, k, :], FP[:, u % 2, k * P:(k + 1) * P], const("ident"))
                mm.then_inc(s("m2_pturned"), 1)
                if u:
                    values(u - 1)
            values(5)
            eng.wait_ge(s("m2_pool"), 8)
            eng.wait_ge(s("m2_masked"), 6)
            eng.wait_ge(s("m2_loaded"), 32)
            for b in range(2):
                for g in (2 * b, 2 * b + 1):
                    mm = nc.tensor.matmul(bank2(b)[:, g % 2, :], pw[:, g, :], pooled[:, g, :], start=True, stop=True)
                mm.then_inc(s("m2_pooled"), 1)
            eng.wait_ge(s("m2_yo"), 2)
            eng.wait_ge(s("m2_pt"), 6)
            for b in range(2):
                for k in range(2):
                    for m in range(2):
                        mm = nc.tensor.transpose(psum[:, 2 + b, k * 256 + m * P:k * 256 + m * P + P],
                                                 yo[:, m, (2 * b + k) * P:(2 * b + k) * P + P], const("ident"))
                mm.then_inc(s("m2_oturned"), 1)
            out_tensor(eng, "hy_w_out", s("m2_ylo"), 6)

        DECAY = float(np.exp(-0.5))
        ar = area(0, 2, 8 * 256).rearrange("p s (k t) -> p s k t", k=8)
        kk = ar[:, 0, :, :]
        rr = ar[:, 1, :, :]
        kx = area(4096, 8, 256)
        sw = area(6144, 8, 256)
        aa = area(8192, 8, 256)
        vt = area(10240, 2, D)
        roots = area(10240, 8, 256)
        shifted = area(12288, 8, 256)
        variant_x = area(14336, 8, 256)
        ht = area(16384, 8, 257)
        sums = area(18440, 8, 256)
        rk = shifted
        bkT = [area(at, 2, 8 * P).rearrange("p s (k t) -> p s k t", k=8) for at in (14336, 12288)]
        bk = [area(at, 2, D) for at in (6144, 14336)]
        ak_flat = [area(16384, 2048), raw[:, 0, :]]
        AK = [[f[:, 1024 * g:1024 * g + 1024].rearrange("p (a s n) -> p a s n", a=4, s=2) for g in range(2)] for f in ak_flat]
        RB = [[raw[:, 1, 1024 * i_ + 512 * g:1024 * i_ + 512 * g + 512].rearrange("p (a n) -> p a n", a=4)
               for g in range(2)] for i_ in range(2)]
        TT7 = [[area(at + 512 * g, 4, P) for g in range(2)] for at in (13312, 19456)]
        T7 = [area(12288 + 512 * g, 4, P) for g in range(2)]
        LT7 = [area(18432 + 512 * g, 4, P) for g in range(2)]
        X7 = [area(20480 + 512 * g, 4, P) for g in range(2)]
        U7, R7 = (raw[:, 2, 512 * i_:512 * i_ + 512].rearrange("p (a n) -> p a n", a=4) for i_ in range(2))
        STREAM_STOPS = CH.get(("rw_o", 0, 2))
        Z = area(21504, 8, P)
        s3m = area(22528, 512)
        pc = s3m[:, 0:32].rearrange("p (k c) -> p k c", k=8)
        bonus = s3m[:, 32:64]
        gsum, gmean, gvar, groot, gscale = (s3m[:, 64 + 32 * k:96 + 32 * k] for k in range(5))
        Y = x
        yt = area(0, 8, 256)
        ysq = area(12288, 2, D)
        wa_hi, wa_lo = ahi[:, 0, 0, :], alo[:, 0, 0, :]
        gm_hi, gm_lo = ahi[:, 1, 0, :], alo[:, 1, 0, :]
        gt_hi, gt_lo = ahi[:, 1, 1, :], alo[:, 1, 1, :]
        lw = area(20488, 3, 256)
        V_AT = lambda name, k: vec[:, VEC_AT[name] + k:VEC_AT[name] + k + 1]
        VARIANTS = (1, 4, 5, 2, 0, 3)
        FIRST_OF = {3: 4, 4: 0, 5: 8}
        RW = lambda j: ("rw", 0, j)
        L0, L1, L2 = (CH.get(("lora", 0, j)) for j in range(3))
        PASSES = [(m, q) for m in range(2) for q in range(2)]

        def z_steps(w, hh):
            return 5 * sum(1 for v_ in range(2 * w + hh) if 2 * PASSES[v_ // 2][0] + v_ % 2 < 3)

        def variant_used(eng, v):
            if v in (1, 2, 3):
                eng.wait_ge(s("rw_first"), v)
            if v > 3:
                eng.wait_ge(chunk_used, CH[RW(FIRST_OF[v - 1] + 3)] + 1)

        def counted(eng, name, k, chunk):
            if k < 4:
                eng.wait_ge(s(name), k)
            else:
                eng.wait_ge(chunk_used, chunk + 1)

        def rwkv_scalar(eng, highs, st):
            n, stage = norm_of[st], STAGES.index(st)
            eng.wait_ge(x_ready, 4 * stage)
            eng.wait_ge(S["rms_scale"], 2 * n)
            for m in range(TT):
                nc.scalar.activation(junk[:, m, :], x[:, m, :], ACT.Square, scale=1.0 / 32, accum_out=stat[:, m:m + 1])\
                    .then_inc(S["rms_squares"], 1)
            eng.wait_ge(S["rms_squares"], 2 * (n + 1))
            nc.scalar.activation(stat[:, 2:4], stat[:, 0:2], ACT.Sqrt, bias=stat[:, 63:64]).then_inc(S["rms_root"], 1)
            eng.wait_ge(S["rows_scaled"], 2 * n + 2)
            eng.dma_start(kept_x, x[:, :, :].rearrange("p m d -> p (m d)")).then_inc(s("x_kept"), 16)
            for b in range(4):
                eng.wait_ge(S["turned"], 4 * n + b + 1)
                for k in (2 * b, 2 * b + 1):
                    nc.scalar.activation(ht[:, k, 1:257], psum[:, b, (k % 2) * 256:(k % 2) * 256 + 256], ACT.Copy,
                                         scale=V_AT(NORMS[n], k)).then_inc(S["h_high"], 1)
            highs.upto(L0 + 2)

            def high_variant(v):
                variant_used(eng, v)
                for b in range(4):
                    eng.wait_ge(s("rw_mixed"), 8 * v + 2 * b + 2)
                    nc.scalar.activation(hhi[:, 2 * b:2 * b + 2, :], variant_x[:, 2 * b:2 * b + 2, :], ACT.Copy)\
                        .then_inc(s("rw_xhi"), 1)

            eng.wait_ge(chunk_used, L0)
            for v in range(3):
                high_variant(v)
            eng.wait_ge(s("rw_first"), 2)
            nc.scalar.activation(lw[0:64, 0, :], psum[0:64, 0, 0:256], ACT.Tanh).then_inc(s("rw_lw"), 1)
            nc.scalar.activation(lw[64:128, 0, :], psum[64:128, 0, 256:512], ACT.Copy).then_inc(s("rw_lw"), 1)
            eng.wait_ge(s("rw_lw"), 2)
            nc.scalar.activation(wa_hi, lw[:, 0, :], ACT.Copy).then_inc(s("rw_lwhi"), 1)
            eng.wait_ge(s("rw_first"), 3)
            nc.scalar.activation(lw[:, 1, :], psum[:, 1, 0:256], ACT.Sigmoid).then_inc(S["rw_lw"], 1)
            nc.scalar.activation(lw[0:32, 2, :], psum[0:32, 1, 256:512], ACT.Sigmoid).then_inc(S["rw_lw"], 1)
            eng.wait_ge(S["rw_lw"], 4)
            nc.scalar.activation(gm_hi, lw[:, 1, :], ACT.Copy).then_inc(S["rw_lwhi"], 1)
            nc.scalar.activation(gt_hi[0:32], lw[0:32, 2, :], ACT.Copy).then_inc(S["rw_lwhi"], 1)
            for k in range(8):
                if k % 2 == 0:
                    counted(eng, "rw_second", k // 2 + 1, L1)
                b = (k // 2) % 2
                nc.scalar.activation(sw[:, k, :], bank2(2 + b)[:, k % 2, :], ACT.Sigmoid, bias=V_AT("w0", k)).then_inc(s("rw_sig"), 1)
                nc.scalar.activation(aa[:, k, :], bank2(4 + b)[:, k % 2, :], ACT.Sigmoid, bias=V_AT("a0", k)).then_inc(s("rw_sig"), 1)

            def root(b):
                eng.wait_ge(s("rw_sums"), b + 1)
                nc.scalar.activation(roots[:, 2 * b:2 * b + 2, :], bank2(b), ACT.Sqrt).then_inc(s("rw_root"), 1)

            high_variant(3)
            for j in range(4):
                name = RW(4 + j)
                highs.upto(CH[name] + 2)
                projected(eng, name)
                read(nc.scalar.activation(kx[:, 2 * j:2 * j + 2, :], bank2(proj_bank(name)), ACT.Copy), name)
                highs.upto(CH[name] + 3)
                if j == 0:
                    eng.wait_ge(s("rw_before"), 1)
                    nc.scalar.activation(sw, sw, ACT.Exp, scale=-DECAY).then_inc(s("rw_pm"), 1)
                if j == 3:
                    high_variant(4)
                eng.wait_ge(s("rw_kk"), 2 * j + 2)
                nc.scalar.activation(roots[:, 2 * j:2 * j + 2, :], kk[:, 2 * j:2 * j + 2, :], ACT.Square).then_inc(s("rw_sq"), 1)
                if j >= 2:
                    root(j - 2)
            for j in range(4):
                name = RW(j)
                highs.upto(CH[name] + 2)
                projected(eng, name)
                eng.wait_ge(s("rw_kx"), 4)
                read(nc.scalar.activation(rr[:, 2 * j:2 * j + 2, :], bank2(proj_bank(name)), ACT.Copy), name)
                if j < 2:
                    root(j + 2)
            high_variant(5)
            eng.wait_ge(s("rw_neg"), 1)
            nc.scalar.activation(sw, sums, ACT.Exp, scale=DECAY).then_inc(s("rw_pinv"), 1)
            eng.wait_ge(s("rw_pinv"), 1)
            nc.scalar.activation(sums, sums, ACT.Exp, scale=-DECAY).then_inc(s("rw_p"), 1)
            for j in range(4):
                name = RW(8 + j)
                highs.upto(CH[name] + 2)
                projected(eng, name)
                read(nc.scalar.activation(vt[:, :, j * 256:(j + 1) * 256], bank2(proj_bank(name)), ACT.Copy), name)
            highs.upto(CH[RW(11)] + 3)
            for m in range(2):
                for b in range(4):
                    eng.wait_ge(s("rw_bkturned"), 4 * m + b + 1)
                    nc.scalar.activation(bk[m][:, b // 2, (b % 2) * 512:(b % 2) * 512 + 512], psum[:, 4 * m + b, :], ACT.Copy)\
                        .then_inc(s("rw_bk"), 1)
            eng.wait_ge(s("x_kept"), 16)
            eng.wait_ge(low_made, STREAM_STOPS)

            def copy_r(w, hh):
                eng.wait_ge(s("rw_usum"), 2 * w + hh + 1)
                r = slice(hh * 64, hh * 64 + 64)
                nc.scalar.activation(R7[r], bank4(4)[r], ACT.Copy).then_inc(s("rw_r"), 1)

            def copy_u(w, hh):
                eng.wait_ge(s("rw_u"), 2 * w + hh + 1)
                r = slice(hh * 64, hh * 64 + 64)
                nc.scalar.activation(U7[r], bank4(5)[r], ACT.Copy).then_inc(s("rw_ub"), 1)

            def copy_y(w, hh):
                m, q = PASSES[w]
                eng.wait_ge(s("rw_ysum"), 2 * w + hh + 1)
                r = slice(hh * 64, hh * 64 + 64)
                nc.scalar.activation(Y[r, m, q * 512:(q + 1) * 512], psum[r, 7, :], ACT.Copy).then_inc(s("rw_y"), 1)

            def squares(m):
                eng.wait_ge(s("rw_centred"), m + 1)
                nc.scalar.activation(ysq[:, m, :], Y[:, m, :], ACT.Square).then_inc(s("rw_ysq"), 1)

            def deviation(m):
                eng.wait_ge(s("rw_gvar"), m + 1)
                hs = slice(16 * m, 16 * m + 16)
                nc.scalar.activation(groot[:, hs], gvar[:, hs], ACT.Sqrt, scale=1.0 / 64, bias=stat[:, 59:60])\
                    .then_inc(s("rw_groot"), 1)

            for w in range(5):
                if w:
                    copy_r(w - 1, 0)
                    copy_u(w - 1, 0)
                if w < 4:
                    inverse_scalar(eng, w + inv0["rwkv"], T7)
                if w:
                    copy_y(w - 1, 0)
                    if w == 4:
                        squares(0)
                    copy_r(w - 1, 1)
                    copy_u(w - 1, 1)
                    copy_y(w - 1, 1)
            deviation(0)
            squares(1)
            deviation(1)
            for b in range(4):
                counted(eng, "rw_out", b + 1, L2)
                for k in (2 * b, 2 * b + 1):
                    nc.scalar.activation(yt[:, k, :], bank2(b % 2)[:, k % 2, :], ACT.Identity, scale=V_AT("ln_w", k),
                                         bias=V_AT("ln_b", k)).then_inc(s("rw_yt"), 1)
                if b == 3:
                    eng.dma_start(x[:, :, :].rearrange("p m d -> p (m d)"), kept_x).then_inc(s("x_back"), 16)
                eng.wait_ge(s("rw_gated"), b + 1)
                nc.scalar.activation(hhi[:, 2 * b:2 * b + 2, :], yt[:, 2 * b:2 * b + 2, :], ACT.Copy).then_inc(s("rw_yhi"), 1)
            for j in range(4):
                highs.upto(CH[("rw_o", 0, j)] + 3)

        def rwkv_vector(eng, st):
            n = norm_of[st]
            steps = Steps(eng, "dve_step")
            eng.wait_ge(S["rms_root"], n + 1)
            nc.vector.reciprocal(stat[:, 4:6], stat[:, 2:4]).then_inc(S["rms_scale"], 1)
            eng.wait_ge(S["rms_scale"], 2 * n + 1)
            for m in range(TT):
                nc.vector.tensor_scalar(xn[:, m, :], x[:, m, :], stat[:, 4 + m:5 + m], None, ALU.mult)\
                    .then_inc(S["rows_scaled"], 1)
            steps(nc.vector.memset(ht[:, :, 0:1], 0.0))
            steps(nc.vector.memset(Z, 0.0))
            for b in range(4):
                eng.wait_ge(S["h_high"], 8 * n + 2 * b + 2)
                for k in (2 * b, 2 * b + 1):
                    nc.vector.tensor_tensor(shifted[:, k, :], ht[:, k, 0:256], ht[:, k, 1:257], ALU.subtract)\
                        .then_inc(S["h_low"], 1)
            eng.wait_ge(S["h_low"], 8 * n + 8)
            nc.vector.tensor_copy(stat[:, 6:7], stat[:, 5:6]).then_inc(S["rms_scale"], 1)
            eng.wait_ge(S["rms_scale"], 2 * n + 2)

            def mix_variant(v):
                if v:
                    eng.wait_ge(s("rw_xlo"), 4 * v)
                for k in range(8):
                    mu = VEC_AT["mu"] + 8 * VARIANTS[v] + k
                    nc.vector.scalar_tensor_tensor(out=variant_x[:, k, :], in0=shifted[:, k, :], scalar=vec[:, mu:mu + 1],
                                                   in1=ht[:, k, 1:257], op0=ALU.mult, op1=ALU.add).then_inc(s("rw_mixed"), 1)

            def low_variant(v):
                for b in range(4):
                    eng.wait_ge(s("rw_xhi"), 4 * v + b + 1)
                    k = slice(2 * b, 2 * b + 2)
                    nc.vector.tensor_tensor(hlo[:, k, :], variant_x[:, k, :], hhi[:, k, :].bitcast(F32), ALU.subtract)\
                        .then_inc(s("rw_xlo"), 1)

            for v in range(3):
                mix_variant(v)
                low_variant(v)
            eng.wait_ge(s("rw_lwhi"), 1)
            nc.vector.tensor_tensor(wa_lo, lw[:, 0, :], wa_hi.bitcast(F32), ALU.subtract).then_inc(s("rw_lwlo"), 1)
            mix_variant(3)
            eng.wait_ge(S["rw_lwhi"], 3)
            nc.vector.tensor_tensor(gm_lo, lw[:, 1, :], gm_hi.bitcast(F32), ALU.subtract).then_inc(S["rw_lwlo"], 1)
            nc.vector.tensor_tensor(gt_lo[0:32], lw[0:32, 2, :], gt_hi[0:32].bitcast(F32), ALU.subtract).then_inc(S["rw_lwlo"], 1)
            low_variant(3)
            mix_variant(4)
            eng.wait_ge(s("rw_sig"), 16)
            for k in range(8):
                ins = nc.vector.tensor_tensor_scan(sums[:, k, :], const("restart", TOK), sw[:, k, :], 0.0, ALU.mult, ALU.add)
            steps(ins)
            nc.vector.tensor_tensor(sw, sums, sw, ALU.subtract).then_inc(s("rw_before"), 1)
            for k in range(8):
                ins = nc.vector.tensor_scalar(rr[:, k, :], aa[:, k, :], 1.0, V_AT("k_a", k), ALU.subtract, ALU.mult)
            steps(ins)

            def unit_kk(b):
                eng.wait_ge(s("rw_root"), b + 1)
                k = slice(2 * b, 2 * b + 2)
                steps(nc.vector.tensor_scalar(roots[:, k, :], roots[:, k, :], 1e-12, None, ALU.max))
                steps(nc.vector.reciprocal(roots[:, k, :], roots[:, k, :]))
                steps(nc.vector.tensor_tensor(kk[:, k, :], kk[:, k, :], roots[:, k, :], ALU.mult))

            for j in range(4):
                name = RW(4 + j)
                eng.wait_ge(bank_read[proj_bank(name)], PROJ[name] // 2 + 1)
                for k in (2 * j, 2 * j + 1):
                    nc.vector.tensor_scalar(kk[:, k, :], kx[:, k, :], V_AT("k_k", k), None, ALU.mult).then_inc(s("rw_kk"), 1)
                eng.wait_ge(s("rw_kk"), 2 * j + 2)
                k = slice(2 * j, 2 * j + 2)
                nc.vector.scalar_tensor_tensor(out=kx[:, k, :], in0=rr[:, k, :], scalar=1.0, in1=kx[:, k, :],
                                               op0=ALU.add, op1=ALU.mult).then_inc(s("rw_kx"), 1)
                if j == 2:
                    unit_kk(0)
            low_variant(4)
            mix_variant(5)
            for b in range(1, 4):
                unit_kk(b)
            steps(nc.vector.tensor_tensor(aa, aa, kk, ALU.mult))
            eng.wait_ge(s("rw_pm"), 1)
            nc.vector.scalar_tensor_tensor(out=kk, in0=kk, scalar=-1.0, in1=sw, op0=ALU.mult, op1=ALU.mult).then_inc(s("rw_neg"), 1)
            low_variant(5)
            for j in range(0, 4):
                eng.wait_ge(bank_read[proj_bank(RW(j))], PROJ[RW(j)] // 2 + 1)
            eng.wait_ge(s("rw_kx"), 4)
            eng.wait_ge(s("rw_mixed"), 48)
            for k in range(8):
                nc.vector.scalar_tensor_tensor(out=rk[:, k, :], in0=rr[:, k, :], scalar=V_AT("r_k", k), in1=kx[:, k, :],
                                               op0=ALU.mult, op1=ALU.mult).then_inc(s("rw_rk"), 1)
            eng.wait_ge(s("rw_pinv"), 1)
            steps(nc.vector.tensor_tensor(aa, aa, sw, ALU.mult))
            eng.wait_ge(s("rw_rk"), 8)
            steps(nc.vector.tensor_tensor(kx, kx, sw, ALU.mult))
            eng.wait_ge(s("rw_p"), 1)
            steps(nc.vector.tensor_tensor(rr, rr, sums, ALU.mult))
            steps(nc.vector.tensor_copy(pc, sums.rearrange("p k (c t) -> p k c t", c=4)[:, :, :, 63]))

            def to_tokens(m):
                pcb = pc[:, :, 2 * m:2 * m + 2].rearrange("p k (c a) -> p k c a", a=1).broadcast_to((P, 8, 2, 64))
                for i_, src in enumerate((aa, kx)):
                    nc.vector.tensor_tensor(bkT[m][:, i_, :, :].rearrange("p k (c t) -> p k c t", c=2),
                                            src[:, :, m * P:(m + 1) * P].rearrange("p k (c t) -> p k c t", c=2), pcb, ALU.mult)\
                        .then_inc(s("rw_bkT"), 1)

            to_tokens(0)
            eng.wait_ge(s("rw_bonus_sum"), 1)
            nc.vector.tensor_copy(bonus, psum[:, 4, 0:32]).then_inc(s("rw_bonus"), 1)
            to_tokens(1)

            def masked_scores(w):
                for b in range(8):
                    g, i_, k = b // 4, (b // 2) % 2, slice(2 * (b % 2), 2 * (b % 2) + 2)
                    eng.wait_ge(s("rw_scores"), 8 * w + b + 1)
                    two = lambda name, n: const(name, n).rearrange("p (a n) -> p a n", a=1).broadcast_to((P, 2, n))
                    if i_ == 0:
                        nc.vector.tensor_tensor(LT7[g][:, k, :], bank2(b % 4)[:, :, 0:P], two("before", P), ALU.mult)
                        nc.vector.tensor_tensor(RB[w % 2][g][:, k, :], bank2(b % 4)[:, :, P:2 * P], two("upto", P), ALU.mult)\
                            .then_inc(s("rw_masked"), 1)
                    else:
                        nc.vector.tensor_tensor(AK[w % 2][g][:, k, :, :].rearrange("p a s n -> p a (s n)"), bank2(b % 4),
                                                two("before", 256), ALU.mult).then_inc(s("rw_masked"), 1)
                eng.wait_ge(S["rw_masked"], 8 * w + 8)

            def next_state(w, hh):
                m, q = PASSES[w]
                c, z0, done = 2 * m + hh, z_steps(w, hh), z_steps(w, hh) // 5
                if c == 3:
                    return
                eng.wait_ge(s("rw_zsum"), done + 1)
                if z0:
                    eng.wait_ge(s("rw_z"), z0)
                nc.vector.tensor_tensor(R7, bank4(6), four(const("same64")), ALU.mult).then_inc(s("rw_z"), 1)
                eng.wait_ge(s("rw_z"), z0 + 1)
                eng.wait_ge(s("rw_ysum"), 2 * w + hh + 1)
                for k in range(4):
                    t = 4 * q + k
                    nc.vector.scalar_tensor_tensor(out=Z[:, t, :], in0=Z[:, t, :], scalar=pc[:, t, c:c + 1],
                                                   in1=R7[:, k, :], op0=ALU.mult, op1=ALU.add).then_inc(s("rw_z"), 1)

            over64 = lambda v: v.rearrange("p (h a) -> p h a", a=1).broadcast_to((P, 16, 64))

            def centre(m):
                eng.wait_ge(s("rw_y"), 4 * m + 4)
                y3 = Y[:, m, :].rearrange("p (h d) -> p h d", h=16)
                hs = slice(16 * m, 16 * m + 16)
                steps(nc.vector.tensor_reduce(gsum[:, hs], y3, AX_X, ALU.add))
                steps(nc.vector.tensor_scalar(gmean[:, hs], gsum[:, hs], 1.0 / 64, None, ALU.mult))
                nc.vector.tensor_tensor(y3, y3, over64(gmean[:, hs]), ALU.subtract).then_inc(s("rw_centred"), 1)
                v3 = vt[:, m, :].rearrange("p (h d) -> p h d", h=16)
                nc.vector.tensor_tensor(v3, v3, over64(bonus[:, 16 * m:16 * m + 16]), ALU.mult).then_inc(s("rw_bv"), 1)

            def variance(m):
                eng.wait_ge(s("rw_ysq"), m + 1)
                nc.vector.tensor_reduce(gvar[:, 16 * m:16 * m + 16], ysq[:, m, :].rearrange("p (h d) -> p h d", h=16),
                                        AX_X, ALU.add).then_inc(s("rw_gvar"), 1)

            def normed(m):
                eng.wait_ge(s("rw_groot"), m + 1)
                y3 = Y[:, m, :].rearrange("p (h d) -> p h d", h=16)
                hs = slice(16 * m, 16 * m + 16)
                steps(nc.vector.reciprocal(gscale[:, hs], groot[:, hs]))
                nc.vector.tensor_tensor(y3, y3, over64(gscale[:, hs]), ALU.mult).then_inc(s("rw_yn"), 1)

            eng.wait_ge(low_made, STREAM_STOPS)
            for w in range(4):
                masked_scores(w)
                inverse_start(steps, LT7, TT7[w % 2], ALU.add)
                for n_ in range(len(LEVELS)):
                    inverse_level_vector(eng, w + inv0["rwkv"], n_, T7, TT7[w % 2], X7, ALU.add)
                    if w and n_ == 0:
                        next_state(w - 1, 0)
                    if w and n_ == 3:
                        next_state(w - 1, 1)
            centre(0)
            next_state(3, 0)
            variance(0)
            centre(1)
            normed(0)
            variance(1)
            normed(1)
            for b in range(4):
                k = slice(2 * b, 2 * b + 2)
                eng.wait_ge(s("rw_yt"), 2 * b + 2)
                steps(nc.vector.tensor_tensor(yt[:, k, :], yt[:, k, :], bank2(2 + b % 2), ALU.add))
                nc.vector.tensor_tensor(yt[:, k, :], yt[:, k, :], bank2(4 + b % 2), ALU.mult).then_inc(s("rw_gated"), 1)
            for b in range(4):
                k = slice(2 * b, 2 * b + 2)
                eng.wait_ge(s("rw_yhi"), b + 1)
                nc.vector.tensor_tensor(hlo[:, k, :], yt[:, k, :], hhi[:, k, :].bitcast(F32), ALU.subtract)\
                    .then_inc(s("rw_ylo"), 1)
            eng.wait_ge(s("x_back"), 16)
            add_out(eng, "rw_o")

        def rwkv_tensor(eng, st):
            n = norm_of[st]
            norm_tensor(eng, n)
            eng.wait_ge(low_made, L0 + 1)

            def first(v, bank, half, slot, at, width, stride):
                rows_ = width
                for k in range(KT):
                    if k % 2 == 0:
                        eng.wait_ge(s("rw_xlo"), 4 * v + k // 2 + 1)
                    w = (slice(None), slot, slice(at + k * stride, at + k * stride + width))
                    mm = three_passes(psum[0:rows_, bank, half * 256:half * 256 + 256], whi[w], wlo[w], hhi[:, k, :],
                                      hlo[:, k, :], True, k == 0, k == KT - 1)
                return mm

            first(0, 0, 0, L0 % SPLIT, 0, P, 256).then_inc(s("rw_first"), 1)
            first(1, 0, 1, L0 % SPLIT, 0, P, 256).then_inc(s("rw_first"), 1)
            first(2, 1, 0, L0 % SPLIT, P, P, 256).then_inc(chunk_used, 1)
            eng.wait_ge(low_made, L1 + 1)
            first(2, 1, 1, L1 % SPLIT, D, 32, 32).then_inc(s("rw_first"), 1)
            eng.wait_ge(s("rw_lwlo"), 1)
            for b in range(4):
                if b >= 2:
                    eng.wait_ge(s("rw_sig"), 4 * (b - 1))
                for base, lo_, hi_ in ((2, 0, 64), (4, 64, 128)):
                    for k in (2 * b, 2 * b + 1):
                        w = (slice(lo_, hi_), L1 % SPLIT, slice(k * P, k * P + P))
                        mm = three_passes(bank2(base + b % 2)[:, k % 2, :], whi[w], wlo[w], wa_hi[lo_:hi_], wa_lo[lo_:hi_],
                                          True, True, True)
                mm.then_inc(chunk_used if b == 3 else s("rw_second"), 1)

            def square_sums(b):
                eng.wait_ge(s("rw_sq"), b + 1)
                nc.tensor.matmul(psum[:, b, :], const("same64"), roots[:, 2 * b:2 * b + 2, :], start=True, stop=True)\
                    .then_inc(s("rw_sums"), 1)

            eng.wait_ge(s("rw_xlo"), 4 * 3 + 4)
            for j in range(4):
                project(eng, RW(4 + j), columns_out)
                if j == 0:
                    eng.wait_ge(s("rw_sig"), 16)
                if j:
                    square_sums(j - 1)
            eng.wait_ge(s("rw_xlo"), 4 * 4 + 4)
            for j in range(4):
                project(eng, RW(j), columns_out)
                if j == 0:
                    square_sums(3)
            eng.wait_ge(s("rw_xlo"), 4 * 5 + 4)
            for j in range(4):
                project(eng, RW(8 + j), tokens_out)
                if j == 1:
                    eng.wait_ge(s("rw_rk"), 8)
                    for m in range(2):
                        for k in range(8):
                            mm = nc.tensor.matmul(psum[:, 4, 16 * m + 2 * k:16 * m + 2 * k + 2], rk[:, k, m * P:(m + 1) * P],
                                                  const("same64")[:, 0:P:64], start=True, stop=True)
                    mm.then_inc(s("rw_bonus_sum"), 1)
            eng.wait_ge(s("rw_root"), 4)
            for m in range(2):
                eng.wait_ge(s("rw_bkT"), 2 * m + 2)
                for b in range(4):
                    if m and b == 0:
                        eng.wait_ge(s("rw_bonus"), 1)
                    if m and b >= 2:
                        name = RW(8 + b)
                        eng.wait_ge(bank_read[proj_bank(name)], PROJ[name] // 2 + 1)
                    for k in range(4):
                        mm = nc.tensor.transpose(bank4(4 * m + b)[:, k, :], bkT[m][:, b // 2, 4 * (b % 2) + k, :], const("ident"))
                    mm.then_inc(s("rw_bkturned"), 1)

            def scores(w):
                m, q = PASSES[w]
                tok = slice(m * P, (m + 1) * P)
                if w:
                    eng.wait_ge(INV["inv_updated"], 10 * (w + inv0["rwkv"]))
                for b in range(8):
                    g, src, half = b // 4, (aa, kx)[(b // 2) % 2], b % 2
                    if b >= 4:
                        eng.wait_ge(s("rw_masked"), 8 * w + b - 3)
                    elif w == 0:
                        eng.wait_ge(s("rw_bk"), b + 1)
                    r = slice(64 * g, 64 * g + 64)
                    for k in range(2):
                        t = 4 * q + 2 * half + k
                        mm = nc.tensor.matmul(bank2(b % 4)[:, k, :], src[r, t, tok], ar[r, :, t, tok], start=True, stop=True)
                    mm.then_inc(s("rw_scores"), 1)

            def u_sums(w, hh):
                m, q = PASSES[w]
                r, tok = slice(hh * 64, hh * 64 + 64), slice(m * P + hh * 64, m * P + hh * 64 + 64)
                if w or hh:
                    eng.wait_ge(s("rw_z"), z_steps(w, hh))
                elif w == 0:
                    eng.wait_ge(s("rw_bk"), 8)
                for k in range(4):
                    nc.tensor.matmul(bank4(4)[r, k, :], kk[:, 4 * q + k, tok], Z[:, 4 * q + k, :], start=True, stop=False)
                    for p in range(2):
                        col = (4 * q + k) * P + p * 64
                        mm = nc.tensor.matmul(bank4(4)[r, k, p * 64:p * 64 + 64], AK[w % 2][p][r, k, 0, r], vt[r, m, col:col + 64],
                                              start=False, stop=p == 1)
                mm.then_inc(s("rw_usum"), 1)

            def u_solve(w, hh):
                r = slice(hh * 64, hh * 64 + 64)
                eng.wait_ge(s("rw_r"), 2 * w + hh + 1)
                if hh == 0:
                    eng.wait_ge(INV["inv_updated"], 10 * (w + inv0["rwkv"]) + 10)
                for k in range(4):
                    for p in range(2):
                        mm = nc.tensor.matmul(bank4(5)[r, k, p * 64:p * 64 + 64], TT7[w % 2][p][r, k, r],
                                              R7[r, k, p * 64:p * 64 + 64], start=True, stop=True)
                mm.then_inc(s("rw_u"), 1)

            def state_and_y(w, hh):
                m, q = PASSES[w]
                c, r, tok = 2 * w + hh, slice(hh * 64, hh * 64 + 64), slice(m * P + hh * 64, m * P + hh * 64 + 64)
                eng.wait_ge(s("rw_ub"), c + 1)
                if 2 * m + hh < 3:
                    for k in range(4):
                        t = 4 * q + k
                        nc.tensor.matmul(bank4(6)[:, k, :], bk[m][r, 0, t * P:(t + 1) * P], U7[r, k, :], start=True, stop=False)
                        mm = nc.tensor.matmul(bank4(6)[:, k, :], bk[m][r, 1, t * P:(t + 1) * P], vt[r, m, t * P:(t + 1) * P],
                                              start=False, stop=True)
                    mm.then_inc(s("rw_zsum"), 1)
                if c:
                    eng.wait_ge(s("rw_y"), c)
                for k in range(4):
                    nc.tensor.matmul(bank4(7)[r, k, :], rr[:, 4 * q + k, tok], Z[:, 4 * q + k, :], start=True, stop=False)
                    for p in range(2):
                        col = (4 * q + k) * P + p * 64
                        o = bank4(7)[r, k, p * 64:p * 64 + 64]
                        nc.tensor.matmul(o, AK[w % 2][p][r, k, 1, r], vt[r, m, col:col + 64], start=False, stop=False)
                        mm = nc.tensor.matmul(o, RB[w % 2][p][r, k, r], U7[r, k, p * 64:p * 64 + 64], start=False, stop=p == 1)
                mm.then_inc(s("rw_ysum"), 1)

            for w in range(4):
                u = w + inv0["rwkv"]
                if w:
                    u_sums(w - 1, 0)
                scores(w)
                if w:
                    u_solve(w - 1, 0)
                inverse_turn_tensor(eng, u, TT7[w % 2])
                for n_ in range(len(LEVELS)):
                    inverse_x_tensor(eng, u, n_, LT7, T7)
                    if w and n_ == 0:
                        state_and_y(w - 1, 0)
                    if w and n_ == 2:
                        u_solve(w - 1, 1)
                    if w and n_ == 3:
                        state_and_y(w - 1, 1)
                    inverse_tx_tensor(eng, u, n_, TT7[w % 2], X7)
                    if w and n_ == 1:
                        u_sums(w - 1, 1)
            for hh in range(2):
                u_sums(3, hh)
                u_solve(3, hh)
                state_and_y(3, hh)
            eng.wait_ge(s("rw_yn"), 2)
            eng.wait_ge(s("rw_bv"), 2)
            eng.wait_ge(s("rw_y"), 8)
            eng.wait_ge(low_made, L2 + 1)
            eng.wait_ge(s("rw_lwlo"), 3)
            for b in range(4):
                if b >= 2:
                    eng.wait_ge(s("rw_gated"), b - 1)
                for base, src in ((0, Y), (2, vt)):
                    for k in range(2):
                        for m in range(2):
                            nc.tensor.transpose(psum[:, base + b % 2, k * 256 + m * P:k * 256 + m * P + P],
                                                src[:, m, (2 * b + k) * P:(2 * b + k + 1) * P], const("ident"))
                for k in range(2):
                    o = bank2(4 + b % 2)[:, k, :]
                    at = (2 * b + k) * P
                    w = (slice(None), L2 % SPLIT, slice(at, at + P))
                    three_passes(o, whi[w], wlo[w], gm_hi, gm_lo, True, True, False)
                    w = (slice(0, 32), L2 % SPLIT, slice(D + at, D + at + P))
                    mm = three_passes(o, whi[w], wlo[w], gt_hi[0:32], gt_lo[0:32], True, False, True)
                mm.then_inc(chunk_used if b == 3 else s("rw_out"), 1)
            out_tensor(eng, "rw_o", s("rw_ylo"), 4)

        block = ctx.enter_context(nc.Block())

        @block.sync
        def _(sp):
            sp.dma_start(x[:, :, :], x_in.rearrange("(m p) d -> p m d", p=P)).then_inc(S["x_loaded"], 16)
            sp.dma_start(con[:, :], consts).then_inc(S["const_loaded"], 16)
            sp.dma_start(vec[:, :], vectors).then_inc(S["const_loaded"], 16)
            for c in range(RAW):
                sp.dma_start(raw[:, c, :], stream[c]).then_inc(raw_loaded[c], 16)
            def load(i, r):
                sp.wait_ge(low_made, 3 * i + (r - 2))
                sp.dma_start(raw[:, r, :], stream[bass.ds(3 * i + r, 1), :, :].rearrange("a p n -> p (a n)"))\
                    .then_inc(raw_loaded[r], 16)

            with sp.Fori(1, STREAM_STOPS // RAW) as i:
                for r in range(RAW):
                    load(i, r)
            for r in range(RAW):
                if r == STREAM_STOPS % RAW:
                    sp.wait_ge(s("rw_ysum"), 8)
                load(STREAM_STOPS // RAW, r)
            with sp.Fori(STREAM_STOPS // RAW + 1, NCH // RAW) as i:
                for r in range(RAW):
                    load(i, r)
            for c in range(NCH // RAW * RAW, NCH):
                sp.wait_ge(low_made, c - 2)
                sp.dma_start(raw[:, c % RAW, :], stream[c]).then_inc(raw_loaded[c % RAW], 16)
            sp.wait_ge(x_ready, 4 * len(STAGES))
            sp.dma_start(out.rearrange("(m p) d -> p m d", p=P), x[:, :, :]).then_inc(S["stored"], 16)
            sp.wait_ge(S["stored"], 16)

        @block.gpsimd
        def _(pool):
            def low(c, i=None):
                slot = c % SPLIT
                pool.wait_ge(high_made, c + 1 if i is None else c + 1 + 3 * i)
                nc.gpsimd.tensor_tensor(wlo[:, slot, :], raw[:, c % RAW, :], whi[:, slot, :].bitcast(F32), ALU.subtract)\
                    .then_inc(low_made, 1)
            with pool.Fori(0, NCH // 3) as i:
                for r in range(3):
                    low(r, i)
            for c in range(NCH // 3 * 3, NCH):
                low(c)

        @block.scalar
        def _(act_eng):
            highs = Highs(act_eng)
            highs.upto(2)
            act_eng.wait_ge(S["const_loaded"], 32)
            act_eng.wait_ge(S["eps_ready"], 5)
            for k, st in enumerate(STAGES):
                if st[0] == "ffn":
                    norm_scalar(act_eng, norm_of[st], firsts[k] - 1 if k else None, k)
                    ffn_scalar(act_eng, st[1], highs)
                if st[0] == "mix1":
                    mix1_scalar(act_eng, highs, st)
                if st[0] == "rms":
                    rms_scalar(act_eng, k)
                if st[0] == "fox":
                    fox_scalar(act_eng, highs, st)
                if st[0] == "rwkv":
                    rwkv_scalar(act_eng, highs, st)

        @block.vector
        def _(dve):
            nc.vector.memset(stat[:, 63:64], EPS).then_inc(S["eps_ready"], 1)
            nc.vector.memset(stat[:, 62:63], 1.0).then_inc(S["eps_ready"], 1)
            nc.vector.memset(stat[:, 61:62], P * EPS).then_inc(S["eps_ready"], 1)
            nc.vector.memset(stat[:, 60:61], 64 * EPS).then_inc(S["eps_ready"], 1)
            nc.vector.memset(stat[:, 59:60], 64e-5).then_inc(S["eps_ready"], 1)
            dve.wait_ge(S["x_loaded"], 16)
            dve.wait_ge(S["const_loaded"], 32)
            for st in STAGES:
                if st[0] == "mix1":
                    mix1_vector(dve, st)
                if st[0] == "rms":
                    rms_vector(dve)
                if st[0] == "fox":
                    fox_vector(dve, st)
                if st[0] == "rwkv":
                    rwkv_vector(dve, st)
                if st[0] == "ffn":
                    norm_vector(dve, norm_of[st])
                    ffn_vector(dve, st[1], 0.5 if st[1] < 2 else 1.0)

        @block.tensor
        def _(pe):
            pe.wait_ge(S["const_loaded"], 32)
            for st in STAGES:
                if st[0] == "mix1":
                    mix1_tensor(pe, st)
                if st[0] == "fox":
                    fox_tensor(pe, st)
                if st[0] == "rwkv":
                    rwkv_tensor(pe, st)
                if st[0] == "ffn":
                    norm_tensor(pe, norm_of[st])
                    ffn_tensor(pe, st[1], norm_of[st])


def kernel(**inputs):
    import concourse.bacc as bacc
    from concourse.bass_utils import run_bass_kernel_spmd

    a = {k: np.asarray(v) for k, v in inputs.items()}
    names = stream_plan(STAGES)
    stream = np.stack([lay_out_chunk(n, a) for n in names])
    rows = {"gm_w_s": a["gm_w_s"][0], "gm_ln_g": a["gm_ln_g"][0], "gm_ln_b": a["gm_ln_b"][0],
            "gm_bias": np.repeat(a["gm_b_s"][0].reshape(4, 2, P), 64, axis=1).transpose(1, 0, 2),
            "dn_norm": a["dn_norm"][0], "gates": np.concatenate([a["dn_a_log"][0], a["dn_dt_bias"][0]]),
            "final_norm": a["final_norm"], "pool_w": a["hy_pool_w_2"][0], "f_bias": a["hy_f_bias_2"][0]}
    rows = {k: np.ascontiguousarray(v) for k, v in rows.items()}
    arrays = {"stream": stream, "consts": CONSTS, "vectors": lay_out_vectors(a), "x_in": a["x"].reshape(TOK, D), **rows}
    nc = bacc.Bacc("TRN2", target_bir_lowering=False, num_devices=1)
    h = {k: nc.dram_tensor(k, v.shape, mybir.dt.from_np(v.dtype), kind="ExternalInput").ap() for k, v in arrays.items()}
    out = nc.dram_tensor("out", (TOK, D), F32, kind="ExternalOutput").ap()
    build(nc, h["stream"], h["consts"], h["vectors"], h["x_in"], {k: h[k] for k in rows},
          nc.dram_tensor("kept_x", (P, TT * D), F32, kind="Internal").ap(), out)
    r = run_bass_kernel_spmd(nc, [arrays], core_ids=[0])
    return r.results[0]["out"].reshape(1, TOK, D)
```

```python
from contextlib import ExitStack

import numpy as np

import concourse.bass as bass
from concourse import mybir

P = 128
TOK = 256
TT = TOK // P
D = 1024
KT = D // P
FF = 2816
GROUPS = FF // 256
CHUNK_COLS = 2048
RAW = 3
SPLIT = 3
EPS = 1e-6

F32 = mybir.dt.float32
F32R = mybir.dt.float32r
ALU = mybir.AluOpType
ACT = mybir.ActivationFunctionType
AX_X = mybir.AxisListType.X


def ffn_chunks(f):
    names = [("gate", f, 0), ("up", f, 0)]
    for g in range(1, GROUPS):
        names += [("gate", f, g), ("up", f, g), ("down", f, g - 1)]
    return names + [("down", f, GROUPS - 1)]


def stream_plan(stages):
    names = []
    for s in stages:
        if s[0] == "ffn":
            names += ffn_chunks(s[1])
        if s[0] == "mix1":
            names += [("w_in", 0, j) for j in MIX1_ORDER] + [("w_out", 0, j) for j in range(4)]
        if s[0] == "fox":
            names += [("hy_w_in", 0, j) for j in FOX_ORDER] + [("hy_w_out", 0, j) for j in range(4)]
        if s[0] == "rwkv":
            names += RWKV_ORDER
    return names


MIX1_ORDER = [6, 12, 7, 4, 5, 8, 9, 2, 3, 0, 1, 10, 11]
FOX_ORDER = [0, 8, 1, 2, 3, 4, 5, 9, 10, 6, 7]
RWKV_ORDER = [("lora", 0, 0), ("lora", 0, 1)] + [("rw", 0, j) for j in (4, 5, 6, 7, 0, 1, 2, 3, 8, 9, 10, 11)] + \
    [("lora", 0, 2)] + \
    [("rw_o", 0, j) for j in range(4)]
STAGES = [("ffn", 0), ("mix1", 0), ("ffn", 1), ("rms", 0), ("fox", 0), ("ffn", 2), ("rwkv", 0), ("ffn", 3)]


def col_chunk(w, c0, n=256):
    part = w[:, c0:c0 + n]
    if part.shape[1] < 256:
        part = np.concatenate([part, np.zeros((w.shape[0], 256 - part.shape[1]), w.dtype)], 1)
    return part.reshape(KT, P, 256).transpose(1, 0, 2).reshape(P, CHUNK_COLS)


def row_chunk(w, g):
    return w[g * 256:(g + 1) * 256].reshape(2, P, D).transpose(1, 0, 2).reshape(P, CHUNK_COLS)


def lay_out_chunk(name, a):
    kind, f, j = name
    ffn = {0: ("ffn1_w_gate", "ffn1_w_up", "ffn1_w_down", 0), 1: ("ffn2_w_gate", "ffn2_w_up", "ffn2_w_down", 0),
           2: ("ffn_w_gate_2", "ffn_w_up_2", "ffn_w_down_2", 0), 3: ("ffn_w_gate_2", "ffn_w_up_2", "ffn_w_down_2", 1)}
    if kind in ("gate", "up", "down"):
        w = a[ffn[f][("gate", "up", "down").index(kind)]][ffn[f][3]]
        return row_chunk(w, j) if kind == "down" else col_chunk(w, j * 256)
    if kind == "rw":
        return col_chunk(a[("rw_w_r_2", "rw_w_k_2", "rw_w_v_2")[j // 4]][0], (j % 4) * 256)
    if kind == "rw_o":
        return col_chunk(a["rw_w_o_2"][0], j * 256)
    if kind == "lora":
        g1, g2 = a["rw_g1_2"][0], a["rw_g2_2"][0]
        if j == 0:
            return col_chunk(np.concatenate([a["rw_w1_2"][0], a["rw_a1_2"][0], g1[:, :P]], 1), 0)
        if j == 1:
            tail = g1[:, P:].reshape(KT, P, 32).transpose(1, 0, 2).reshape(P, 256)
            top = np.concatenate([a["rw_w2_2"][0], a["rw_a2_2"][0]], 0)
            return np.concatenate([top, tail, np.zeros((P, 768), g1.dtype)], 1)
        return np.concatenate([g2[:P], np.concatenate([g2[P:], np.zeros((96, D), g2.dtype)], 0)], 1)
    if kind == "hy_w_in":
        return col_chunk(a["hy_w_in_2"][0], *{8: (2048, 8), 9: (2056,), 10: (2312,)}.get(j, (j * 256,)))
    return col_chunk(a[{"w_in": "w_in", "w_out": "w_out", "hy_w_in": "hy_w_in_2", "hy_w_out": "hy_w_out_2"}[kind]][0], j * 256)


def shape_constants():
    i = np.arange(P)[None, :]
    j = np.arange(P)[:, None]
    same = (i // 64) == (j // 64)
    parts = {
        "ident": i == j,
        "before": (j < i) & same,
        "upto": (j <= i) & same,
        "neg_upto": -1.0 * ((j <= i) & same),
        "after": (j > i) & same,
        "chunk0": (j < 64) & (i >= 0),
        "chunk1": (j >= 64) & (i >= 0),
        "upto_all": j <= i,
        "ones": (i >= 0) & (j >= 0),
        "same64": same,
        "gm_mask": ~((j >= 64) & (i < 64)),
    }
    parts["level1"] = (i // 2 == j // 2) & (i % 2 == 1) & (j % 2 == 0)
    for s in (2, 4, 8, 16, 32):
        parts[f"level{s}"] = (i // (2 * s) == j // (2 * s)) & ((j // s) % 2 == 1) & ((i // s) % 2 == 0)
    cols, at = [], {}
    n = 0
    for name, m in parts.items():
        at[name] = n
        cols.append(np.asarray(m).astype(np.float32))
        n += P
    at["zero_causal"] = n
    n += P
    at["causal"] = n
    cols.append(np.zeros((P, P), np.float32))
    cols.append(np.where(i > j, np.float32(-1e30), np.float32(0)).astype(np.float32))
    n += P
    at["pool"] = n
    t = np.arange(16)
    pool = np.concatenate([1.0 / np.minimum(t + 1, w) for w in (2, 4, 8, 16)]).astype(np.float32)
    cols.append(np.broadcast_to(pool, (P, 64)))
    n += 64
    at["restart"] = n
    cols.append(np.broadcast_to((np.arange(TOK) % 64 != 0).astype(np.float32), (P, TOK)))
    n += TOK
    return np.ascontiguousarray(np.concatenate(cols, 1)), at


CONSTS, CONST_AT = shape_constants()

VEC = [("ffn1_norm", 8), ("mix_norm", 8), ("ffn2_norm", 8), ("mix_norm_2a", 8), ("ffn_norm_2a", 8),
       ("mix_norm_2b", 8), ("ffn_norm_2b", 8), ("conv", 48), ("pool_scale", 4), ("q_gain", 1), ("k_gain", 1),
       ("mu", 48), ("w0", 8), ("a0", 8), ("k_k", 8), ("k_a", 8), ("r_k", 8), ("ln_w", 8), ("ln_b", 8)]
VEC_AT = {}
_n = 0
for _name, _w in VEC:
    VEC_AT[_name] = _n
    _n += _w
VEC_COLS = _n


def lay_out_vectors(a):
    cm = lambda v: v.reshape(-1, P).T
    twice = lambda v: np.concatenate([v, v]).reshape(1, P).T
    parts = [cm(a["ffn1_norm"][0]), cm(a["mix_norm"][0]), cm(a["ffn2_norm"][0]), cm(a["mix_norm_2"][0]),
             cm(a["ffn_norm_2"][0]), cm(a["mix_norm_2"][1]), cm(a["ffn_norm_2"][1]),
             np.concatenate([cm(a["dn_conv_w"][0, k]) for k in range(4)], 1),
             cm(a["hy_pool_scale_2"][0]), twice(a["hy_q_gain_2"][0]), twice(a["hy_k_gain_2"][0]),
             np.concatenate([cm(a["rw_mu_2"][0, k]) for k in range(6)], 1),
             cm(a["rw_w0_2"][0]), cm(a["rw_a0_2"][0]), cm(a["rw_k_k_2"][0]), cm(a["rw_k_a_2"][0]),
             cm(a["rw_r_k_2"][0]), cm(a["rw_ln_w_2"][0]), cm(a["rw_ln_b_2"][0])]
    return np.ascontiguousarray(np.concatenate(parts, 1))


def build(nc, stream, consts, vectors, x_in, rows, kept_x, out):
    names = stream_plan(STAGES)
    CH = {name: c for c, name in enumerate(names)}
    NCH = len(names)
    ctx = ExitStack()
    with ctx:
        def sb(name, shape, dt=F32):
            return ctx.enter_context(nc.sbuf_tensor(name, shape, dt))

        def sem(name):
            return ctx.enter_context(nc.semaphore(name))

        raw = sb("raw", [P, RAW, CHUNK_COLS])
        whi = sb("whi", [P, SPLIT, CHUNK_COLS], F32R)
        wlo = sb("wlo", [P, SPLIT, CHUNK_COLS], F32R)
        hhi = sb("hhi", [P, KT, TOK], F32R)
        hlo = sb("hlo", [P, KT, TOK], F32R)
        ahi = sb("ahi", [P, 2, 2, TOK], F32R)
        alo = sb("alo", [P, 2, 2, TOK], F32R)
        x = sb("x", [P, TT, D])
        con = sb("con", [P, CONSTS.shape[1]])
        vec = sb("vec", [P, VEC_COLS])
        stat = sb("stat", [P, 64])
        ARENA = 23360
        arena = sb("arena", [P, ARENA])
        psum = ctx.enter_context(nc.psum_tensor("psum", [P, 8, 512], F32))

        def const(name, n=P):
            return con[:, CONST_AT[name]:CONST_AT[name] + n]

        def area(at, *shape):
            n = int(np.prod(shape))
            assert at + n <= ARENA, (at, shape)
            v = arena[:, at:at + n]
            if len(shape) == 2:
                v = v.rearrange("p (a b) -> p a b", a=shape[0])
            if len(shape) == 3:
                v = v.rearrange("p (a b c) -> p a b c", a=shape[0], b=shape[1])
            return v

        xn = area(0, TT, D)
        junk = area(2048, TT, D)
        sg = area(4096, 2, 512)
        act = area(5120, 2, 512)

        S = {}

        def s(name):
            if name not in S:
                S[name] = sem(name)
            return S[name]

        raw_loaded = [sem(f"raw_loaded{i}") for i in range(RAW)]
        for n in ("high_made", "low_made", "chunk_used", "const_loaded", "x_loaded", "stored",
                  "x_ready", "rms_squares", "rms_root", "rms_scale", "rows_scaled", "turned", "h_high", "h_low",
                  "act_step", "dve_step", "eps_ready"):
            s(n)
        x_ready = S["x_ready"]
        high_made, low_made, chunk_used = S["high_made"], S["low_made"], S["chunk_used"]

        STEPS_DONE = {}

        class Steps:

            def __init__(self, eng, name):
                self.eng, self.sem, self.n = eng, s(name), STEPS_DONE.get(name, 0)
                self.name = name

            def __call__(self, ins):
                ins.then_inc(self.sem, 1)
                self.n += 1
                STEPS_DONE[self.name] = self.n
                self.eng.wait_ge(self.sem, self.n)

        def high(eng, c, i=None):
            loaded, used, slot = 16 * (c // RAW + 1), c - SPLIT + 1, c % SPLIT
            eng.wait_ge(raw_loaded[c % RAW], loaded if i is None else loaded + 32 * i)
            if used > 0:
                eng.wait_ge(chunk_used, used if i is None else used + 6 * i)
            nc.scalar.activation(whi[:, slot, :], raw[:, c % RAW, :], ACT.Copy).then_inc(high_made, 1)

        x_base = {}
        for stage_, st_ in enumerate(STAGES):
            kind_ = {"mix1": "w_out", "fox": "hy_w_out", "rwkv": "rw_o"}.get(st_[0])
            if kind_:
                x_base[kind_] = 4 * stage_

        norm_of = {st_: n_ for n_, st_ in enumerate([st_ for st_ in STAGES if st_[0] != "rms"])}

        class Highs:

            def __init__(self, eng):
                self.eng, self.next = eng, 0

            def upto(self, c):
                while self.next <= min(c, NCH - 1):
                    high(self.eng, self.next)
                    self.next += 1

        def three_passes(out, w_hi, w_lo, h_hi, h_lo, weights_stand, start, stop):
            if weights_stand:
                nc.tensor.matmul(out, w_hi, h_hi, start=start, stop=False)
                nc.tensor.matmul(out, w_hi, h_lo, start=False, stop=False)
                return nc.tensor.matmul(out, w_lo, h_hi, start=False, stop=stop)
            nc.tensor.matmul(out, h_hi, w_hi, start=start, stop=False)
            nc.tensor.matmul(out, h_hi, w_lo, start=False, stop=False)
            return nc.tensor.matmul(out, h_lo, w_hi, start=False, stop=stop)

        def columns_out(slot, bank, hi=hhi, lo=hlo, halves=(0, 1), wait=None, used=None):
            for j in halves:
                for k in range(KT):
                    if wait and j == 0:
                        wait(k)
                    w = (slice(None), slot, slice(k * 256 + j * P, k * 256 + j * P + P))
                    mm = three_passes(psum[:, bank, j * 256:(j + 1) * 256], whi[w], wlo[w], hi[:, k, :], lo[:, k, :],
                                      True, k == 0, k == KT - 1)
                    if used and j == 1 and k % 2 and k < KT - 1:
                        mm.then_inc(used, 1)
            return mm

        def tokens_out(slot, bank, hi=hhi, lo=hlo, n=256, halves=(0, 1), order=range(KT), wait=None):
            for m in halves:
                for k in order:
                    if wait and m == 0:
                        wait(k)
                    w = (slice(None), slot, slice(k * 256, k * 256 + n))
                    t = (slice(None), k, slice(m * P, m * P + P))
                    mm = three_passes(psum[:, bank, m * 256:m * 256 + n], whi[w], wlo[w], hi[t], lo[t],
                                      False, k == order[0], k == order[-1])
            return mm

        NORM_BANK = {n_: 4 if st_[0] == "ffn" else 0 for st_, n_ in norm_of.items()}
        NORMS = ["ffn1_norm", "mix_norm", "ffn2_norm", "mix_norm_2a", "ffn_norm_2a", "mix_norm_2b", "ffn_norm_2b"]

        def pieces(stage):
            if stage and STAGES[stage - 1][0] in ("mix1", "fox", "rwkv"):
                return [[(m, slice(j * 256, j * 256 + 256)) for m in range(TT)] for j in range(4)]
            return [[(m, slice(half * 512, half * 512 + 512))] for m in range(TT) for half in range(2)]

        SQUARES, SUMS = {}, {}
        for stage_, st_ in enumerate(STAGES):
            if st_[0] != "rms":
                n_ = norm_of[st_]
                ops = sum(len(part) for part in pieces(stage_))
                SQUARES[n_] = SQUARES.get(n_ - 1, 0) + ops
                SUMS[n_] = ops // TT

        def mean_squares(eng, n, stage):
            nc.scalar.activation(stat[:, 40 + n:41 + n], stat[:, 63:64], ACT.Sqrt)
            if n == 0:
                eng.wait_ge(S["x_loaded"], 16)
            else:
                eng.wait_ge(S["rms_scale"], 3 * n)
            at = [16, 20]
            for i, part in enumerate(pieces(stage)):
                if n:
                    eng.wait_ge(x_ready, 4 * (stage - 1) + i + 1)
                for m, cols in part:
                    nc.scalar.activation(junk[:, m, cols], x[:, m, cols], ACT.Square, scale=1.0 / 32,
                                         accum_out=stat[:, at[m]:at[m] + 1]).then_inc(S["rms_squares"], 1)
                    at[m] += 1
            eng.wait_ge(S["rms_scale"], 3 * n + 1)
            nc.scalar.activation(stat[:, 2:4], stat[:, 0:2], ACT.Sqrt, bias=stat[:, 63:64]).then_inc(S["rms_root"], 1)

        def scaled_rows(eng, n):
            eng.wait_ge(S["rms_squares"], SQUARES[n])
            nc.vector.tensor_reduce(stat[:, 0:2], stat[:, 16:24].rearrange("p (m i) -> p m i", m=2)[:, :, 0:SUMS[n]],
                                    AX_X, ALU.add).then_inc(S["rms_scale"], 1)
            eng.wait_ge(S["rms_root"], n + 1)
            nc.vector.reciprocal(stat[:, 4:6], stat[:, 2:4]).then_inc(S["rms_scale"], 1)
            eng.wait_ge(S["rms_scale"], 3 * n + 2)
            for m in range(TT):
                nc.vector.tensor_scalar(xn[:, m, :], x[:, m, :], stat[:, 4 + m:5 + m], None, ALU.mult)\
                    .then_inc(S["rows_scaled"], 1)

        def norm_scalar(eng, n, last_use, stage, highs=None, load=None):
            mean_squares(eng, n, stage)
            if load:
                load()
            if n == 0:
                highs.upto(1)
            if last_use is not None:
                eng.wait_ge(chunk_used, last_use + 1)
            gain = VEC_AT[NORMS[n]]
            for b in range(4):
                eng.wait_ge(S["turned"], 4 * n + b + 1)
                for k in (2 * b, 2 * b + 1):
                    nc.scalar.activation(hhi[:, k, :], bank2(NORM_BANK[n] + b)[:, k % 2, :], ACT.Copy,
                                         scale=vec[:, gain + k:gain + k + 1]).then_inc(S["h_high"], 1)

        def norm_vector(eng, n):
            scaled_rows(eng, n)
            gain = VEC_AT[NORMS[n]]
            for b in range(4):
                for k in (2 * b, 2 * b + 1):
                    eng.wait_ge(S["h_high"], 8 * n + 2 * b + 2)
                    ins = nc.vector.scalar_tensor_tensor(
                        out=hlo[:, k, :], in0=bank2(NORM_BANK[n] + b)[:, k % 2, :],
                        scalar=vec[:, gain + k:gain + k + 1], in1=hhi[:, k, :].bitcast(F32),
                        op0=ALU.mult, op1=ALU.subtract)
                    ins.then_inc(S["h_low"], 1)
            eng.wait_ge(S["h_low"], 8 * n + 8)
            nc.vector.tensor_copy(stat[:, 6:7], stat[:, 5:6]).then_inc(S["rms_scale"], 1)

        def norm_tensor(eng, n):
            if n:
                eng.wait_ge(S["h_low"], 8 * n)
            for b in range(4):
                for k in (2 * b, 2 * b + 1):
                    for m in range(TT):
                        eng.wait_ge(S["rows_scaled"], 2 * n + m + 1)
                        at = (k % 2) * 256 + m * P
                        mm = nc.tensor.transpose(psum[:, NORM_BANK[n] + b, at:at + P], xn[:, m, k * P:(k + 1) * P],
                                                 const("ident"))
                mm.then_inc(S["turned"], 1)

        def ffn_tensor(eng, f, n):
            product, act_low = s("ffn_product"), s("ffn_act_low")
            c0 = CH[("gate", f, 0)]

            def step(kind, c, g, start=False, stop=False, i=None, wait=None):
                b, slot, more = g % 2, c % SPLIT, lambda v, k: v if i is None else v + k * i
                eng.wait_ge(low_made, more(c + 1, 6))
                if kind == "gate":
                    if g >= 2:
                        eng.wait_ge(product, GROUPS * f + more(g - 1, 2))
                    columns_out(slot, b, wait=wait).then_inc(chunk_used, 1)
                if kind == "up":
                    columns_out(slot, 2 + b).then_inc(chunk_used, 1)
                if kind == "down":
                    eng.wait_ge(act_low, GROUPS * f + more(g + 1, 2))
                    for m in range(TT):
                        for half in range(2):
                            for j in range(2):
                                t = (slice(None), b, j, slice(m * P, m * P + P))
                                w = (slice(None), slot, slice(j * D + half * 512, j * D + half * 512 + 512))
                                mm = three_passes(psum[:, 4 + 2 * m + half, :], whi[w], wlo[w], ahi[t], alo[t],
                                                  False, start and j == 0, stop and j == 1)
                            if stop and (m, half) != (1, 1):
                                mm.then_inc(s("ffn_out"), 1)
                    mm.then_inc(chunk_used, 1)

            def group(c, g, start=False, i=None):
                step("gate", c, g, i=i)
                step("up", c + 1, g, i=i)
                step("down", c + 2, g - 1, start=start, i=i)

            step("gate", c0, 0, wait=lambda k: eng.wait_ge(S["h_low"], 8 * n + k + 1))
            step("up", c0 + 1, 0)
            group(c0 + 2, 1, start=True)
            group(c0 + 5, 2)
            with eng.Fori(0, (GROUPS - 3) // 2) as i:
                group(c0 + 8, 3, i=i)
                group(c0 + 11, 4, i=i)
            step("down", c0 + 32, GROUPS - 1, stop=True)

        def ffn_scalar(eng, f, highs):
            silu_done, act_high, product = s("ffn_silu_done"), s("ffn_act_high"), s("ffn_product")
            c0 = CH[("gate", f, 0)]

            def silu(c, g, i=None):
                more = lambda v, k: v if i is None else v + k * i
                eng.wait_ge(chunk_used, more(c + 1, 6))
                if g >= 2:
                    eng.wait_ge(product, GROUPS * f + more(g - 1, 2))
                nc.scalar.activation(sg[:, g % 2, :], psum[:, g % 2, :], ACT.Silu).then_inc(silu_done, 1)

            def act_highs(c, g, i=None):
                more = lambda v, k: v if i is None else v + k * i
                eng.wait_ge(product, GROUPS * f + more(g + 1, 2))
                if g >= 2:
                    eng.wait_ge(chunk_used, more(c, 6))
                b = g % 2
                nc.scalar.activation(ahi[:, b, :, :], act[:, b, :].rearrange("p (a b) -> p a b", a=2), ACT.Copy)\
                    .then_inc(act_high, 1)

            def group(c, g, i=None):
                if i is None:
                    highs.upto(c + 3)
                else:
                    high(eng, c + 3, i)
                silu(c, g, i)
                if i is None:
                    highs.upto(c + 4)
                else:
                    high(eng, c + 4, i)
                act_highs(c, g, i)
                if i is None:
                    highs.upto(c + 5)
                else:
                    high(eng, c + 5, i)

            highs.upto(c0 + 2)
            silu(c0, 0)
            highs.upto(c0 + 3)
            act_highs(c0, 0)
            highs.upto(c0 + 4)
            group(c0 + 2, 1)
            group(c0 + 5, 2)
            with eng.Fori(0, (GROUPS - 5) // 2) as i:
                group(c0 + 8, 3, i)
                group(c0 + 11, 4, i)
            highs.next = c0 + 8 + 3 * (GROUPS - 5) + 3
            group(c0 + 26, 9)
            group(c0 + 29, 10)

        def ffn_vector(eng, f, factor):
            silu_done, act_high, act_low = s("ffn_silu_done"), s("ffn_act_high"), s("ffn_act_low")
            product = s("ffn_product")
            c0 = CH[("gate", f, 0)]

            def group(c, g, i=None):
                more = lambda v, k: v if i is None else v + k * i
                b = g % 2
                eng.wait_ge(silu_done, GROUPS * f + more(g + 1, 2))
                eng.wait_ge(chunk_used, more(c + 2, 6))
                if g >= 2:
                    eng.wait_ge(act_low, GROUPS * f + more(g - 1, 2))
                nc.vector.tensor_tensor(act[:, b, :], sg[:, b, :], psum[:, 2 + b, :], ALU.mult).then_inc(product, 1)
                eng.wait_ge(act_high, GROUPS * f + more(g + 1, 2))
                flat = lambda t: t[:, b, :, :].rearrange("p a b -> p (a b)")
                nc.vector.tensor_tensor(flat(alo), act[:, b, :], flat(ahi).bitcast(F32), ALU.subtract)\
                    .then_inc(act_low, 1)

            group(c0, 0)
            group(c0 + 2, 1)
            group(c0 + 5, 2)
            with eng.Fori(0, (GROUPS - 3) // 2) as i:
                group(c0 + 8, 3, i)
                group(c0 + 11, 4, i)
            for m in range(TT):
                for half in range(2):
                    if (m, half) == (1, 1):
                        eng.wait_ge(chunk_used, c0 + 33)
                    else:
                        eng.wait_ge(s("ffn_out"), 3 * f + 2 * m + half + 1)
                    xs = x[:, m, half * 512:half * 512 + 512]
                    nc.vector.scalar_tensor_tensor(out=xs, in0=psum[:, 4 + 2 * m + half, :], scalar=factor, in1=xs,
                                                   op0=ALU.mult, op1=ALU.add).then_inc(x_ready, 1)

        LEVELS = (2, 4, 8, 16, 32)
        for n_ in ("inv_start", "inv_turned", "inv_copied", "inv_x", "inv_masked", "inv_summed", "inv_updated"):
            s(n_)
        INV = {k: S[k] for k in S if k.startswith("inv_")}

        def inverse_start(steps, LT, TTr, op):
            for g in range(2):
                steps(nc.vector.tensor_tensor(TTr[g], LT[g], four(const("level1")), ALU.mult))
                nc.vector.tensor_tensor(TTr[g], four(const("ident")), TTr[g], op).then_inc(INV["inv_start"], 1)

        def inverse_level_vector(eng, u, n, T, TTr, X, op):
            for g in range(2):
                eng.wait_ge(INV["inv_x"], 10 * u + 2 * n + g + 1)
                nc.vector.tensor_tensor(X[g], bank4(2 * g), four(const(f"level{LEVELS[n]}")), ALU.mult)\
                    .then_inc(INV["inv_masked"], 1)
            for g in range(2):
                eng.wait_ge(INV["inv_summed"], 10 * u + 2 * n + g + 1)
                if n < len(LEVELS) - 1:
                    nc.vector.tensor_tensor(T[g], T[g], bank4(2 * g), op)
                nc.vector.tensor_tensor(TTr[g], TTr[g], bank4(2 * g + 1), op).then_inc(INV["inv_updated"], 1)

        def inverse_scalar(eng, u, T):
            for g in range(2):
                eng.wait_ge(INV["inv_turned"], 2 * u + g + 1)
                nc.scalar.activation(T[g], bank4(2 * g), ACT.Copy).then_inc(INV["inv_copied"], 1)

        def inverse_turn_tensor(eng, u, TTr):
            for g in range(2):
                eng.wait_ge(INV["inv_start"], 2 * u + g + 1)
                for h in range(4):
                    mm = nc.tensor.transpose(bank4(2 * g)[:, h, :], TTr[g][:, h, :], const("ident"))
                mm.then_inc(INV["inv_turned"], 1)

        def inverse_x_tensor(eng, u, n, LT, T):
            for g in range(2):
                if n:
                    eng.wait_ge(INV["inv_updated"], 10 * u + 2 * (n - 1) + g + 1)
                else:
                    eng.wait_ge(INV["inv_copied"], 2 * u + g + 1)
                for h in range(4):
                    mm = nc.tensor.matmul(bank4(2 * g)[:, h, :], LT[g][:, h, :], T[g][:, h, :], start=True, stop=True)
                mm.then_inc(INV["inv_x"], 1)

        def inverse_tx_tensor(eng, u, n, TTr, X):
            for g in range(2):
                eng.wait_ge(INV["inv_masked"], 10 * u + 2 * n + g + 1)
                if n < len(LEVELS) - 1:
                    for h in range(4):
                        nc.tensor.matmul(bank4(2 * g)[:, h, :], TTr[g][:, h, :], X[g][:, h, :], start=True, stop=True)
                for h in range(4):
                    mm = nc.tensor.matmul(bank4(2 * g + 1)[:, h, :], X[g][:, h, :], TTr[g][:, h, :], start=True, stop=True)
                mm.then_inc(INV["inv_summed"], 1)

        def four(m):
            return m.rearrange("p (a n) -> p a n", a=1).broadcast_to((P, 4, m.shape[1]))

        def bank4(b):
            return psum[:, b, :].rearrange("p (a n) -> p a n", a=4)

        def bank2(b):
            return psum[:, b, :].rearrange("p (a n) -> p a n", a=2)

        bank_read = {6: s("bank_read6"), 7: s("bank_read7")}
        PROJ = {}
        inv0 = {"rwkv": 1 if ("mix1", 0) in STAGES else 0}
        for name_ in names:
            if name_[0] in ("w_in", "hy_w_in", "rw"):
                PROJ[name_] = len(PROJ)

        def proj_bank(name):
            return 6 + PROJ[name] % 2

        def project(eng, name, form, **kw):
            c, q = CH[name], PROJ[name]
            eng.wait_ge(low_made, c + 1)
            if q >= 2:
                eng.wait_ge(bank_read[6 + q % 2], q // 2)
            form(c % SPLIT, 6 + q % 2, **kw).then_inc(chunk_used, 1)

        def project_half(eng, name, form, half):
            c, q = CH[name], PROJ[name]
            if half == 0:
                eng.wait_ge(low_made, c + 1)
                eng.wait_ge(bank_read[6 + q % 2], q // 2)
            mm = form(c % SPLIT, 6 + q % 2, halves=(half,))
            if half == 1:
                mm.then_inc(chunk_used, 1)

        def projected(eng, name):
            eng.wait_ge(chunk_used, CH[name] + 1)

        def read(ins, name):
            return ins.then_inc(bank_read[proj_bank(name)], 1)

        def add_out(eng, kind):
            for j in range(4):
                name = (kind, 0, j)
                projected(eng, name)
                xs = x[:, :, j * 256:(j + 1) * 256]
                nc.vector.tensor_tensor(xs, xs, bank2(6 + j % 2), ALU.add).then_inc(x_ready, 1)

        def out_tensor(eng, kind, ready, order):
            for j in range(4):
                c = CH[(kind, 0, j)]
                eng.wait_ge(low_made, c + 1)
                if j < 2:
                    eng.wait_ge(bank_read[6 + j], sum(1 for n_, q_ in PROJ.items() if CH[n_] < c and q_ % 2 == j))
                else:
                    eng.wait_ge(x_ready, x_base[kind] + j - 1)
                wait = (lambda k: eng.wait_ge(ready, order[k])) if j == 0 else None
                tokens_out(c % SPLIT, 6 + j % 2, order=list(order), wait=wait).then_inc(chunk_used, 1)

        cin = area(0, 12, 260)
        sq = area(3120, 8, 256)
        rs = area(5168, 8, 256)
        Dm = [area(0 + 512 * g, 4, P) for g in range(2)]
        LTm = [area(1024 + 512 * g, 4, P) for g in range(2)]
        ATm = [area(2048 + 512 * g, 4, P) for g in range(2)]
        Tm = [area(3072 + 512 * g, 4, P) for g in range(2)]
        TTm = [area(4096 + 512 * g, 4, P) for g in range(2)]
        Xm = [area(5120 + 512 * g, 4, P) for g in range(2)]
        ngB = [area(21296 + 512 * g, 4, P) for g in range(2)]
        qkv = area(7216, 12, 256)
        ktok = area(10288, 2, 512)
        vtok = area(11312, 2, 512)
        zg = area(12336, 2, 512)
        va = area(13360, 2, 512)
        yraw = area(14384, 4, 256)
        wsT = area(15408, 8, P)
        ws = area(16432, 8, P)
        Om = area(16432, 2, 512)
        lnp = area(17456, 2, 512)
        gbias = area(18480, 4, P)
        sm = area(18992, 256)
        Rm = area(19248, 4, P)
        Wb = area(19760, 2, 512)
        Sm = area(20784, 4, P)
        OQ = area(21296, 4, P)
        osq = area(21808, 2, 512)
        dnn = area(22832, P)
        alog = area(22960, 8)

        ba_y, ba_abs, ba_beta, ba_g, ba_l = (sm[:, 8 * k:8 * k + 8] for k in range(5))
        ex = sm[:, 40:72].rearrange("p (m k h) -> p m k h", m=2, k=4)
        neg_eg = sm[:, 72:80]
        bd = sm[:, 80:88]
        lnst = sm[:, 96:108]
        mv = sm[:, 108:112]
        lnr = sm[:, 112:116]
        osum = sm[:, 120:128]
        ort = sm[:, 128:136]
        orr = sm[:, 136:144]
        ealog = sm[:, 144:148]
        spl = sm[:, 152:160]
        mh = lambda v: v.rearrange("p (m h) -> p m h", m=2)
        KV_BANKS = (2, 3, 4, 0)
        DLOG_BANKS = (1, 5)
        QKV = {6: 4, 7: 6, 4: 0, 5: 2, 8: 8, 9: 10}

        def mix1_scalar(eng, highs, st):
            n, stage = norm_of[st], STAGES.index(st)
            def load():
                eng.dma_start(ws, rows["gm_w_s"].rearrange("g i j -> i g j")).then_inc(s("m1_loaded"), 16)
                eng.dma_start(lnp[:, 0, :], rows["gm_ln_g"].partition_broadcast(P)).then_inc(s("m1_loaded"), 16)
                eng.dma_start(lnp[:, 1, :], rows["gm_ln_b"].partition_broadcast(P)).then_inc(s("m1_loaded"), 16)
                eng.dma_start(gbias, rows["gm_bias"]).then_inc(s("m1_loaded"), 16)
                eng.dma_start(dnn, rows["dn_norm"].partition_broadcast(P)).then_inc(s("m1_loaded"), 16)
                eng.dma_start(alog, rows["gates"].partition_broadcast(P)).then_inc(s("m1_loaded"), 16)

            norm_scalar(eng, n, CH[("w_in", 0, 6)] - 1, stage, load=load)
            highs.upto(CH[("w_in", 0, 12)] + 2)
            steps = Steps(eng, "act_step")
            projected(eng, ("w_in", 0, 12))
            eng.wait_ge(s("m1_y"), 1)
            read(nc.scalar.activation(mh(ba_beta), bank2(proj_bank(("w_in", 0, 12)))[:, :, 0:4], ACT.Sigmoid),
                 ("w_in", 0, 12))
            steps(nc.scalar.activation(ba_abs, ba_y, ACT.Abs))
            eng.wait_ge(S["m1_loaded"], 96)
            nc.scalar.activation(ealog, alog[:, 0:4], ACT.Exp).then_inc(s("m1_sp"), 1)
            steps(nc.scalar.activation(ba_abs, ba_abs, ACT.Exp, scale=-1.0))
            nc.scalar.activation(ba_l, ba_abs, ACT.Ln, bias=stat[:, 62:63]).then_inc(s("m1_sp"), 1)

            def conv_in(j):
                name = ("w_in", 0, j)
                highs.upto(CH[name] + 2)
                projected(eng, name)
                t = QKV[j]
                if j == 6:
                    eng.wait_ge(s("m1_pads"), 1)
                read(nc.scalar.activation(cin[:, t:t + 2, 3:259], bank2(proj_bank(name)), ACT.Copy), name)

            def silu(j, order):
                t = QKV[j]
                eng.wait_ge(s("m1_conv"), order + 1)
                nc.scalar.activation(qkv[:, t:t + 2, :], qkv[:, t:t + 2, :], ACT.Silu).then_inc(s("m1_silu"), 1)
                if t < 8:
                    eng.wait_ge(S["m1_silu"], order + 1)
                    nc.scalar.activation(sq[:, t:t + 2, :], qkv[:, t:t + 2, :], ACT.Square).then_inc(s("m1_sq"), 1)

            def root(b, count):
                eng.wait_ge(s("m1_sums"), count)
                nc.scalar.activation(rs[:, 2 * b:2 * b + 2, :], bank2(b), ACT.Sqrt, scale=float(P) if b < 2 else 1.0,
                                     bias=stat[:, 61:62] if b < 2 else stat[:, 63:64]).then_inc(s("m1_root"), 1)

            for order, j in enumerate((6, 7, 4, 5, 8, 9)):
                conv_in(j)
                if order:
                    silu((6, 7, 4, 5, 8, 9)[order - 1], order - 1)
                if j == 5:
                    root(2, 1)
                    root(3, 2)
            silu(9, 5)
            root(0, 3)
            root(1, 4)
            eng.wait_ge(s("m1_gsums"), 1)
            nc.scalar.activation(ex, psum[:, 5, 0:32].rearrange("p (m k h) -> p m k h", m=2, k=4), ACT.Exp)\
                .then_inc(s("m1_ex"), 1)

            def gelu(j, to):
                name = ("w_in", 0, j)
                highs.upto(CH[name] + 2)
                projected(eng, name)
                read(nc.scalar.activation(to, bank2(proj_bank(name)), ACT.Gelu_apprx_tanh), name)
                highs.upto(CH[name] + 3)

            gelu(2, va[:, :, 0:256])
            for k, dst in enumerate((ktok[:, 0, :], ktok[:, 1, :], vtok[:, 0, :], vtok[:, 1, :])):
                eng.wait_ge(s("m1_kvturned"), k + 1)
                nc.scalar.activation(dst, psum[:, KV_BANKS[k], :], ACT.Copy).then_inc(s("m1_kvtok"), 1)
            for m in range(2):
                eng.wait_ge(s("m1_dlog"), m + 1)
                nc.scalar.activation(Dm[m], Dm[m], ACT.Exp).then_inc(s("m1_dexp"), 1)
            gelu(3, va[:, :, 256:512])
            inverse_scalar(eng, 0, Tm)
            gelu(0, yraw[:, 0:2, :])
            eng.wait_ge(s("m1_var"), 1)
            nc.scalar.activation(lnr[:, 0:2], mv.rearrange("p (m k) -> p m k", m=2)[:, :, 1], ACT.Sqrt,
                                 bias=stat[:, 63:64]).then_inc(s("m1_lnroot"), 1)
            gelu(1, yraw[:, 2:4, :])
            for c in range(4):
                r = slice((c % 2) * 64, (c % 2) * 64 + 64)
                eng.wait_ge(s("m1_ks"), c + 1)
                if c:
                    eng.wait_ge(s("m1_o"), c)
                for h in range(4):
                    nc.scalar.activation(OQ[r, h, :], psum[r, 1, h * P:(h + 1) * P], ACT.Copy,
                                         scale=ex[r, c // 2, 0, h:h + 1]).then_inc(s("m1_oq"), 1)
                if c % 2:
                    j = 10 + c // 2
                    name = ("w_in", 0, j)
                    projected(eng, name)
                    zc = zg[:, :, (j - 10) * 256:(j - 10) * 256 + 256]
                    read(nc.scalar.activation(zc, bank2(proj_bank(name)), ACT.Silu), name)
                    highs.upto(CH[name] + 3)
            for m in range(2):
                eng.wait_ge(s("m1_o"), 2 * m + 2)
                nc.scalar.activation(osq[:, m, :], Om[:, m, :], ACT.Square).then_inc(s("m1_osq"), 1)
            eng.wait_ge(s("m1_osum"), 2)
            nc.scalar.activation(ort, osum, ACT.Sqrt, scale=1.0 / P, bias=stat[:, 63:64]).then_inc(s("m1_oroot"), 1)
            eng.wait_ge(s("m1_gated"), 2)
            eng.wait_ge(chunk_used, CH[("w_in", 0, 11)] + 1)
            nc.scalar.activation(hhi[:, 0:4, :], yraw, ACT.Copy).then_inc(s("m1_yhi"), 1)
            for b in range(2):
                eng.wait_ge(s("m1_oturned"), b + 1)
                nc.scalar.activation(hhi[:, 4 + 2 * b:6 + 2 * b, :], bank2(b), ACT.Copy).then_inc(s("m1_yhi"), 1)
            for j in range(4):
                highs.upto(CH[("w_out", 0, j)] + 3)

        def mix1_vector(eng, st):
            eng.wait_ge(s("masks_loaded"), 16)
            norm_vector(eng, norm_of[st])
            steps = Steps(eng, "dve_step")
            eng.wait_ge(chunk_used, CH[("w_in", 0, 12)] + 1)
            eng.wait_ge(s("m1_loaded"), 96)
            nc.vector.tensor_tensor(mh(ba_y), bank2(proj_bank(("w_in", 0, 12)))[:, :, 4:8],
                                    alog[:, 4:8].rearrange("p (a h) -> p a h", a=1).broadcast_to((P, 2, 4)), ALU.add)\
                .then_inc(s("m1_y"), 1)
            nc.vector.memset(cin[:, :, 0:3], 0.0).then_inc(s("m1_pads"), 1)
            eng.wait_ge(S["m1_y"], 1)
            steps(nc.vector.tensor_scalar(spl, ba_y, 0.0, None, ALU.max))
            eng.wait_ge(s("m1_sp"), 2)
            steps(nc.vector.tensor_tensor(spl, spl, ba_l, ALU.add))
            nc.vector.scalar_tensor_tensor(out=mh(ba_g), in0=mh(spl), scalar=-1.0,
                                           in1=ealog.rearrange("p (a h) -> p a h", a=1).broadcast_to((P, 2, 4)),
                                           op0=ALU.mult, op1=ALU.mult).then_inc(s("m1_g"), 1)
            nc.vector.memset(Rm, 0.0).then_inc(s("m1_zero"), 1)
            nc.vector.memset(Wb, 0.0).then_inc(S["m1_zero"], 1)
            nc.vector.memset(Sm, 0.0).then_inc(S["m1_zero"], 1)
            for b in range(2):
                eng.wait_ge(s("m1_wturned"), b + 1)
                nc.vector.tensor_tensor(wsT[:, 4 * b:4 * b + 4, :], bank4(4 + b), four(const("gm_mask")), ALU.mult)\
                    .then_inc(s("m1_wsT"), 1)
            eng.wait_ge(S["m1_g"], 1)
            for m in range(2):
                nc.vector.tensor_scalar(ngB[m], mh(ba_g)[:, m, :].rearrange("p (h a) -> p h a", a=1).broadcast_to((P, 4, P)),
                                        -1.0, None, ALU.mult).then_inc(s("m1_ngB"), 1)

            def conv(j):
                name = ("w_in", 0, j)
                eng.wait_ge(bank_read[proj_bank(name)], PROJ[name] // 2 + 1)
                t0 = QKV[j]
                tap = lambda k, t: vec[:, VEC_AT["conv"] + 12 * k + t:VEC_AT["conv"] + 12 * k + t + 1]
                for k in (3, 2, 1, 0):
                    for t in (t0, t0 + 1):
                        if k == 3:
                            ins = nc.vector.tensor_scalar(qkv[:, t, :], cin[:, t, 3:259], tap(3, t), None, ALU.mult)
                        else:
                            ins = nc.vector.scalar_tensor_tensor(out=qkv[:, t, :], in0=cin[:, t, k:k + 256], scalar=tap(k, t),
                                                                 in1=qkv[:, t, :], op0=ALU.mult, op1=ALU.add)
                    if k:
                        steps(ins)
                ins.then_inc(s("m1_conv"), 1)

            def unit(b, count):
                eng.wait_ge(s("m1_root"), count)
                eng.wait_ge(s("m1_sq"), 2 if b >= 2 else 4)
                steps(nc.vector.reciprocal(rs[:, 2 * b:2 * b + 2, :], rs[:, 2 * b:2 * b + 2, :]))
                nc.vector.tensor_tensor(qkv[:, 2 * b:2 * b + 2, :], qkv[:, 2 * b:2 * b + 2, :], rs[:, 2 * b:2 * b + 2, :],
                                        ALU.mult).then_inc(s("m1_unit"), 1)

            conv(6)
            conv(7)
            conv(4)
            conv(5)
            unit(2, 1)
            conv(8)
            unit(3, 2)
            conv(9)
            unit(0, 3)
            unit(1, 4)
            eng.wait_ge(s("m1_ex"), 1)
            nc.vector.tensor_scalar(mh(neg_eg), ex[:, :, 0, :], -1.0, None, ALU.mult).then_inc(s("m1_bd"), 1)
            eng.wait_ge(bank_read[proj_bank(("w_in", 0, 12))], PROJ[("w_in", 0, 12)] // 2 + 1)
            nc.vector.tensor_tensor(mh(bd), mh(ba_beta), ex[:, :, 1, :], ALU.mult).then_inc(s("m1_bd"), 1)
            eng.wait_ge(s("m1_conv"), 6)
            for m in range(2):
                eng.wait_ge(s("m1_dpsum"), m + 1)
                nc.vector.tensor_scalar(Dm[m], bank4(DLOG_BANKS[m]), 0.0, None, ALU.min).then_inc(s("m1_dlog"), 1)
            over = lambda v: v.rearrange("p (h a) -> p h a", a=1).broadcast_to((P, 4, P))
            for m in range(2):
                eng.wait_ge(s("m1_dexp"), m + 1)
                steps(nc.vector.tensor_tensor(Dm[m], Dm[m], four(const("upto")), ALU.mult))
                steps(nc.vector.tensor_tensor(Dm[m], Dm[m], over(mh(ba_beta)[:, m, :]), ALU.mult))
            for m in range(2):
                eng.wait_ge(s("m1_kk"), m + 1)
                nc.vector.tensor_tensor(LTm[m], bank4(m), Dm[m], ALU.mult)
                steps(nc.vector.tensor_tensor(ATm[m], bank4(2 + m), Dm[m], ALU.mult))
            eng.wait_ge(S["m1_unit"], 4)
            inverse_start(steps, LTm, TTm, ALU.subtract)
            eng.wait_ge(s("m1_kvtok"), 4)
            eng.wait_ge(S["m1_bd"], 2)
            for m in range(2):
                kt4 = ktok[:, m, :].rearrange("p (h d) -> p h d", h=4)
                nc.vector.tensor_tensor(kt4, kt4, over(mh(bd)[:, m, :]), ALU.mult).then_inc(s("m1_kd"), 1)
            inverse_level_vector(eng, 0, 0, Tm, TTm, Xm, ALU.subtract)
            eng.wait_ge(bank_read[proj_bank(("w_in", 0, 2))], PROJ[("w_in", 0, 2)] // 2 + 1)
            eng.wait_ge(bank_read[proj_bank(("w_in", 0, 3))], PROJ[("w_in", 0, 3)] // 2 + 1)
            for m in range(2):
                steps(nc.vector.bn_stats(lnst[:, 6 * m:6 * m + 6], va[:, m, :]))
            steps(nc.vector.bn_aggr(mv[:, 0:2], lnst[:, 0:6]))
            nc.vector.bn_aggr(mv[:, 2:4], lnst[:, 6:12]).then_inc(s("m1_var"), 1)
            inverse_level_vector(eng, 0, 1, Tm, TTm, Xm, ALU.subtract)
            eng.wait_ge(s("m1_lnroot"), 1)
            steps(nc.vector.reciprocal(lnr[:, 2:4], lnr[:, 0:2]))
            for m in range(2):
                steps(nc.vector.tensor_scalar(va[:, m, :], va[:, m, :], mv[:, 2 * m:2 * m + 1], lnr[:, 2 + m:3 + m],
                                              ALU.subtract, ALU.mult))
            for k, op in enumerate((ALU.mult, ALU.add)):
                ins = nc.vector.tensor_tensor(va, va, lnp[:, k:k + 1, :].broadcast_to((P, 2, 512)), op)
                if k == 0:
                    steps(ins)
            ins.then_inc(s("m1_ln"), 1)
            for n in range(2, len(LEVELS)):
                inverse_level_vector(eng, 0, n, Tm, TTm, Xm, ALU.subtract)
            for j in (0, 1):
                eng.wait_ge(bank_read[proj_bank(("w_in", 0, j))], PROJ[("w_in", 0, j)] // 2 + 1)
            for m in range(2):
                eng.wait_ge(s("m1_mixed"), m + 1)
                steps(nc.vector.tensor_tensor(osq[:, m, :].rearrange("p (a n) -> p a n", a=4), bank4(4 + m), gbias, ALU.add))
                ys = yraw[:, :, m * P:(m + 1) * P]
                nc.vector.tensor_tensor(ys, ys, osq[:, m, :].rearrange("p (a n) -> p a n", a=4), ALU.mult)\
                    .then_inc(s("m1_gated"), 1)
            eng.wait_ge(S["m1_zero"], 3)
            for c in range(4):
                m, r = c // 2, slice((c % 2) * 64, (c % 2) * 64 + 64)
                eng.wait_ge(s("m1_ks"), c + 1)
                for h in range(4):
                    nc.vector.scalar_tensor_tensor(out=Rm[r, h, :], in0=psum[r, 0, h * P:(h + 1) * P],
                                                   scalar=neg_eg[r, 4 * m + h:4 * m + h + 1],
                                                   in1=vtok[r, m, h * P:(h + 1) * P], op0=ALU.mult, op1=ALU.add)\
                        .then_inc(s("m1_r"), 1)
                eng.wait_ge(s("m1_w"), c + 1)
                nc.vector.tensor_copy(Wb[r, c % 2, :], psum[r, 2, :]).then_inc(s("m1_wb"), 1)
                if c < 3:
                    eng.wait_ge(s("m1_spsum"), c + 1)
                    for h in range(4):
                        nc.vector.scalar_tensor_tensor(out=Sm[:, h, :], in0=Sm[:, h, :], scalar=ex[:, m, 2 + c % 2, h:h + 1],
                                                       in1=psum[:, 4, h * P:(h + 1) * P], op0=ALU.mult, op1=ALU.add)\
                            .then_inc(s("m1_s"), 1)
                eng.wait_ge(s("m1_opsum"), c + 1)
                eng.wait_ge(s("m1_oq"), 4 * c + 4)
                nc.vector.tensor_tensor(Om[r, m, :], psum[r, 3, :], OQ[r, :, :].rearrange("p h d -> p (h d)"), ALU.add)\
                    .then_inc(s("m1_o"), 1)
            for j in (10, 11):
                eng.wait_ge(bank_read[proj_bank(("w_in", 0, j))], PROJ[("w_in", 0, j)] // 2 + 1)
            steps(nc.vector.tensor_tensor(zg.rearrange("p m (h d) -> p (m h) d", h=4), zg.rearrange("p m (h d) -> p (m h) d", h=4),
                                          dnn.rearrange("p (a d) -> p a d", a=1).broadcast_to((P, 8, P)), ALU.mult))
            for m in range(2):
                eng.wait_ge(s("m1_osq"), m + 1)
                nc.vector.tensor_reduce(osum[:, 4 * m:4 * m + 4], osq[:, m, :].rearrange("p (h d) -> p h d", h=4), AX_X, ALU.add)\
                    .then_inc(s("m1_osum"), 1)
            eng.wait_ge(s("m1_oroot"), 1)
            steps(nc.vector.reciprocal(orr, ort))
            for m in range(2):
                o4 = Om[:, m, :].rearrange("p (h d) -> p h d", h=4)
                steps(nc.vector.tensor_tensor(o4, o4, over(orr[:, 4 * m:4 * m + 4]), ALU.mult))
                nc.vector.tensor_tensor(Om[:, m, :], Om[:, m, :], zg[:, m, :], ALU.mult).then_inc(s("m1_on"), 1)
            eng.wait_ge(s("m1_yhi"), 1)
            nc.vector.tensor_tensor(hlo[:, 0:4, :], yraw, hhi[:, 0:4, :].bitcast(F32), ALU.subtract).then_inc(s("m1_ylo"), 1)
            for b in range(2):
                eng.wait_ge(S["m1_yhi"], b + 2)
                nc.vector.tensor_tensor(hlo[:, 4 + 2 * b:6 + 2 * b, :], bank2(b), hhi[:, 4 + 2 * b:6 + 2 * b, :].bitcast(F32),
                                        ALU.subtract).then_inc(s("m1_ylo"), 1)
            add_out(eng, "w_out")

        def mix1_tensor(eng, st):
            eng.wait_ge(s("masks_loaded"), 16)
            norm_tensor(eng, norm_of[st])
            eng.wait_ge(s("m1_loaded"), 96)
            for b in range(2):
                for g in range(4):
                    mm = nc.tensor.transpose(bank4(4 + b)[:, g, :], ws[:, 4 * b + g, :], const("ident"))
                mm.then_inc(s("m1_wturned"), 1)
            project(eng, ("w_in", 0, 6), columns_out, wait=lambda k: eng.wait_ge(S["h_low"], 8 * norm_of[st] + k + 1))
            project(eng, ("w_in", 0, 12), tokens_out, n=8)
            def square_sums(b):
                eng.wait_ge(s("m1_sq"), 2 if b >= 2 else 4)
                nc.tensor.matmul(psum[:, b, :], const("ones"), sq[:, 2 * b:2 * b + 2, :], start=True, stop=True)\
                    .then_inc(s("m1_sums"), 1)

            for j in (7, 4, 5):
                project(eng, ("w_in", 0, j), columns_out)
            square_sums(2)
            square_sums(3)
            for j in (8, 9):
                project(eng, ("w_in", 0, j), columns_out)
            square_sums(0)
            square_sums(1)
            eng.wait_ge(s("m1_g"), 1)
            eng.wait_ge(s("m1_wsT"), 2)
            for m in range(2):
                for k, mat in enumerate(("upto", "after", "chunk0", "chunk1")):
                    mm = nc.tensor.matmul(psum[:, 5, 16 * m + 4 * k:16 * m + 4 * k + 4], const(mat), mh(ba_g)[:, m, :],
                                          start=True, stop=True)
            mm.then_inc(s("m1_gsums"), 1)
            project(eng, ("w_in", 0, 2), tokens_out)
            eng.wait_ge(s("m1_root"), 4)
            eng.wait_ge(s("m1_unit"), 2)
            eng.wait_ge(s("m1_silu"), 6)
            for k, (t0, m) in enumerate(((4, 0), (4, 1), (8, 0), (8, 1))):
                for h in range(4):
                    mm = nc.tensor.transpose(bank4(KV_BANKS[k])[:, h, :], qkv[:, t0 + h, m * P:(m + 1) * P], const("ident"))
                mm.then_inc(s("m1_kvturned"), 1)
            eng.wait_ge(s("m1_ngB"), 2)
            eng.wait_ge(s("m1_ex"), 1)
            for m in range(2):
                b = DLOG_BANKS[m]
                nc.tensor.matmul(bank4(b), const("upto"), ngB[m], start=True, stop=False)
                for h in range(4):
                    mm = nc.tensor.matmul(bank4(b)[:, h, :], ngB[m][:, h, :], const("neg_upto"), start=False, stop=h == 3)
                mm.then_inc(s("m1_dpsum"), 1)
            project(eng, ("w_in", 0, 3), tokens_out)
            eng.wait_ge(s("m1_unit"), 4)
            eng.wait_ge(s("m1_kvtok"), 4)
            for m in range(2):
                eng.wait_ge(s("m1_dlog"), m + 1)
                for h in range(4):
                    nc.tensor.matmul(bank4(m)[:, h, :], qkv[:, 4 + h, m * P:(m + 1) * P], qkv[:, 4 + h, m * P:(m + 1) * P],
                                     start=True, stop=True)
                for h in range(4):
                    mm = nc.tensor.matmul(bank4(2 + m)[:, h, :], qkv[:, 4 + h, m * P:(m + 1) * P],
                                          qkv[:, h, m * P:(m + 1) * P], start=True, stop=True)
                mm.then_inc(s("m1_kk"), 1)

            def mixed(m):
                eng.wait_ge(s("m1_ln"), 1)
                for g in range(8):
                    p0 = (g % 2) * 64
                    mm = nc.tensor.matmul(psum[p0:p0 + 64, 4 + m, (g // 2) * P:(g // 2) * P + P], va[:, m, g * 64:g * 64 + 64],
                                          wsT[:, g, :], start=True, stop=True)
                mm.then_inc(s("m1_mixed"), 1)

            inverse_turn_tensor(eng, 0, TTm)
            for n in range(len(LEVELS)):
                inverse_x_tensor(eng, 0, n, LTm, Tm)
                if n < 2:
                    project_half(eng, ("w_in", 0, n), columns_out, 0)
                if n == 3:
                    mixed(0)
                inverse_tx_tensor(eng, 0, n, TTm, Xm)
                if n < 2:
                    project_half(eng, ("w_in", 0, n), columns_out, 1)
                if n == 3:
                    mixed(1)
            eng.wait_ge(INV["inv_updated"], 10)
            for c in range(4):
                m, tok = c // 2, slice((c // 2) * P, (c // 2) * P + P)
                if c == 0:
                    eng.wait_ge(s("m1_zero"), 3)
                else:
                    eng.wait_ge(s("m1_s"), 4 * c)
                    eng.wait_ge(s("m1_oq"), 4 * c)
                for h in range(4):
                    nc.tensor.matmul(bank4(0)[:, h, :], qkv[:, 4 + h, tok], Sm[:, h, :], start=True, stop=True)
                for h in range(4):
                    mm = nc.tensor.matmul(bank4(1)[:, h, :], qkv[:, h, tok], Sm[:, h, :], start=True, stop=True)
                mm.then_inc(s("m1_ks"), 1)
                project_half(eng, ("w_in", 0, 10 + c // 2), tokens_out, c % 2)
                eng.wait_ge(s("m1_r"), 4 * c + 4)
                for h in range(4):
                    mm = nc.tensor.matmul(bank4(2)[:, h, :], TTm[m][:, h, :], Rm[:, h, :], start=True, stop=True)
                mm.then_inc(s("m1_w"), 1)
                eng.wait_ge(s("m1_wb"), c + 1)
                eng.wait_ge(s("m1_kd"), 2)
                if c == 0:
                    eng.wait_ge(s("m1_gated"), 2)
                if c < 3:
                    for h in range(4):
                        mm = nc.tensor.matmul(bank4(4)[:, h, :], ktok[:, m, h * P:(h + 1) * P],
                                              Wb[:, c % 2, h * P:(h + 1) * P], start=True, stop=True)
                    mm.then_inc(s("m1_spsum"), 1)
                if c:
                    eng.wait_ge(s("m1_o"), c)
                for h in range(4):
                    mm = nc.tensor.matmul(bank4(3)[:, h, :], ATm[m][:, h, :], Wb[:, c % 2, h * P:(h + 1) * P],
                                          start=True, stop=True)
                mm.then_inc(s("m1_opsum"), 1)
            eng.wait_ge(s("m1_on"), 2)
            for b in range(2):
                for k in range(2):
                    for m in range(2):
                        mm = nc.tensor.transpose(psum[:, b, k * 256 + m * P:k * 256 + m * P + P],
                                                 Om[:, m, (2 * b + k) * P:(2 * b + k) * P + P], const("ident"))
                mm.then_inc(s("m1_oturned"), 1)
            out_tensor(eng, "w_out", s("m1_ylo"), {0: 1, 1: 1, 2: 1, 3: 1, 4: 2, 5: 2, 6: 3, 7: 3})

        rsq = area(2048, TT, D)
        fin = area(4096, D)

        def rms_scalar(eng, stage):
            nc.scalar.activation(stat[:, 50:51], stat[:, 63:64], ACT.Sqrt)
            eng.wait_ge(x_ready, 4 * (stage - 1) + 1)
            eng.dma_start(fin, rows["final_norm"].partition_broadcast(P)).then_inc(s("fin_loaded"), 16)
            for i in range(4):
                m, cols = i // 2, slice((i % 2) * 512, (i % 2) * 512 + 512)
                eng.wait_ge(x_ready, 4 * (stage - 1) + i + 1)
                nc.scalar.activation(rsq[:, m, cols], x[:, m, cols], ACT.Square, scale=1.0 / 32, accum_out=stat[:, 24 + i:25 + i])\
                    .then_inc(s("fin_squares"), 1)
            eng.wait_ge(s("fin_scale"), 1)
            nc.scalar.activation(stat[:, 10:12], stat[:, 8:10], ACT.Sqrt, bias=stat[:, 63:64]).then_inc(s("fin_root"), 1)

        def rms_vector(eng):
            eng.wait_ge(s("fin_squares"), 4)
            nc.vector.tensor_reduce(stat[:, 8:10], stat[:, 24:28].rearrange("p (m i) -> p m i", m=2), AX_X, ALU.add)\
                .then_inc(s("fin_scale"), 1)
            eng.wait_ge(s("fin_root"), 1)
            nc.vector.reciprocal(stat[:, 12:14], stat[:, 10:12]).then_inc(S["fin_scale"], 1)
            eng.wait_ge(S["fin_scale"], 2)
            eng.wait_ge(s("fin_loaded"), 16)
            for m in range(TT):
                for half in range(2):
                    xs = x[:, m, half * 512:half * 512 + 512]
                    nc.vector.scalar_tensor_tensor(out=xs, in0=xs, scalar=stat[:, 12 + m:13 + m],
                                                   in1=fin[:, half * 512:half * 512 + 512], op0=ALU.mult, op1=ALU.mult)\
                        .then_inc(x_ready, 1)

        fqk = area(0, 8, 256)
        fsq = area(2048, 8, 256)
        frs = area(4096, 8, 256)
        nlfB = area(6144, 2, 8 * P)
        fv = area(8192, 2, 512)
        fog = area(9216, 2, 512)
        U = area(10240, 4, 272)
        WA = area(11328, 4, 272)
        WB = area(12416, 4, 272)
        pooled = area(13504, 4, 256)
        pw = area(14528, 4, P)
        FL = area(15040, 2, 512)
        FP = area(16064, 2, 512)
        FT = area(17088, 2, 512)
        yo = area(18112, 2, 512)
        sf = area(19136, 256)
        fb, f_y, f_abs, f_l, f_n = (sf[:, 16 * k:16 * k + 16] for k in range(5))
        fmax, fneg = sf[:, 80:104], sf[:, 104:128]
        fsum, frec = sf[:, 128:144], sf[:, 144:160]
        UNITS = [(0, [p, p + 2, p + 4, p + 6]) for p in range(2)] + \
                [(1, [p + 4 * k, p + 4 * k + 2]) for k in range(2) for p in range(2)]
        mh8 = lambda v: v.rearrange("p (m h) -> p m h", m=2)

        def fox_scalar(eng, highs, st):
            n, stage = norm_of[st], STAGES.index(st)
            def load():
                eng.dma_start(pw, rows["pool_w"].rearrange("g c d -> c g d")).then_inc(s("m2_loaded"), 16)
                eng.dma_start(fb[:, 0:8], rows["f_bias"].partition_broadcast(P)).then_inc(s("m2_loaded"), 16)

            norm_scalar(eng, n, CH[("hy_w_in", 0, 0)] - 1, stage, load=load)
            steps = Steps(eng, "act_step")
            N = lambda j: ("hy_w_in", 0, j)

            def ready(j):
                highs.upto(CH[N(j)] + 2)
                projected(eng, N(j))

            highs.upto(CH[N(8)] + 2)
            eng.wait_ge(s("m2_y"), 1)
            steps(nc.scalar.activation(f_abs, f_y, ACT.Abs))
            steps(nc.scalar.activation(f_abs, f_abs, ACT.Exp, scale=-1.0))
            nc.scalar.activation(f_l, f_abs, ACT.Ln, bias=stat[:, 62:63]).then_inc(s("m2_l"), 1)
            for k, j in enumerate((0, 1, 2, 3)):
                ready(j)
                b = proj_bank(N(j))
                nc.scalar.activation(fqk[:, 2 * k:2 * k + 2, :], bank2(b), ACT.Copy).then_inc(s("m2_qk"), 1)
                read(nc.scalar.activation(fsq[:, 2 * k:2 * k + 2, :], bank2(b), ACT.Square), N(j))
            for j in (4, 5):
                ready(j)
                read(nc.scalar.activation(fv[:, :, (j - 4) * 256:(j - 4) * 256 + 256], bank2(proj_bank(N(j))), ACT.Copy), N(j))
            for b in range(4):
                eng.wait_ge(s("m2_sums"), b + 1)
                nc.scalar.activation(frs[:, 2 * b:2 * b + 2, :], bank2(b), ACT.Sqrt, scale=1.0 if b < 2 else 1.0 / 64,
                                     bias=stat[:, 60:61] if b < 2 else stat[:, 63:64]).then_inc(s("m2_root"), 1)
            eng.wait_ge(s("m2_pads"), 3)
            for j in (9, 10):
                ready(j)
                read(nc.scalar.activation(U[:, 2 * (j - 9):2 * (j - 9) + 2, 16:272], bank2(proj_bank(N(j))), ACT.Copy), N(j))
            for j in (6, 7):
                ready(j)
                read(nc.scalar.activation(fog[:, :, (j - 6) * 256:(j - 6) * 256 + 256], bank2(proj_bank(N(j))), ACT.Sigmoid),
                     N(j))
            highs.upto(CH[N(7)] + 3)
            for u, (m, heads) in enumerate(UNITS):
                keys = P * (m + 1)
                eng.wait_ge(s("m2_neg"), u + 1)
                if u >= 2:
                    eng.wait_ge(s("m2_pturned"), u - 1)
                for k, h in enumerate(heads):
                    nc.scalar.activation(FP[:, u % 2, k * keys:(k + 1) * keys], FL[:, u % 2, k * keys:(k + 1) * keys], ACT.Exp,
                                         bias=fneg[:, 4 * u + k:4 * u + k + 1], accum_out=fsum[:, 8 * m + h:8 * m + h + 1])\
                        .then_inc(s("m2_p"), 1)
                eng.wait_ge(s("m2_pturned"), u + 1)
                if u >= 2:
                    eng.wait_ge(s("m2_pv"), u - 1)
                nc.scalar.activation(FT[:, u % 2, :], psum[:, 2 + u % 2, :], ACT.Copy).then_inc(s("m2_pt"), 1)
            eng.wait_ge(chunk_used, CH[N(7)] + 1)
            for b in range(2):
                eng.wait_ge(s("m2_pooled"), b + 1)
                for g in (2 * b, 2 * b + 1):
                    nc.scalar.activation(hhi[:, 4 + g, :], bank2(b)[:, g % 2, :], ACT.Copy,
                                         scale=vec[:, VEC_AT["pool_scale"] + g:VEC_AT["pool_scale"] + g + 1])\
                        .then_inc(s("m2_yhi"), 1)
            for b in range(2):
                eng.wait_ge(s("m2_oturned"), b + 1)
                nc.scalar.activation(hhi[:, 2 * b:2 * b + 2, :], bank2(2 + b), ACT.Copy).then_inc(s("m2_yhi"), 1)
            for j in range(4):
                highs.upto(CH[("hy_w_out", 0, j)] + 3)

        def fox_vector(eng, st):
            norm_vector(eng, norm_of[st])
            steps = Steps(eng, "dve_step")
            N = lambda j: ("hy_w_in", 0, j)
            projected(eng, N(8))
            eng.wait_ge(s("m2_loaded"), 32)
            nc.vector.tensor_tensor(mh8(f_y), bank2(proj_bank(N(8)))[:, :, 0:8],
                                    fb[:, 0:8].rearrange("p (a h) -> p a h", a=1).broadcast_to((P, 2, 8)), ALU.add)\
                .then_inc(s("m2_y"), 1)
            eng.wait_ge(S["m2_y"], 1)
            read(nc.vector.tensor_scalar(f_n, f_y, -1.0, 0.0, ALU.mult, ALU.max), N(8))
            for t in (U, WA, WB):
                nc.vector.memset(t[:, :, 0:16], 0.0).then_inc(s("m2_pads"), 1)
            eng.wait_ge(s("m2_l"), 1)
            eng.wait_ge(bank_read[proj_bank(N(8))], PROJ[N(8)] // 2 + 1)
            steps(nc.vector.tensor_tensor(f_n, f_n, f_l, ALU.add))
            for m in range(2):
                nc.vector.tensor_scalar(nlfB[:, m, :].rearrange("p (h a) -> p h a", h=8),
                                        f_n[:, 8 * m:8 * m + 8].rearrange("p (h a) -> p h a", a=1).broadcast_to((P, 8, P)),
                                        1.0, None, ALU.mult).then_inc(s("m2_nlfB"), 1)
            for b in range(4):
                eng.wait_ge(s("m2_root"), b + 1)
                eng.wait_ge(s("m2_qk"), b + 1)
                t = slice(2 * b, 2 * b + 2)
                steps(nc.vector.reciprocal(frs[:, t, :], frs[:, t, :]))
                gain = VEC_AT["q_gain" if b < 2 else "k_gain"]
                nc.vector.scalar_tensor_tensor(out=fqk[:, t, :], in0=fqk[:, t, :], scalar=vec[:, gain:gain + 1],
                                               in1=frs[:, t, :], op0=ALU.mult, op1=ALU.mult).then_inc(s("m2_unit"), 1)
            for j in (9, 10):
                eng.wait_ge(bank_read[proj_bank(N(j))], PROJ[N(j)] // 2 + 1)
            eng.wait_ge(S["m2_pads"], 3)
            src = U
            for g0, dst in enumerate((WA, WB, WA, WB)):
                back = 2 ** g0
                steps(nc.vector.tensor_tensor(dst[:, g0:4, 16:272], src[:, g0:4, 16:272], src[:, g0:4, 16 - back:272 - back],
                                              ALU.add))
                src = dst
            for g, t in enumerate((WA, WB, WA, WB)):
                inv = const("pool", 64)[:, 16 * g:16 * g + 16]
                nc.vector.scalar_tensor_tensor(out=pooled[:, g, 16:256], in0=t[:, g, 32:272], scalar=1.0 / 2 ** (g + 1),
                                               in1=U[:, g, 32:272], op0=ALU.mult, op1=ALU.subtract).then_inc(s("m2_pool"), 1)
                steps(nc.vector.tensor_tensor(t[:, g, 16:32], t[:, g, 16:32], inv, ALU.mult))
                nc.vector.tensor_tensor(pooled[:, g, 0:16], t[:, g, 16:32], U[:, g, 16:32], ALU.subtract)\
                    .then_inc(S["m2_pool"], 1)
            def logits(u):
                m, heads = UNITS[u]
                nh, keys = len(heads), P * (m + 1)
                eng.wait_ge(s("m2_logits"), u + 1)
                if u >= 2:
                    eng.wait_ge(s("m2_p"), sum(len(x_[1]) for x_ in UNITS[:u - 1]))
                L3 = FL[:, u % 2, :].rearrange("p (h k) -> p h k", h=nh)
                mask = const("causal") if m == 0 else const("zero_causal", 256)
                mask = mask.rearrange("p (a k) -> p a k", a=1).broadcast_to((P, nh, keys))
                nc.vector.tensor_tensor(L3, psum[:, u % 2, :].rearrange("p (h k) -> p h k", h=nh), mask, ALU.add)\
                    .then_inc(s("m2_masked"), 1)
                eng.wait_ge(S["m2_masked"], u + 1)
                steps(nc.vector.tensor_reduce(fmax[:, 4 * u:4 * u + nh], L3, AX_X, ALU.max))
                nc.vector.tensor_scalar(fneg[:, 4 * u:4 * u + nh], fmax[:, 4 * u:4 * u + nh], -1.0, None, ALU.mult)\
                    .then_inc(s("m2_neg"), 1)

            for u in range(6):
                logits(u)
            for m in range(2):
                eng.wait_ge(s("m2_pv"), 2 if m == 0 else 6)
                steps(nc.vector.reciprocal(frec[:, 8 * m:8 * m + 8], fsum[:, 8 * m:8 * m + 8]))
                y3 = yo[:, m, :].rearrange("p (h d) -> p h d", h=8)
                steps(nc.vector.tensor_tensor(y3, psum[:, 4 + m, :].rearrange("p (h d) -> p h d", h=8),
                                              frec[:, 8 * m:8 * m + 8].rearrange("p (h a) -> p h a", a=1).broadcast_to((P, 8, 64)),
                                              ALU.mult))
                nc.vector.tensor_tensor(yo[:, m, :], yo[:, m, :], fog[:, m, :], ALU.mult).then_inc(s("m2_yo"), 1)
            for b in range(2):
                eng.wait_ge(s("m2_yhi"), 2 * b + 2)
                for g in (2 * b, 2 * b + 1):
                    nc.vector.scalar_tensor_tensor(out=hlo[:, 4 + g, :], in0=bank2(b)[:, g % 2, :],
                                                   scalar=vec[:, VEC_AT["pool_scale"] + g:VEC_AT["pool_scale"] + g + 1],
                                                   in1=hhi[:, 4 + g, :].bitcast(F32), op0=ALU.mult, op1=ALU.subtract)\
                        .then_inc(s("m2_ylo"), 1)
            for b in range(2):
                eng.wait_ge(s("m2_yhi"), 5 + b)
                nc.vector.tensor_tensor(hlo[:, 2 * b:2 * b + 2, :], bank2(2 + b), hhi[:, 2 * b:2 * b + 2, :].bitcast(F32),
                                        ALU.subtract).then_inc(s("m2_ylo"), 1)
            add_out(eng, "hy_w_out")

        def fox_tensor(eng, st):
            N = lambda j: ("hy_w_in", 0, j)
            norm_tensor(eng, norm_of[st])
            project(eng, N(0), columns_out, wait=lambda k: eng.wait_ge(S["h_low"], 8 * norm_of[st] + k + 1))
            project(eng, N(8), tokens_out, n=8)
            for j in (1, 2, 3):
                project(eng, N(j), columns_out)
            for j in (4, 5):
                project(eng, N(j), tokens_out)
            for b in range(4):
                eng.wait_ge(bank_read[proj_bank(N(b))], PROJ[N(b)] // 2 + 1)
                nc.tensor.matmul(psum[:, b, :], const("same64"), fsq[:, 2 * b:2 * b + 2, :], start=True, stop=True)\
                    .then_inc(s("m2_sums"), 1)
            for j in (9, 10):
                project(eng, N(j), columns_out)
            for j in (6, 7):
                project(eng, N(j), tokens_out)
            eng.wait_ge(s("m2_unit"), 4)
            eng.wait_ge(s("m2_nlfB"), 2)

            def logits(u):
                m, heads = UNITS[u]
                keys = P * (m + 1)
                if u >= 2:
                    eng.wait_ge(s("m2_masked"), u - 1)
                for k, h in enumerate(heads):
                    o = psum[:, u % 2, k * keys:(k + 1) * keys]
                    r, t = slice((h % 2) * 64, (h % 2) * 64 + 64), h // 2
                    nc.tensor.matmul(o, fqk[r, t, m * P:(m + 1) * P], fqk[r, 4 + t, 0:keys], start=True, stop=False)
                    mm = nc.tensor.matmul(o, nlfB[:, 0, h * P:(h + 1) * P], const("upto_all", keys), start=False, stop=m == 0)
                    if m == 1:
                        mm = nc.tensor.matmul(o[:, P:2 * P], nlfB[:, 1, h * P:(h + 1) * P], const("upto_all"), start=False,
                                              stop=True)
                mm.then_inc(s("m2_logits"), 1)

            def values(u):
                m, heads = UNITS[u]
                eng.wait_ge(s("m2_pt"), u + 1)
                for k, h in enumerate(heads):
                    for t in range(m + 1):
                        mm = nc.tensor.matmul(psum[:, 4 + m, h * 64:h * 64 + 64],
                                              FT[:, u % 2, (k * (m + 1) + t) * P:(k * (m + 1) + t + 1) * P],
                                              fv[:, t, h * 64:h * 64 + 64], start=t == 0, stop=t == m)
                mm.then_inc(s("m2_pv"), 1)

            logits(0)
            for u, (m, heads) in enumerate(UNITS):
                if u < 5:
                    logits(u + 1)
                eng.wait_ge(s("m2_p"), sum(len(x_[1]) for x_ in UNITS[:u + 1]))
                if u >= 2:
                    eng.wait_ge(s("m2_pt"), u - 1)
                for k in range(4):
                    mm = nc.tensor.transpose(bank4(2 + u % 2)[:, k, :], FP[:, u % 2, k * P:(k + 1) * P], const("ident"))
                mm.then_inc(s("m2_pturned"), 1)
                if u:
                    values(u - 1)
            values(5)
            eng.wait_ge(s("m2_pool"), 8)
            eng.wait_ge(s("m2_masked"), 6)
            eng.wait_ge(s("m2_loaded"), 32)
            for b in range(2):
                for g in (2 * b, 2 * b + 1):
                    mm = nc.tensor.matmul(bank2(b)[:, g % 2, :], pw[:, g, :], pooled[:, g, :], start=True, stop=True)
                mm.then_inc(s("m2_pooled"), 1)
            eng.wait_ge(s("m2_yo"), 2)
            eng.wait_ge(s("m2_pt"), 6)
            for b in range(2):
                for k in range(2):
                    for m in range(2):
                        mm = nc.tensor.transpose(psum[:, 2 + b, k * 256 + m * P:k * 256 + m * P + P],
                                                 yo[:, m, (2 * b + k) * P:(2 * b + k) * P + P], const("ident"))
                mm.then_inc(s("m2_oturned"), 1)
            out_tensor(eng, "hy_w_out", s("m2_ylo"), {4: 1, 5: 2, 6: 3, 7: 4, 0: 5, 1: 5, 2: 6, 3: 6})

        DECAY = float(np.exp(-0.5))
        ar = area(0, 2, 8 * 256).rearrange("p s (k t) -> p s k t", k=8)
        kk = ar[:, 0, :, :]
        rr = ar[:, 1, :, :]
        kx = area(4096, 8, 256)
        sw = area(6144, 8, 256)
        aa = area(8192, 8, 256)
        vt = area(10240, 2, D)
        roots = area(10240, 8, 256)
        shifted = area(12288, 8, 256)
        variant_x = area(14336, 8, 256)
        ht = area(16384, 8, 257)
        sums = area(18440, 8, 256)
        rk = shifted
        bkT = [area(at, 2, 8 * P).rearrange("p s (k t) -> p s k t", k=8) for at in (14336, 12288)]
        bk = [area(at, 2, D) for at in (6144, 14336)]
        ak_flat = [area(16384, 2048), raw[:, 0, :]]
        AK = [[f[:, 1024 * g:1024 * g + 1024].rearrange("p (a s n) -> p a s n", a=4, s=2) for g in range(2)] for f in ak_flat]
        RB = [[raw[:, 1, 1024 * i_ + 512 * g:1024 * i_ + 512 * g + 512].rearrange("p (a n) -> p a n", a=4)
               for g in range(2)] for i_ in range(2)]
        TTr_pass = [[area(at + 512 * g, 4, P) for g in range(2)] for at in (13312, 19456)]
        T_pass = [area(12288 + 512 * g, 4, P) for g in range(2)]
        LT_pass = [area(18432 + 512 * g, 4, P) for g in range(2)]
        X_pass = [area(20480 + 512 * g, 4, P) for g in range(2)]
        U_pass, R_pass = (raw[:, 2, 512 * i_:512 * i_ + 512].rearrange("p (a n) -> p a n", a=4) for i_ in range(2))
        STREAM_STOPS = CH.get(("rw_o", 0, 2))
        Z = area(21504, 8, P)
        s3m = area(22528, 512)
        pc = s3m[:, 0:32].rearrange("p (k c) -> p k c", k=8)
        bonus = s3m[:, 32:64]
        gsum, gmean, gvar, groot, gscale = (s3m[:, 64 + 32 * k:96 + 32 * k] for k in range(5))
        Y = x
        yt = area(0, 8, 256)
        ysq = area(12288, 2, D)
        wa_hi, wa_lo = ahi[:, 0, 0, :], alo[:, 0, 0, :]
        gm_hi, gm_lo = ahi[:, 1, 0, :], alo[:, 1, 0, :]
        gt_hi, gt_lo = ahi[:, 1, 1, :], alo[:, 1, 1, :]
        lw = area(20488, 3, 256)
        V_AT = lambda name, k: vec[:, VEC_AT[name] + k:VEC_AT[name] + k + 1]
        VARIANTS = (1, 4, 5, 2, 0, 3)
        FIRST_OF = {3: 4, 4: 0, 5: 8}
        RW = lambda j: ("rw", 0, j)
        L0, L1, L2 = (CH.get(("lora", 0, j)) for j in range(3))
        TURNED = [(4, 5), (6, 7), (0, 1), (4, 5)]
        PASSES = [(m, q) for m in range(2) for q in range(2)]

        def z_steps(w, hh):
            return 5 * sum(1 for v_ in range(2 * w + hh) if 2 * PASSES[v_ // 2][0] + v_ % 2 < 3)

        def variant_used(eng, v):
            if v in (1, 2, 3):
                eng.wait_ge(s("rw_first"), v)
            if v > 3:
                eng.wait_ge(chunk_used, CH[RW(FIRST_OF[v - 1] + 3)] + 1)

        def counted(eng, name, k, chunk):
            if k < 4:
                eng.wait_ge(s(name), k)
            else:
                eng.wait_ge(chunk_used, chunk + 1)

        def rwkv_scalar(eng, highs, st):
            n, stage = norm_of[st], STAGES.index(st)
            mean_squares(eng, n, stage)
            eng.wait_ge(S["rows_scaled"], 2 * n + 2)
            eng.dma_start(kept_x, x[:, :, :].rearrange("p m d -> p (m d)")).then_inc(s("x_kept"), 16)
            for b in range(4):
                eng.wait_ge(S["turned"], 4 * n + b + 1)
                for k in (2 * b, 2 * b + 1):
                    nc.scalar.activation(ht[:, k, 1:257], psum[:, b, (k % 2) * 256:(k % 2) * 256 + 256], ACT.Copy,
                                         scale=V_AT(NORMS[n], k)).then_inc(S["h_high"], 1)
            highs.upto(L0 + 2)

            def high_variant(v):
                if v < 4:
                    variant_used(eng, v)
                for b in range(4):
                    if v >= 4 and b < 3:
                        eng.wait_ge(s("rw_tiles_used"), 3 * (v - 4) + b + 1)
                    elif v >= 4:
                        variant_used(eng, v)
                    eng.wait_ge(s("rw_mixed"), 8 * v + 2 * b + 2)
                    nc.scalar.activation(hhi[:, 2 * b:2 * b + 2, :], variant_x[:, 2 * b:2 * b + 2, :], ACT.Copy)\
                        .then_inc(s("rw_xhi"), 1)

            eng.wait_ge(chunk_used, L0)
            for v in range(3):
                high_variant(v)
            eng.wait_ge(s("rw_first"), 2)
            nc.scalar.activation(lw[0:64, 0, :], psum[0:64, 0, 0:256], ACT.Tanh).then_inc(s("rw_lw"), 1)
            nc.scalar.activation(lw[64:128, 0, :], psum[64:128, 0, 256:512], ACT.Copy).then_inc(s("rw_lw"), 1)
            eng.wait_ge(s("rw_lw"), 2)
            nc.scalar.activation(wa_hi, lw[:, 0, :], ACT.Copy).then_inc(s("rw_lwhi"), 1)
            eng.wait_ge(s("rw_first"), 3)
            nc.scalar.activation(lw[:, 1, :], psum[:, 1, 0:256], ACT.Sigmoid).then_inc(S["rw_lw"], 1)
            nc.scalar.activation(lw[0:32, 2, :], psum[0:32, 1, 256:512], ACT.Sigmoid).then_inc(S["rw_lw"], 1)
            eng.wait_ge(S["rw_lw"], 4)
            nc.scalar.activation(gm_hi, lw[:, 1, :], ACT.Copy).then_inc(S["rw_lwhi"], 1)
            nc.scalar.activation(gt_hi[0:32], lw[0:32, 2, :], ACT.Copy).then_inc(S["rw_lwhi"], 1)
            for k in range(8):
                if k % 2 == 0:
                    counted(eng, "rw_second", k // 2 + 1, L1)
                b = (k // 2) % 2
                nc.scalar.activation(sw[:, k, :], bank2(2 + b)[:, k % 2, :], ACT.Sigmoid, bias=V_AT("w0", k)).then_inc(s("rw_sig"), 1)
                nc.scalar.activation(aa[:, k, :], bank2(4 + b)[:, k % 2, :], ACT.Sigmoid, bias=V_AT("a0", k)).then_inc(s("rw_sig"), 1)

            def root(b):
                eng.wait_ge(s("rw_sums"), b + 1)
                nc.scalar.activation(roots[:, 2 * b:2 * b + 2, :], bank2(b), ACT.Sqrt).then_inc(s("rw_root"), 1)

            high_variant(3)
            for j in range(4):
                name = RW(4 + j)
                highs.upto(CH[name] + 2)
                if j == 3:
                    high_variant(4)
                projected(eng, name)
                read(nc.scalar.activation(kx[:, 2 * j:2 * j + 2, :], bank2(proj_bank(name)), ACT.Copy), name)
                highs.upto(CH[name] + 3)
                if j == 0:
                    eng.wait_ge(s("rw_before"), 1)
                    nc.scalar.activation(sw, sw, ACT.Exp, scale=-DECAY).then_inc(s("rw_pm"), 1)
                eng.wait_ge(s("rw_kk"), 2 * j + 2)
                nc.scalar.activation(roots[:, 2 * j:2 * j + 2, :], kk[:, 2 * j:2 * j + 2, :], ACT.Square).then_inc(s("rw_sq"), 1)
                if j >= 2:
                    root(j - 2)
            for j in range(4):
                name = RW(j)
                highs.upto(CH[name] + 2)
                if j == 3:
                    high_variant(5)
                projected(eng, name)
                eng.wait_ge(s("rw_kx"), 4)
                read(nc.scalar.activation(rr[:, 2 * j:2 * j + 2, :], bank2(proj_bank(name)), ACT.Copy), name)
                if j < 2:
                    root(j + 2)
            eng.wait_ge(s("rw_neg"), 1)
            nc.scalar.activation(sw, sums, ACT.Exp, scale=DECAY).then_inc(s("rw_pinv"), 1)
            eng.wait_ge(s("rw_pinv"), 1)
            nc.scalar.activation(sums, sums, ACT.Exp, scale=-DECAY).then_inc(s("rw_p"), 1)
            for j in range(4):
                name = RW(8 + j)
                highs.upto(CH[name] + 2)
                projected(eng, name)
                read(nc.scalar.activation(vt[:, :, j * 256:(j + 1) * 256], bank2(proj_bank(name)), ACT.Copy), name)
            highs.upto(CH[RW(11)] + 3)
            for m in range(2):
                for b in range(4):
                    eng.wait_ge(s("rw_bkturned"), 4 * m + b + 1)
                    nc.scalar.activation(bk[m][:, b // 2, (b % 2) * 512:(b % 2) * 512 + 512], psum[:, 4 * m + b, :], ACT.Copy)\
                        .then_inc(s("rw_bk"), 1)
            eng.wait_ge(s("x_kept"), 16)
            eng.wait_ge(low_made, STREAM_STOPS)

            def copy_r(w, hh):
                eng.wait_ge(s("rw_usum"), 2 * w + hh + 1)
                r = slice(hh * 64, hh * 64 + 64)
                nc.scalar.activation(R_pass[r], bank4(4)[r], ACT.Copy).then_inc(s("rw_r"), 1)

            def copy_u(w, hh):
                eng.wait_ge(s("rw_u"), 2 * w + hh + 1)
                r = slice(hh * 64, hh * 64 + 64)
                nc.scalar.activation(U_pass[r], bank4(5)[r], ACT.Copy).then_inc(s("rw_ub"), 1)

            def copy_y(w, hh):
                m, q = PASSES[w]
                eng.wait_ge(s("rw_ysum"), 2 * w + hh + 1)
                r = slice(hh * 64, hh * 64 + 64)
                nc.scalar.activation(Y[r, m, q * 512:(q + 1) * 512], psum[r, 7, :], ACT.Copy).then_inc(s("rw_y"), 1)

            def squares(w):
                m, q = PASSES[w]
                eng.wait_ge(s("rw_centred"), w + 1)
                cols = slice(q * 512, q * 512 + 512)
                nc.scalar.activation(ysq[:, m, cols], Y[:, m, cols], ACT.Square).then_inc(s("rw_ysq"), 1)

            def deviation(w):
                eng.wait_ge(s("rw_gvar"), w + 1)
                hs = slice(8 * w, 8 * w + 8)
                nc.scalar.activation(groot[:, hs], gvar[:, hs], ACT.Sqrt, scale=1.0 / 64, bias=stat[:, 59:60])\
                    .then_inc(s("rw_groot"), 1)

            def normed_turned(b):
                eng.wait_ge(s("rw_out"), b + 1)
                for k in (2 * b, 2 * b + 1):
                    nc.scalar.activation(yt[:, k, :], bank2(TURNED[b][0])[:, k % 2, :], ACT.Identity, scale=V_AT("ln_w", k),
                                         bias=V_AT("ln_b", k)).then_inc(s("rw_yt"), 1)

            def y_high(b):
                eng.wait_ge(s("rw_gated"), b + 1)
                nc.scalar.activation(hhi[:, 2 * b:2 * b + 2, :], yt[:, 2 * b:2 * b + 2, :], ACT.Copy).then_inc(s("rw_yhi"), 1)

            for w in range(5):
                if w:
                    copy_r(w - 1, 0)
                    copy_u(w - 1, 0)
                if w < 4:
                    inverse_scalar(eng, w + inv0["rwkv"], T_pass)
                if w == 4:
                    for piece in range(3):
                        squares(piece)
                if w:
                    copy_y(w - 1, 0)
                    copy_r(w - 1, 1)
                    copy_u(w - 1, 1)
                if w == 4:
                    for piece in range(3):
                        deviation(piece)
                if w:
                    copy_y(w - 1, 1)
            normed_turned(0)
            squares(3)
            deviation(3)
            normed_turned(1)
            y_high(0)
            normed_turned(2)
            y_high(1)
            normed_turned(3)
            eng.dma_start(x[:, :, :].rearrange("p m d -> p (m d)"), kept_x).then_inc(s("x_back"), 16)
            y_high(2)
            y_high(3)
            for j in range(4):
                highs.upto(CH[("rw_o", 0, j)] + 3)

        def rwkv_vector(eng, st):
            n = norm_of[st]
            steps = Steps(eng, "dve_step")
            scaled_rows(eng, n)
            steps(nc.vector.memset(ht[:, :, 0:1], 0.0))
            steps(nc.vector.memset(Z, 0.0))
            for b in range(4):
                eng.wait_ge(S["h_high"], 8 * n + 2 * b + 2)
                for k in (2 * b, 2 * b + 1):
                    nc.vector.tensor_tensor(shifted[:, k, :], ht[:, k, 0:256], ht[:, k, 1:257], ALU.subtract)\
                        .then_inc(S["h_low"], 1)
            eng.wait_ge(S["h_low"], 8 * n + 8)
            nc.vector.tensor_copy(stat[:, 6:7], stat[:, 5:6]).then_inc(S["rms_scale"], 1)
            eng.wait_ge(S["rms_scale"], 3 * n + 3)

            def mix_variant(v):
                if v:
                    eng.wait_ge(s("rw_xlo"), 4 * v)
                for k in range(8):
                    mu = VEC_AT["mu"] + 8 * VARIANTS[v] + k
                    nc.vector.scalar_tensor_tensor(out=variant_x[:, k, :], in0=shifted[:, k, :], scalar=vec[:, mu:mu + 1],
                                                   in1=ht[:, k, 1:257], op0=ALU.mult, op1=ALU.add).then_inc(s("rw_mixed"), 1)

            def low_variant(v):
                for b in range(4):
                    eng.wait_ge(s("rw_xhi"), 4 * v + b + 1)
                    k = slice(2 * b, 2 * b + 2)
                    nc.vector.tensor_tensor(hlo[:, k, :], variant_x[:, k, :], hhi[:, k, :].bitcast(F32), ALU.subtract)\
                        .then_inc(s("rw_xlo"), 1)

            for v in range(3):
                mix_variant(v)
                low_variant(v)
            eng.wait_ge(s("rw_lwhi"), 1)
            nc.vector.tensor_tensor(wa_lo, lw[:, 0, :], wa_hi.bitcast(F32), ALU.subtract).then_inc(s("rw_lwlo"), 1)
            mix_variant(3)
            eng.wait_ge(S["rw_lwhi"], 3)
            nc.vector.tensor_tensor(gm_lo, lw[:, 1, :], gm_hi.bitcast(F32), ALU.subtract).then_inc(S["rw_lwlo"], 1)
            nc.vector.tensor_tensor(gt_lo[0:32], lw[0:32, 2, :], gt_hi[0:32].bitcast(F32), ALU.subtract).then_inc(S["rw_lwlo"], 1)
            low_variant(3)
            mix_variant(4)
            eng.wait_ge(s("rw_sig"), 16)
            for k in range(8):
                ins = nc.vector.tensor_tensor_scan(sums[:, k, :], const("restart", TOK), sw[:, k, :], 0.0, ALU.mult, ALU.add)
            steps(ins)
            nc.vector.tensor_tensor(sw, sums, sw, ALU.subtract).then_inc(s("rw_before"), 1)
            for k in range(8):
                ins = nc.vector.tensor_scalar(rr[:, k, :], aa[:, k, :], 1.0, V_AT("k_a", k), ALU.subtract, ALU.mult)
            steps(ins)

            def unit_kk(b):
                eng.wait_ge(s("rw_root"), b + 1)
                k = slice(2 * b, 2 * b + 2)
                steps(nc.vector.tensor_scalar(roots[:, k, :], roots[:, k, :], 1e-12, None, ALU.max))
                steps(nc.vector.reciprocal(roots[:, k, :], roots[:, k, :]))
                steps(nc.vector.tensor_tensor(kk[:, k, :], kk[:, k, :], roots[:, k, :], ALU.mult))

            for j in range(4):
                name = RW(4 + j)
                eng.wait_ge(bank_read[proj_bank(name)], PROJ[name] // 2 + 1)
                for k in (2 * j, 2 * j + 1):
                    nc.vector.tensor_scalar(kk[:, k, :], kx[:, k, :], V_AT("k_k", k), None, ALU.mult).then_inc(s("rw_kk"), 1)
                eng.wait_ge(s("rw_kk"), 2 * j + 2)
                k = slice(2 * j, 2 * j + 2)
                nc.vector.scalar_tensor_tensor(out=kx[:, k, :], in0=rr[:, k, :], scalar=1.0, in1=kx[:, k, :],
                                               op0=ALU.add, op1=ALU.mult).then_inc(s("rw_kx"), 1)
                if j == 2:
                    unit_kk(0)
                    low_variant(4)
            mix_variant(5)
            for b in range(1, 4):
                unit_kk(b)
            low_variant(5)
            steps(nc.vector.tensor_tensor(aa, aa, kk, ALU.mult))
            eng.wait_ge(s("rw_pm"), 1)
            nc.vector.scalar_tensor_tensor(out=kk, in0=kk, scalar=-1.0, in1=sw, op0=ALU.mult, op1=ALU.mult).then_inc(s("rw_neg"), 1)
            for j in range(0, 4):
                eng.wait_ge(bank_read[proj_bank(RW(j))], PROJ[RW(j)] // 2 + 1)
            eng.wait_ge(s("rw_kx"), 4)
            eng.wait_ge(s("rw_mixed"), 48)
            for k in range(8):
                nc.vector.scalar_tensor_tensor(out=rk[:, k, :], in0=rr[:, k, :], scalar=V_AT("r_k", k), in1=kx[:, k, :],
                                               op0=ALU.mult, op1=ALU.mult).then_inc(s("rw_rk"), 1)
            eng.wait_ge(s("rw_pinv"), 1)
            steps(nc.vector.tensor_tensor(aa, aa, sw, ALU.mult))
            eng.wait_ge(s("rw_rk"), 8)
            steps(nc.vector.tensor_tensor(kx, kx, sw, ALU.mult))
            eng.wait_ge(s("rw_p"), 1)
            steps(nc.vector.tensor_tensor(rr, rr, sums, ALU.mult))
            steps(nc.vector.tensor_copy(pc, sums.rearrange("p k (c t) -> p k c t", c=4)[:, :, :, 63]))

            def to_tokens(m):
                pcb = pc[:, :, 2 * m:2 * m + 2].rearrange("p k (c a) -> p k c a", a=1).broadcast_to((P, 8, 2, 64))
                for i_, src in enumerate((aa, kx)):
                    nc.vector.tensor_tensor(bkT[m][:, i_, :, :].rearrange("p k (c t) -> p k c t", c=2),
                                            src[:, :, m * P:(m + 1) * P].rearrange("p k (c t) -> p k c t", c=2), pcb, ALU.mult)\
                        .then_inc(s("rw_bkT"), 1)

            to_tokens(0)
            eng.wait_ge(s("rw_bonus_sum"), 1)
            nc.vector.tensor_copy(bonus, psum[:, 4, 0:32]).then_inc(s("rw_bonus"), 1)
            to_tokens(1)

            def masked_scores(w):
                for b in range(8):
                    g, i_, k = b // 4, (b // 2) % 2, slice(2 * (b % 2), 2 * (b % 2) + 2)
                    eng.wait_ge(s("rw_scores"), 8 * w + b + 1)
                    two = lambda name, n: const(name, n).rearrange("p (a n) -> p a n", a=1).broadcast_to((P, 2, n))
                    if i_ == 0:
                        nc.vector.tensor_tensor(LT_pass[g][:, k, :], bank2(b % 4)[:, :, 0:P], two("before", P), ALU.mult)
                        nc.vector.tensor_tensor(RB[w % 2][g][:, k, :], bank2(b % 4)[:, :, P:2 * P], two("upto", P), ALU.mult)\
                            .then_inc(s("rw_masked"), 1)
                    else:
                        nc.vector.tensor_tensor(AK[w % 2][g][:, k, :, :].rearrange("p a s n -> p a (s n)"), bank2(b % 4),
                                                two("before", 256), ALU.mult).then_inc(s("rw_masked"), 1)
                eng.wait_ge(S["rw_masked"], 8 * w + 8)

            def next_state(w, hh):
                m, q = PASSES[w]
                c, z0, done = 2 * m + hh, z_steps(w, hh), z_steps(w, hh) // 5
                if c == 3:
                    return
                eng.wait_ge(s("rw_zsum"), done + 1)
                if z0:
                    eng.wait_ge(s("rw_z"), z0)
                nc.vector.tensor_tensor(R_pass, bank4(6), four(const("same64")), ALU.mult).then_inc(s("rw_z"), 1)
                eng.wait_ge(s("rw_z"), z0 + 1)
                eng.wait_ge(s("rw_ysum"), 2 * w + hh + 1)
                for k in range(4):
                    t = 4 * q + k
                    nc.vector.scalar_tensor_tensor(out=Z[:, t, :], in0=Z[:, t, :], scalar=pc[:, t, c:c + 1],
                                                   in1=R_pass[:, k, :], op0=ALU.mult, op1=ALU.add).then_inc(s("rw_z"), 1)

            over64 = lambda v: v.rearrange("p (h a) -> p h a", a=1).broadcast_to((P, 8, 64))
            piece = lambda t, w: t[:, PASSES[w][0], PASSES[w][1] * 512:PASSES[w][1] * 512 + 512].rearrange("p (h d) -> p h d", h=8)

            def centre(w):
                eng.wait_ge(s("rw_y"), 2 * w + 2)
                y3, hs = piece(Y, w), slice(8 * w, 8 * w + 8)
                steps(nc.vector.tensor_reduce(gsum[:, hs], y3, AX_X, ALU.add))
                steps(nc.vector.tensor_scalar(gmean[:, hs], gsum[:, hs], 1.0 / 64, None, ALU.mult))
                nc.vector.tensor_tensor(y3, y3, over64(gmean[:, hs]), ALU.subtract).then_inc(s("rw_centred"), 1)

            def bonus_v(w):
                eng.wait_ge(s("rw_ysum"), 2 * w + 2)
                v3 = piece(vt, w)
                nc.vector.tensor_tensor(v3, v3, over64(bonus[:, 8 * w:8 * w + 8]), ALU.mult).then_inc(s("rw_bv"), 1)

            def variance(w):
                eng.wait_ge(s("rw_ysq"), w + 1)
                nc.vector.tensor_reduce(gvar[:, 8 * w:8 * w + 8], piece(ysq, w), AX_X, ALU.add).then_inc(s("rw_gvar"), 1)

            def normed(w):
                eng.wait_ge(s("rw_groot"), w + 1)
                y3, hs = piece(Y, w), slice(8 * w, 8 * w + 8)
                steps(nc.vector.reciprocal(gscale[:, hs], groot[:, hs]))
                nc.vector.tensor_tensor(y3, y3, over64(gscale[:, hs]), ALU.mult).then_inc(s("rw_yn"), 1)

            eng.wait_ge(low_made, STREAM_STOPS)
            for w in range(4):
                masked_scores(w)
                inverse_start(steps, LT_pass, TTr_pass[w % 2], ALU.add)
                for n_ in range(len(LEVELS)):
                    inverse_level_vector(eng, w + inv0["rwkv"], n_, T_pass, TTr_pass[w % 2], X_pass, ALU.add)
                    if w and n_ == 0:
                        next_state(w - 1, 0)
                    if w and n_ == 3:
                        next_state(w - 1, 1)
            for w in range(3):
                centre(w)
            next_state(3, 0)
            for w in range(3):
                variance(w)
            for w in range(3):
                bonus_v(w)
            for w in range(3):
                normed(w)
            bonus_v(3)

            def gated(b):
                k = slice(2 * b, 2 * b + 2)
                eng.wait_ge(s("rw_yt"), 2 * b + 2)
                eng.wait_ge(chunk_used, L2 + 1)
                steps(nc.vector.tensor_tensor(yt[:, k, :], yt[:, k, :], bank2(TURNED[b][1]), ALU.add))
                nc.vector.tensor_tensor(yt[:, k, :], yt[:, k, :], bank2(b), ALU.mult).then_inc(s("rw_gated"), 1)

            def y_low(b):
                k = slice(2 * b, 2 * b + 2)
                eng.wait_ge(s("rw_yhi"), b + 1)
                nc.vector.tensor_tensor(hlo[:, k, :], yt[:, k, :], hhi[:, k, :].bitcast(F32), ALU.subtract)\
                    .then_inc(s("rw_ylo"), 1)

            centre(3)
            gated(0)
            variance(3)
            normed(3)
            gated(1)
            y_low(0)
            gated(2)
            y_low(1)
            gated(3)
            y_low(2)
            y_low(3)
            eng.wait_ge(s("x_back"), 16)
            add_out(eng, "rw_o")

        def rwkv_tensor(eng, st):
            n = norm_of[st]
            norm_tensor(eng, n)
            eng.wait_ge(low_made, L0 + 1)

            def first(v, bank, half, slot, at, width, stride):
                rows_ = width
                for k in range(KT):
                    if k % 2 == 0:
                        eng.wait_ge(s("rw_xlo"), 4 * v + k // 2 + 1)
                    w = (slice(None), slot, slice(at + k * stride, at + k * stride + width))
                    mm = three_passes(psum[0:rows_, bank, half * 256:half * 256 + 256], whi[w], wlo[w], hhi[:, k, :],
                                      hlo[:, k, :], True, k == 0, k == KT - 1)
                return mm

            first(0, 0, 0, L0 % SPLIT, 0, P, 256).then_inc(s("rw_first"), 1)
            first(1, 0, 1, L0 % SPLIT, 0, P, 256).then_inc(s("rw_first"), 1)
            first(2, 1, 0, L0 % SPLIT, P, P, 256).then_inc(chunk_used, 1)
            eng.wait_ge(low_made, L1 + 1)
            first(2, 1, 1, L1 % SPLIT, D, 32, 32).then_inc(s("rw_first"), 1)
            eng.wait_ge(s("rw_lwlo"), 1)
            for b in range(4):
                if b >= 2:
                    eng.wait_ge(s("rw_sig"), 4 * (b - 1))
                for base, lo_, hi_ in ((2, 0, 64), (4, 64, 128)):
                    for k in (2 * b, 2 * b + 1):
                        w = (slice(lo_, hi_), L1 % SPLIT, slice(k * P, k * P + P))
                        mm = three_passes(bank2(base + b % 2)[:, k % 2, :], whi[w], wlo[w], wa_hi[lo_:hi_], wa_lo[lo_:hi_],
                                          True, True, True)
                mm.then_inc(chunk_used if b == 3 else s("rw_second"), 1)

            def square_sums(b):
                eng.wait_ge(s("rw_sq"), b + 1)
                nc.tensor.matmul(psum[:, b, :], const("same64"), roots[:, 2 * b:2 * b + 2, :], start=True, stop=True)\
                    .then_inc(s("rw_sums"), 1)

            def made(v):
                return lambda k: eng.wait_ge(s("rw_xlo"), 4 * v + k // 2 + 1)

            for j in range(4):
                project(eng, RW(4 + j), columns_out, wait=made(3) if j == 0 else None,
                        used=s("rw_tiles_used") if j == 3 else None)
                if j == 0:
                    eng.wait_ge(s("rw_sig"), 16)
                if j:
                    square_sums(j - 1)
            for j in range(4):
                project(eng, RW(j), columns_out, wait=made(4) if j == 0 else None,
                        used=s("rw_tiles_used") if j == 3 else None)
                if j == 0:
                    square_sums(3)
            for j in range(4):
                project(eng, RW(8 + j), tokens_out, wait=made(5) if j == 0 else None)
                if j == 1:
                    eng.wait_ge(s("rw_rk"), 8)
                    for m in range(2):
                        for k in range(8):
                            mm = nc.tensor.matmul(psum[:, 4, 16 * m + 2 * k:16 * m + 2 * k + 2], rk[:, k, m * P:(m + 1) * P],
                                                  const("same64")[:, 0:P:64], start=True, stop=True)
                    mm.then_inc(s("rw_bonus_sum"), 1)
            eng.wait_ge(s("rw_root"), 4)
            for m in range(2):
                eng.wait_ge(s("rw_bkT"), 2 * m + 2)
                for b in range(4):
                    if m and b == 0:
                        eng.wait_ge(s("rw_bonus"), 1)
                    if m and b >= 2:
                        name = RW(8 + b)
                        eng.wait_ge(bank_read[proj_bank(name)], PROJ[name] // 2 + 1)
                    for k in range(4):
                        mm = nc.tensor.transpose(bank4(4 * m + b)[:, k, :], bkT[m][:, b // 2, 4 * (b % 2) + k, :], const("ident"))
                    mm.then_inc(s("rw_bkturned"), 1)

            def scores(w):
                m, q = PASSES[w]
                tok = slice(m * P, (m + 1) * P)
                if w:
                    eng.wait_ge(INV["inv_updated"], 10 * (w + inv0["rwkv"]))
                for b in range(8):
                    g, src, half = b // 4, (aa, kx)[(b // 2) % 2], b % 2
                    if b >= 4:
                        eng.wait_ge(s("rw_masked"), 8 * w + b - 3)
                    elif w == 0:
                        eng.wait_ge(s("rw_bk"), b + 1)
                    r = slice(64 * g, 64 * g + 64)
                    for k in range(2):
                        t = 4 * q + 2 * half + k
                        mm = nc.tensor.matmul(bank2(b % 4)[:, k, :], src[r, t, tok], ar[r, :, t, tok], start=True, stop=True)
                    mm.then_inc(s("rw_scores"), 1)

            def u_sums(w, hh):
                m, q = PASSES[w]
                r, tok = slice(hh * 64, hh * 64 + 64), slice(m * P + hh * 64, m * P + hh * 64 + 64)
                if w or hh:
                    eng.wait_ge(s("rw_z"), z_steps(w, hh))
                elif w == 0:
                    eng.wait_ge(s("rw_bk"), 8)
                for k in range(4):
                    nc.tensor.matmul(bank4(4)[r, k, :], kk[:, 4 * q + k, tok], Z[:, 4 * q + k, :], start=True, stop=False)
                    for p in range(2):
                        col = (4 * q + k) * P + p * 64
                        mm = nc.tensor.matmul(bank4(4)[r, k, p * 64:p * 64 + 64], AK[w % 2][p][r, k, 0, r], vt[r, m, col:col + 64],
                                              start=False, stop=p == 1)
                mm.then_inc(s("rw_usum"), 1)

            def u_solve(w, hh):
                r = slice(hh * 64, hh * 64 + 64)
                eng.wait_ge(s("rw_r"), 2 * w + hh + 1)
                if hh == 0:
                    eng.wait_ge(INV["inv_updated"], 10 * (w + inv0["rwkv"]) + 10)
                for k in range(4):
                    for p in range(2):
                        mm = nc.tensor.matmul(bank4(5)[r, k, p * 64:p * 64 + 64], TTr_pass[w % 2][p][r, k, r],
                                              R_pass[r, k, p * 64:p * 64 + 64], start=True, stop=True)
                mm.then_inc(s("rw_u"), 1)

            def state_and_y(w, hh):
                m, q = PASSES[w]
                c, r, tok = 2 * w + hh, slice(hh * 64, hh * 64 + 64), slice(m * P + hh * 64, m * P + hh * 64 + 64)
                eng.wait_ge(s("rw_ub"), c + 1)
                if 2 * m + hh < 3:
                    for k in range(4):
                        t = 4 * q + k
                        nc.tensor.matmul(bank4(6)[:, k, :], bk[m][r, 0, t * P:(t + 1) * P], U_pass[r, k, :], start=True, stop=False)
                        mm = nc.tensor.matmul(bank4(6)[:, k, :], bk[m][r, 1, t * P:(t + 1) * P], vt[r, m, t * P:(t + 1) * P],
                                              start=False, stop=True)
                    mm.then_inc(s("rw_zsum"), 1)
                if c:
                    eng.wait_ge(s("rw_y"), c)
                for k in range(4):
                    nc.tensor.matmul(bank4(7)[r, k, :], rr[:, 4 * q + k, tok], Z[:, 4 * q + k, :], start=True, stop=False)
                    for p in range(2):
                        col = (4 * q + k) * P + p * 64
                        o = bank4(7)[r, k, p * 64:p * 64 + 64]
                        nc.tensor.matmul(o, AK[w % 2][p][r, k, 1, r], vt[r, m, col:col + 64], start=False, stop=False)
                        mm = nc.tensor.matmul(o, RB[w % 2][p][r, k, r], U_pass[r, k, p * 64:p * 64 + 64], start=False, stop=p == 1)
                mm.then_inc(s("rw_ysum"), 1)

            for w in range(4):
                u = w + inv0["rwkv"]
                if w:
                    u_sums(w - 1, 0)
                scores(w)
                if w:
                    u_solve(w - 1, 0)
                inverse_turn_tensor(eng, u, TTr_pass[w % 2])
                for n_ in range(len(LEVELS)):
                    inverse_x_tensor(eng, u, n_, LT_pass, T_pass)
                    if w and n_ == 0:
                        state_and_y(w - 1, 0)
                    if w and n_ == 2:
                        u_solve(w - 1, 1)
                    if w and n_ == 3:
                        state_and_y(w - 1, 1)
                    inverse_tx_tensor(eng, u, n_, TTr_pass[w % 2], X_pass)
                    if w and n_ == 1:
                        u_sums(w - 1, 1)

            def gates(b):
                for k in range(2):
                    o = bank2(b)[:, k, :]
                    at = (2 * b + k) * P
                    w = (slice(None), L2 % SPLIT, slice(at, at + P))
                    three_passes(o, whi[w], wlo[w], gm_hi, gm_lo, True, True, False)
                    w = (slice(0, 32), L2 % SPLIT, slice(D + at, D + at + P))
                    mm = three_passes(o, whi[w], wlo[w], gt_hi[0:32], gt_lo[0:32], True, False, True)
                return mm

            u_sums(3, 0)
            eng.wait_ge(INV["inv_updated"], 10 * (3 + inv0["rwkv"]) + 10)
            eng.wait_ge(low_made, L2 + 1)
            eng.wait_ge(s("rw_lwlo"), 3)
            gates(0)
            u_solve(3, 0)
            gates(1)
            state_and_y(3, 0)
            gates(2)
            u_sums(3, 1)
            gates(3).then_inc(chunk_used, 1)
            u_solve(3, 1)
            state_and_y(3, 1)
            for b in range(4):
                if b == 0:
                    eng.wait_ge(s("rw_r"), 8)
                    eng.wait_ge(s("rw_ub"), 8)
                if b == 1:
                    eng.wait_ge(s("rw_z"), z_steps(3, 1))
                    eng.wait_ge(s("rw_y"), 8)
                if b == 2:
                    eng.wait_ge(s("rw_gated"), 2)
                if b % 2 == 0:
                    eng.wait_ge(s("rw_yn"), 3 + b // 2)
                    eng.wait_ge(s("rw_bv"), 3 + b // 2)
                for bank, src in zip(TURNED[b], (Y, vt)):
                    for k in range(2):
                        for m in range(2):
                            mm = nc.tensor.transpose(psum[:, bank, k * 256 + m * P:k * 256 + m * P + P],
                                                     src[:, m, (2 * b + k) * P:(2 * b + k + 1) * P], const("ident"))
                mm.then_inc(s("rw_out"), 1)
            eng.wait_ge(s("rw_gated"), 2)
            out_tensor(eng, "rw_o", s("rw_ylo"), {k: k // 2 + 1 for k in range(KT)})

        block = ctx.enter_context(nc.Block())

        @block.sync
        def _(sp):
            sp.dma_start(x[:, :, :], x_in.rearrange("(m p) d -> p m d", p=P)).then_inc(S["x_loaded"], 16)
            sp.dma_start(con[:, 0:P], consts[:, 0:P]).then_inc(S["const_loaded"], 16)
            sp.dma_start(raw[:, 0, :], stream[0]).then_inc(raw_loaded[0], 16)
            sp.dma_start(vec[:, :], vectors).then_inc(S["const_loaded"], 16)
            for c in range(1, RAW):
                sp.dma_start(raw[:, c, :], stream[c]).then_inc(raw_loaded[c], 16)
            sp.dma_start(con[:, P:], consts[:, P:]).then_inc(s("masks_loaded"), 16)

            def load(i, r):
                sp.wait_ge(low_made, 3 * i + (r - 2))
                sp.dma_start(raw[:, r, :], stream[bass.ds(3 * i + r, 1), :, :].rearrange("a p n -> p (a n)"))\
                    .then_inc(raw_loaded[r], 16)

            with sp.Fori(1, STREAM_STOPS // RAW) as i:
                for r in range(RAW):
                    load(i, r)
            for r in range(RAW):
                if r == STREAM_STOPS % RAW:
                    sp.wait_ge(s("rw_ysum"), 8)
                load(STREAM_STOPS // RAW, r)
            with sp.Fori(STREAM_STOPS // RAW + 1, NCH // RAW) as i:
                for r in range(RAW):
                    load(i, r)
            for c in range(NCH // RAW * RAW, NCH):
                sp.wait_ge(low_made, c - 2)
                sp.dma_start(raw[:, c % RAW, :], stream[c]).then_inc(raw_loaded[c % RAW], 16)
            sp.wait_ge(x_ready, 4 * len(STAGES))
            sp.dma_start(out.rearrange("(m p) d -> p m d", p=P), x[:, :, :]).then_inc(S["stored"], 16)
            sp.wait_ge(S["stored"], 16)

        @block.gpsimd
        def _(pool):
            def low(c, i=None):
                slot = c % SPLIT
                pool.wait_ge(high_made, c + 1 if i is None else c + 1 + 3 * i)
                nc.gpsimd.tensor_tensor(wlo[:, slot, :], raw[:, c % RAW, :], whi[:, slot, :].bitcast(F32), ALU.subtract)\
                    .then_inc(low_made, 1)
            with pool.Fori(0, NCH // 3) as i:
                for r in range(3):
                    low(r, i)
            for c in range(NCH // 3 * 3, NCH):
                low(c)

        @block.scalar
        def _(act_eng):
            highs = Highs(act_eng)
            act_eng.wait_ge(S["const_loaded"], 32)
            act_eng.wait_ge(S["eps_ready"], 5)
            for k, st in enumerate(STAGES):
                if st[0] == "ffn":
                    norm_scalar(act_eng, norm_of[st], CH[("gate", st[1], 0)] - 1 if k else None, k, highs)
                    ffn_scalar(act_eng, st[1], highs)
                if st[0] == "mix1":
                    mix1_scalar(act_eng, highs, st)
                if st[0] == "rms":
                    rms_scalar(act_eng, k)
                if st[0] == "fox":
                    fox_scalar(act_eng, highs, st)
                if st[0] == "rwkv":
                    rwkv_scalar(act_eng, highs, st)

        @block.vector
        def _(dve):
            nc.vector.memset(stat[:, 63:64], EPS).then_inc(S["eps_ready"], 1)
            nc.vector.memset(stat[:, 62:63], 1.0).then_inc(S["eps_ready"], 1)
            nc.vector.memset(stat[:, 61:62], P * EPS).then_inc(S["eps_ready"], 1)
            nc.vector.memset(stat[:, 60:61], 64 * EPS).then_inc(S["eps_ready"], 1)
            nc.vector.memset(stat[:, 59:60], 64e-5).then_inc(S["eps_ready"], 1)
            dve.wait_ge(S["x_loaded"], 16)
            dve.wait_ge(S["const_loaded"], 32)
            for st in STAGES:
                if st[0] == "mix1":
                    mix1_vector(dve, st)
                if st[0] == "rms":
                    rms_vector(dve)
                if st[0] == "fox":
                    fox_vector(dve, st)
                if st[0] == "rwkv":
                    rwkv_vector(dve, st)
                if st[0] == "ffn":
                    norm_vector(dve, norm_of[st])
                    ffn_vector(dve, st[1], 0.5 if st[1] < 2 else 1.0)

        @block.tensor
        def _(pe):
            pe.wait_ge(S["const_loaded"], 32)
            for st in STAGES:
                if st[0] == "mix1":
                    mix1_tensor(pe, st)
                if st[0] == "fox":
                    fox_tensor(pe, st)
                if st[0] == "rwkv":
                    rwkv_tensor(pe, st)
                if st[0] == "ffn":
                    norm_tensor(pe, norm_of[st])
                    ffn_tensor(pe, st[1], norm_of[st])


def kernel(**inputs):
    import concourse.bacc as bacc
    from concourse.bass_utils import run_bass_kernel_spmd

    a = {k: np.asarray(v) for k, v in inputs.items()}
    names = stream_plan(STAGES)
    stream = np.stack([lay_out_chunk(n, a) for n in names])
    rows = {"gm_w_s": a["gm_w_s"][0], "gm_ln_g": a["gm_ln_g"][0], "gm_ln_b": a["gm_ln_b"][0],
            "gm_bias": np.repeat(a["gm_b_s"][0].reshape(4, 2, P), 64, axis=1).transpose(1, 0, 2),
            "dn_norm": a["dn_norm"][0], "gates": np.concatenate([a["dn_a_log"][0], a["dn_dt_bias"][0]]),
            "final_norm": a["final_norm"], "pool_w": a["hy_pool_w_2"][0], "f_bias": a["hy_f_bias_2"][0]}
    rows = {k: np.ascontiguousarray(v) for k, v in rows.items()}
    arrays = {"stream": stream, "consts": CONSTS, "vectors": lay_out_vectors(a), "x_in": a["x"].reshape(TOK, D), **rows}
    nc = bacc.Bacc("TRN2", target_bir_lowering=False, num_devices=1)
    h = {k: nc.dram_tensor(k, v.shape, mybir.dt.from_np(v.dtype), kind="ExternalInput").ap() for k, v in arrays.items()}
    out = nc.dram_tensor("out", (TOK, D), F32, kind="ExternalOutput").ap()
    build(nc, h["stream"], h["consts"], h["vectors"], h["x_in"], {k: h[k] for k in rows},
          nc.dram_tensor("kept_x", (P, TT * D), F32, kind="Internal").ap(), out)
    r = run_bass_kernel_spmd(nc, [arrays], core_ids=[0])
    return r.results[0]["out"].reshape(1, TOK, D)
```
